# Optimizing a Trainium2 kernel written in Bass

```python
import math
import jax, jax.numpy as jnp
from jax import lax
import numpy as np

D_MODEL = 1024
BATCH = 1
SEQ = 128
DEPTH = 2
DEC_BATCH = 1
DEC_SEQ = 512
PAST_LEN = 128

GRID_W = 64
MIX_W = D_MODEL
N_HEADS = 4
QK_DIM = 64
V_DIM = 2 * QK_DIM
ATTN_W = N_HEADS * V_DIM
F_GROUPS = 4
F_CH = (MIX_W - ATTN_W) // F_GROUPS
FOURIER_W = F_GROUPS * F_CH
QK_W = N_HEADS * 2 * QK_DIM
IN_W = 2 * QK_W + ATTN_W + FOURIER_W
ROPE_THETA = 10000.0
Q_BLOCK = 128
D_FF = 2816
N_EXPERTS = 8
TOP_K = 2
D_FF_E = 1024
N_DENSE = (DEPTH + 1) // 2
N_MOE = DEPTH // 2
N_MOD = 6
EPS = 1e-6

kernel_name = "hybrid_diffattn_fnet_prefix_dit_step"

def rms_norm(x, g):
    xf = x.astype(jnp.float32)
    y = xf * lax.rsqrt(jnp.mean(xf * xf, axis=-1, keepdims=True) + EPS)
    return (y * g.astype(jnp.float32)).astype(x.dtype)

def axial_rope_tables(T):
    rows = T // GRID_W
    row = jnp.repeat(jnp.arange(rows), GRID_W)
    col = jnp.tile(jnp.arange(GRID_W), rows)
    half = QK_DIM // 2
    inv = 1.0 / (ROPE_THETA ** (jnp.arange(0, half, 2, dtype=jnp.float32) / half))

    def tab(pos):
        ang = pos.astype(jnp.float32)[:, None] * inv[None, :]
        return jnp.concatenate([ang, ang], axis=-1)

    ang = jnp.concatenate([tab(row), tab(col)], axis=-1)
    return jnp.cos(ang), jnp.sin(ang)

def apply_axial_rope(x, cos, sin):
    qd = QK_DIM // 4
    xs = x.reshape(x.shape[:-1] + (2, 2, qd))
    rot = jnp.stack([-xs[..., 1, :], xs[..., 0, :]], axis=-2).reshape(x.shape)
    c = cos[None, :, None, None, :]
    s = sin[None, :, None, None, :]
    return (x.astype(jnp.float32) * c + rot.astype(jnp.float32) * s).astype(x.dtype)

def diff_attention(q, k, v, lam, g_subln, lam_init):
    B, Tq = q.shape[0], q.shape[1]
    nb = Tq // Q_BLOCK
    qb = jnp.moveaxis(q.reshape((B, nb, Q_BLOCK) + q.shape[2:]), 1, 0)
    scale = QK_DIM ** -0.5

    def block(qblk):
        s = jnp.einsum('bqhmd,bkhmd->bmhqk', qblk, k, preferred_element_type=jnp.float32) * scale
        p = jax.nn.softmax(s, axis=-1)
        a = p[:, 0] - lam * p[:, 1]
        return jnp.einsum('bhqk,bkhv->bqhv', a.astype(v.dtype), v)

    o = lax.map(block, qb)
    o = jnp.moveaxis(o, 0, 1).reshape(B, Tq, N_HEADS, V_DIM)
    o = rms_norm(o, g_subln) * (1.0 - lam_init)
    return o.reshape(B, Tq, ATTN_W)

def fourier_mix(f, w_fnet):
    B, T = f.shape[0], f.shape[1]
    fg = f.astype(jnp.float32).reshape(B, T, F_GROUPS, F_CH)
    mixed = jnp.fft.fft2(fg, axes=(1, 3), norm="ortho").real.astype(f.dtype)
    return jnp.einsum('btgc,gce->btge', mixed, w_fnet).reshape(B, T, FOURIER_W)

def swiglu(x, w_gate, w_up, w_down):
    return (jax.nn.silu(x @ w_gate) * (x @ w_up)) @ w_down

def moe_ffn(x, w_router, e_gate, e_up, e_down):
    logits = jnp.einsum('btd,de->bte', x, w_router, preferred_element_type=jnp.float32)
    top_v, top_i = lax.top_k(logits, TOP_K)
    w = jax.nn.softmax(top_v, axis=-1)
    gates = jnp.sum(jax.nn.one_hot(top_i, N_EXPERTS, dtype=jnp.float32) * w[..., None], axis=-2)
    out = jnp.zeros(x.shape, jnp.float32)
    for e in range(N_EXPERTS):
        out = out + gates[..., e:e + 1] * swiglu(x, e_gate[e], e_up[e], e_down[e]).astype(jnp.float32)
    return out.astype(x.dtype)

def run_layer(x, cond, l, P, rope, ctx_k, ctx_v):
    B, T, _ = x.shape
    lam_init = 0.8 - 0.6 * math.exp(-0.3 * l)
    mod = jnp.einsum('bd,de->be', jax.nn.silu(cond.astype(jnp.float32)),
                     P['w_ada'][l].astype(jnp.float32)) + P['b_ada'][l].astype(jnp.float32)
    mod = mod.astype(x.dtype)[:, None, :]
    sh_a, sc_a, gt_a, sh_f, sc_f, gt_f = jnp.split(mod, N_MOD, axis=-1)

    hn = rms_norm(x, P['g_attn_pre'][l]) * (1 + sc_a) + sh_a
    proj = hn @ P['w_in'][l]
    q = proj[..., :QK_W].reshape(B, T, N_HEADS, 2, QK_DIM)
    k = proj[..., QK_W:2 * QK_W].reshape(B, T, N_HEADS, 2, QK_DIM)
    v = proj[..., 2 * QK_W:2 * QK_W + ATTN_W].reshape(B, T, N_HEADS, V_DIM)
    f = proj[..., 2 * QK_W + ATTN_W:]
    lp = P['lam_params'][l].astype(jnp.float32)
    lam = jnp.exp(jnp.sum(lp[0] * lp[1])) - jnp.exp(jnp.sum(lp[2] * lp[3])) + lam_init
    if rope is None:
        keys, vals = k, v
        qr = q
    else:
        cos, sin = rope
        qr = apply_axial_rope(q, cos, sin)
        keys = jnp.concatenate([ctx_k.astype(k.dtype), apply_axial_rope(k, cos, sin)], axis=1)
        vals = jnp.concatenate([ctx_v.astype(v.dtype), v], axis=1)
    attn_o = diff_attention(qr, keys, vals, lam, P['g_subln'][l], lam_init)
    four_o = fourier_mix(f, P['w_fnet'][l])
    mixed = jnp.concatenate([attn_o, four_o], axis=-1) @ P['w_out'][l]
    x = x + gt_a * rms_norm(mixed, P['g_attn_post'][l])

    hn = rms_norm(x, P['g_ffn_pre'][l]) * (1 + sc_f) + sh_f
    i = l // 2
    if l % 2 == 0:
        ff = swiglu(hn, P['w_gate'][i], P['w_up'][i], P['w_down'][i])
    else:
        ff = moe_ffn(hn, P['w_router'][i], P['e_gate'][i], P['e_up'][i], P['e_down'][i])
    x = x + gt_f * rms_norm(ff, P['g_ffn_post'][l])
    return x, k, v

def setup_inputs(seed: int = 0) -> dict:
    key = jax.random.key(seed)
    ks = jax.random.split(key, 24)
    D = D_MODEL

    def nrm(k, shape, s):
        return jax.random.normal(k, shape, jnp.float32) * s

    return {
        "x_prompt": nrm(ks[0], (BATCH, SEQ, D), 1.0),
        "x_sample": nrm(ks[1], (DEC_BATCH, DEC_SEQ, D), 1.0),
        "cache_k": nrm(ks[2], (DEC_BATCH, DEPTH, PAST_LEN, N_HEADS, 2, QK_DIM), 1.0),
        "cache_v": nrm(ks[3], (DEC_BATCH, DEPTH, PAST_LEN, N_HEADS, V_DIM), 1.0),
        "c": nrm(ks[4], (DEC_BATCH, D), 1.0),
        "c_ctx": nrm(ks[5], (D,), 1.0),
        "g_attn_pre": 1.0 + nrm(ks[6], (DEPTH, D), 0.05),
        "g_attn_post": 1.0 + nrm(ks[7], (DEPTH, D), 0.05),
        "g_ffn_pre": 1.0 + nrm(ks[8], (DEPTH, D), 0.05),
        "g_ffn_post": 1.0 + nrm(ks[9], (DEPTH, D), 0.05),
        "w_ada": nrm(ks[10], (DEPTH, D, N_MOD * D), 0.5 * D ** -0.5),
        "b_ada": nrm(ks[11], (DEPTH, N_MOD * D), 0.01),
        "w_in": nrm(ks[12], (DEPTH, D, IN_W), D ** -0.5),
        "lam_params": nrm(ks[13], (DEPTH, 4, QK_DIM), 0.1),
        "g_subln": 1.0 + nrm(ks[14], (DEPTH, V_DIM), 0.05),
        "w_fnet": nrm(ks[15], (DEPTH, F_GROUPS, F_CH, F_CH), F_CH ** -0.5),
        "w_out": nrm(ks[16], (DEPTH, MIX_W, D), MIX_W ** -0.5),
        "w_gate": nrm(ks[17], (N_DENSE, D, D_FF), D ** -0.5),
        "w_up": nrm(ks[18], (N_DENSE, D, D_FF), D ** -0.5),
        "w_down": nrm(ks[19], (N_DENSE, D_FF, D), D_FF ** -0.5),
        "w_router": nrm(ks[20], (N_MOE, D, N_EXPERTS), D ** -0.5),
        "e_gate": nrm(ks[21], (N_MOE, N_EXPERTS, D, D_FF_E), D ** -0.5),
        "e_up": nrm(ks[22], (N_MOE, N_EXPERTS, D, D_FF_E), D ** -0.5),
        "e_down": nrm(ks[23], (N_MOE, N_EXPERTS, D_FF_E, D), D_FF_E ** -0.5),
    }

def reference(x_prompt, x_sample, cache_k, cache_v, c, c_ctx, g_attn_pre, g_attn_post, g_ffn_pre,
              g_ffn_post, w_ada, b_ada, w_in, lam_params, g_subln, w_fnet, w_out, w_gate, w_up, w_down,
              w_router, e_gate, e_up, e_down):
    P = {
        'g_attn_pre': g_attn_pre, 'g_attn_post': g_attn_post, 'g_ffn_pre': g_ffn_pre,
        'g_ffn_post': g_ffn_post, 'w_ada': w_ada, 'b_ada': b_ada, 'w_in': w_in,
        'lam_params': lam_params, 'g_subln': g_subln, 'w_fnet': w_fnet, 'w_out': w_out,
        'w_gate': w_gate, 'w_up': w_up, 'w_down': w_down, 'w_router': w_router,
        'e_gate': e_gate, 'e_up': e_up, 'e_down': e_down,
    }
    h = x_prompt
    ks_list = []
    vs_list = []
    for l in range(DEPTH):
        h, k_l, v_l = run_layer(h, c_ctx[None, :], l, P, None, None, None)
        ks_list.append(k_l)
        vs_list.append(v_l)
    y_prompt = h
    new_cache_k = jnp.stack(ks_list, axis=1)
    new_cache_v = jnp.stack(vs_list, axis=1)

    rope = axial_rope_tables(x_sample.shape[1])
    h = x_sample
    for l in range(DEPTH):
        h, _, _ = run_layer(h, c, l, P, rope, cache_k[:, l], cache_v[:, l])
    y_sample = h
    return (y_prompt, y_sample, new_cache_k, new_cache_v)


_drawn_inputs = setup_inputs


def setup_inputs(seed=0):
    import zlib

    import numpy as np

    out = dict(_drawn_inputs(seed))
    spreads = {}
    factors = {}
    for name, (base, spread) in spreads.items():
        noise = np.random.default_rng([zlib.crc32(name.encode()), seed]).standard_normal(out[name].shape)
        drawn = base * np.exp(spread * noise) if base else spread * noise
        out[name] = __import__('jax').numpy.asarray(drawn.astype(out[name].dtype))
    for name, factor in factors.items():
        out[name] = (out[name] * factor).astype(out[name].dtype)
    return out
```

```python
import math
from contextlib import ExitStack

import numpy as np
import concourse.bass as bass
from concourse import mybir
from concourse.alu_op_type import AluOpType as ALU

F32 = mybir.dt.float32
F32R = mybir.dt.float32r
U32 = mybir.dt.uint32
ACT = mybir.ActivationFunctionType
AX = mybir.AxisListType

D = 1024
KC = D // 128
L = 2
T_LAT, T_CTX, PAST = 512, 128, 128
T = T_LAT + T_CTX
NT = T // 128
H, QK, V = 4, 64, 128
G = 4
F_DENSE, F_EXP, E = 2816, 1024, 8
UNIT = 2048
RING = 3
COLS = UNIT // KC
N_BLK = (F_DENSE // COLS, E * F_EXP // COLS)
EPS = 1e-6
SCALE = QK ** -0.5
HALF = T // 2
BANK = 512
ADA_STEPS = ((1, 1, 1, 1, 2), (1, 1, 1, 1, 0))
SH_A, SC_A, GT_A, SH_F, SC_F, GT_F = range(6)
V_BADA, V_GAPRE, V_GAPOST, V_GFPRE, V_GFPOST, V_C, V_CTX, V_SUB = 0, 48, 56, 64, 72, 80, 88, 96


def plan_units():
    units = [("ada", 0, u) for u in range(8)]
    ada = [[("ada", 0, u) for u in range(8, 24)] + [("ada", 1, u) for u in range(8)],
           [("ada", 1, u) for u in range(8, 24)]]
    for l in range(L):
        units += [("in", l, u) for u in range(8)]
        units += ada[l]
        units += [("cos", l, 0), ("sin", l, 0)]
        units += [("out", l, u) for u in range(4)]
        nb = N_BLK[l]
        units += [("gate", l, 0), ("up", l, 0)]
        for b in range(1, nb):
            units += [("gate", l, b), ("up", l, b), ("down", l, b - 1)]
        units += [("down", l, nb - 1)]
    return units


def stat_no(l, kind, t=0):
    return l * 21 + {"pre_a": 0, "sub": 5, "post_a": 6, "pre_f": 11, "post_f": 16}[kind] + t + 1


def stat_col(l, kind, t=0):
    return l * 40 + {"pre_a": 0, "sub": 20, "post_a": 5, "pre_f": 10, "post_f": 15}[kind] + t


class Fills:

    def __init__(self):
        self.total = [0] * 8
        self.named = {}
        self.i, self.per = None, None

    def enter(self, i, per):
        self.i, self.per, self.at = i, per, list(self.total)

    def leave(self, n):
        for b, k in self.per.items():
            assert self.total[b] - self.at[b] == k, (b, k, self.total[b] - self.at[b])
        assert all(self.total[b] == self.at[b] for b in range(8) if b not in self.per)
        for b, k in self.per.items():
            self.total[b] = self.at[b] + n * k
        self.i = None

    def next(self, key, b):
        before, k = self.total[b], self.per.get(b, 0) if self.i is not None else 0
        self.total[b] += 1
        self.named[key] = (b, before + 1, k)
        return before if not k else before + self.i * k


def build(nc, dram, out):
    units = plan_units()
    unit_no = {u: n for n, u in enumerate(units)}
    N_UNITS = len(units)

    with ExitStack() as ctx:
        def sem(name):
            return ctx.enter_context(nc.semaphore(name))

        top = [(nc.sbuf_base + 31) // 32 * 32]

        def at(name, shape, dt, offset):
            return nc.alloc_sbuf_tensor_at(name, shape, dt, offset=offset)

        def sb(name, shape, dt=F32):
            off = top[0]
            top[0] += (int(np.prod(shape[1:])) * 4 + 31) // 32 * 32
            return at(name, shape, dt, off)

        x = sb("x", [128, NT, D])
        act_off = top[0]
        hn_h = sb("hn_h", [128, KC, T], F32R)
        hn_l = sb("hn_l", [128, KC, T], F32R)
        half_kc = KC // 2 * T * 4
        mx_h = at("mx_h", [128, KC, T], F32R, act_off)
        mx_l = at("mx_l", [128, KC, T], F32R, act_off + 2 * half_kc)
        junk = at("junk", [128, NT, D], F32, act_off)
        o_all = at("o_all", [128, NT, H * V], F32, act_off + half_kc)
        probs = at("probs", [128, 2, 2, T], F32, act_off + 3 * half_kc)
        o_sq = at("o_sq", [128, NT, H * V], F32, act_off + 3 * half_kc)
        raw = [sb(f"raw{s}", [128, UNIT]) for s in range(RING)]
        wh = [sb(f"wh{s}", [128, UNIT], F32R) for s in range(RING)]
        wl = [sb(f"wl{s}", [128, UNIT], F32R) for s in range(RING)]
        m_off = top[0]
        top[0] += 51200
        fT = at("fT", [128, G, T], F32, m_off)
        qT = at("qT", [128, H, T], F32, m_off + 10240)
        kT = at("kT", [128, H, T + PAST], F32, m_off + 20480)
        vt = at("vt", [128, NT + 1, H * V], F32, m_off + 32768)
        rope_t = at("rope_t", [128, T_LAT], F32, m_off + 45056)
        aT = at("aT", [128, 2, T], F32, m_off + 45056)
        z_h = at("z_h", [128, NT, G, 256], F32R, m_off + 10240)
        z_l = at("z_l", [128, NT, G, 256], F32R, m_off + 30720)
        sub_v = at("sub_v", [128, 2, T], F32, act_off + 3 * half_kc)
        diag = at("diag", [128, KC, 128], F32, m_off + 10240)
        nrm_v = at("nrm_v", [128, 2, T], F32, m_off)
        sg = at("sg", [128, 2, T], F32, m_off)
        hid_h = at("hid_h", [128, 2, T], F32R, m_off + 5120)
        hid_l = at("hid_l", [128, 2, T], F32R, m_off + 10240)
        acc = at("acc", [128, NT, D], F32, m_off + 25600)
        z = at("z", [128, NT, D], F32, m_off + 25600)
        gate_off = top[0]
        gate_bc = sb("gate_bc", [128, 2, D])
        w_fn = at("w_fn", [128, G * 128], F32, gate_off)
        m12 = at("m12", [128, G, 2, 128], F32, gate_off + 2048)
        NCONST = 4 * 128 + 2 * T_LAT + 8 + 2
        consts = sb("consts", [128, NCONST])
        ident, rot, c128, s128 = (consts[:, 128 * i:128 * (i + 1)] for i in range(4))
        cos_r, sin_r = consts[:, 512:512 + T_LAT], consts[:, 512 + T_LAT:512 + 2 * T_LAT]
        iota8 = consts[:, 512 + 2 * T_LAT:512 + 2 * T_LAT + 8]
        sel4 = consts[0:4, NCONST - 2:NCONST]
        dft_h = sb("dft_h", [128, 2 * 128], F32R)
        dft_l = sb("dft_l", [128, 2 * 128], F32R)
        ones = sb("ones", [128, 128])
        vcol = sb("vcol", [128, L, 128])
        modc = sb("modc", [128, L, 48, 2])
        mulc = sb("mulc", [128, 2 * L, KC, 2])
        arow = sb("arow", [4, COLS])
        cond_s = sb("cond_s", [128, KC, 2])
        cond_p = sb("cond_p", [128, KC, 4], F32R)
        ssq = sb("ssq", [128, L * 40])
        msq = sb("msq", [128, L * 40])
        rstd = sb("rstd", [128, L * 40])
        mhalf = sb("mhalf", [128, 20])
        lamt = sb("lamt", [64, L, 4])
        lam2 = sb("lam2", [64, L, 2])
        lame = sb("lame", [128, L, 2])
        nlam = sb("nlam", [128, L])
        gsub = sb("gsub", [128, L])
        smx = sb("smx", [128, 2])
        nmx = sb("nmx", [128, 2])
        ssum = sb("ssum", [128, 2])
        rsum = sb("rsum", [128, 2])
        rneg = sb("rneg", [128, 1])
        gcol = sb("gcol", [128, KC, 2])
        w_rt = sb("w_rt", [128, KC, E])
        rt_h = sb("rt_h", [128, KC, E], F32R)
        rt_l = sb("rt_l", [128, KC, E], F32R)
        logit = sb("logit", [128, NT, E])
        top8 = sb("top8", [128, NT, 8])
        idx8 = sb("idx8", [128, NT, 8], U32)
        idxf = sb("idxf", [128, NT, 2])
        gdif = sb("gdif", [128, NT])
        gexp = sb("gexp", [128, NT])
        gden = sb("gden", [128, NT])
        g12 = sb("g12", [128, NT, 2])
        gsel = sb("gsel", [128, NT, E])
        gates = sb("gates", [128, NT, E])
        gates_b = sb("gates_b", [128, NT, E, N_BLK[1] // E])
        assert top[0] <= nc.sbuf_usable_end, top[0]

        ps = ctx.enter_context(nc.psum_tensor("ps", [128, 8 * BANK], F32))

        def bank(b, lo, hi):
            return ps[:, b * BANK + lo:b * BANK + hi]

        def pair(b):
            return ps[:, b * BANK:(b + 2) * BANK].rearrange("p (a n) -> p a n", a=2)[:, :, 0:HALF]

        raw_landed = [sem(f"raw_landed{s}") for s in range(RING)]
        wh_ready, wl_ready = sem("wh_ready"), sem("wl_ready")
        sums_used = sem("sums_used")
        bank_full = [sem(f"bank_full{b}") for b in range(8)]
        bank_free = [sem(f"bank_free{b}") for b in range(8)]
        params_landed, x_landed = sem("params_landed"), sem("x_landed")
        cache_landed, stored = sem("cache_landed"), sem("stored")
        pool_const, pool_step = sem("pool_const"), sem("pool_step")
        cond_act, cond_ready = sem("cond_act"), sem("cond_ready")
        act_const = sem("act_const")
        dft_ready = sem("dft_ready")
        arow_ready, mod_ready, mul_ready = sem("arow_ready"), sem("mod_ready"), sem("mul_ready")
        ssq_ready, rstd_ready = sem("ssq_ready"), sem("rstd_ready")
        z_ready = sem("z_ready")
        nrm_v_ready, nrm_h_ready, hn_ready = sem("nrm_v_ready"), sem("nrm_h_ready"), sem("hn_ready")
        q_out, k_out, f_out, v_out = sem("q_out"), sem("k_out"), sem("f_out"), sem("v_out")
        rope_ready = sem("rope_ready")
        nmax_ready, exp_ready, a_ready, aT_ready = sem("nmax_ready"), sem("exp_ready"), sem("a_ready"), sem("aT_ready")
        o_ready = sem("o_ready")
        sub_v_ready, sub_h_ready, mxa_ready = sem("sub_v_ready"), sem("sub_h_ready"), sem("mxa_ready")
        m12_ready = sem("m12_ready")
        zh_ready, zl_ready = sem("zh_ready"), sem("zl_ready")
        mf_h_ready, mf_ready = sem("mf_h_ready"), sem("mf_ready")
        y_ready, x_ready = sem("y_ready"), sem("x_ready")
        diag_ready, gate_ready = sem("diag_ready"), sem("gate_ready")
        lam_v, lam_e = sem("lam_v"), sem("lam_e")
        sg_ready, hv_ready, hid_h_ready, hid_ready = sem("sg_ready"), sem("hv_ready"), sem("hid_h_ready"), sem("hid_ready")
        acc_zero = sem("acc_zero")
        gexp_ready = sem("gexp_ready")
        dve_step = sem("dve_step")
        act_step = sem("act_step")

        fills = Fills()
        block = ctx.enter_context(nc.Block())

        hid_base = [0, 2 * N_BLK[0]]

        @block.tensor
        def _(pe):
            mm = nc.tensor.matmul

            def fill(key, b):
                before = fills.next(key, b)
                if not (isinstance(before, int) and before == 0):
                    pe.wait_ge(bank_free[b], before)

            def all_read():
                for b in range(8):
                    if fills.total[b]:
                        pe.wait_ge(bank_free[b], fills.total[b])

            def three(outs, w_of, x_of, keys, sl, ks):
                for k in ks:
                    for hi, xs in ((wh, (hn_h, hn_l)), (wl, (hn_h,))):
                        for xp in xs:
                            for o, xc in zip(outs, x_of):
                                last = mm(o, w_of(hi[sl], k), xp[:, k, xc[0]:xc[1]],
                                          start=(k == ks[0] and hi is wh and xp is hn_h),
                                          stop=(k == ks[-1] and hi is wl))
                return last

            def ada(n):
                _, l, u = units[n]
                s = n % RING
                pe.wait_ge(wl_ready, n + 1)
                fill(("ada_row", l, u), 7)
                for k in range(KC):
                    for w in (wh, wl):
                        last = mm(ps[0:4, 7 * BANK:7 * BANK + COLS], cond_p[:, k, :], w[s][:, k * COLS:(k + 1) * COLS],
                                  start=(k == 0 and w is wh), stop=(k == KC - 1 and w is wl))
                last.then_inc(bank_full[7], 1)
                pe.wait_ge(arow_ready, l * 24 + u + 1)
                fill(("ada_col", l, u), 7)
                for j in range(2):
                    last = mm(bank(7, 2 * j, 2 * j + 2), arow[:, j * 128:(j + 1) * 128], sel4,
                              start=True, stop=True)
                last.then_inc(bank_full[7], 1)

            def turn_norm(l, kind):
                all_read()
                m = 2 * l + (kind == "pre_f")
                pe.wait_ge(z_ready, NT * (m + 1))
                for c in range(KC):
                    b = 2 * (c % 4)
                    fill(("turn", m, c), b)
                    for t in range(NT):
                        last = nc.tensor.transpose(bank(b, t * 128, (t + 1) * 128), z[:, t, c * 128:(c + 1) * 128], ident)
                    last.then_inc(bank_full[b], 1)
                all_read()

            def proj_in(l):
                pe.wait_ge(hn_ready, KC * (2 * l + 1))
                for u in range(6):
                    n = unit_no["in", l, u]
                    pe.wait_ge(wl_ready, n + 1)
                    for j in range(2):
                        c = 2 * u + j
                        b = 2 * (c % 4)
                        fill(("in", l, c), b)
                        three([bank(b, 0, HALF), bank(b + 1, 0, HALF)],
                              lambda w, k, j=j: w[:, k * COLS + j * 128:k * COLS + j * 128 + 128],
                              [(0, HALF), (HALF, T)], None, n % RING, range(KC)).then_inc(bank_full[b], 1)
                all_read()
                for c in range(2 * H):
                    pe.wait_ge(q_out if c % 2 == 0 else k_out, H * l + c // 2 + 1)
                    fill(("rot", l, c), c)
                    mm(bank(c, 0, T_LAT), rot, (qT if c % 2 == 0 else kT)[:, c // 2, 0:T_LAT],
                       start=True, stop=True).then_inc(bank_full[c], 1)
                for u in range(6, 8):
                    n = unit_no["in", l, u]
                    pe.wait_ge(wl_ready, n + 1)
                    for t in range(NT):
                        b = (5 * (u - 6) + t) % 8
                        fill(("val", l, u - 6, t), b)
                        for k in range(KC):
                            for i, (xp, w) in enumerate(((hn_h, wh), (hn_h, wl), (hn_l, wh))):
                                last = mm(bank(b, 0, COLS), xp[:, k, t * 128:(t + 1) * 128],
                                          w[n % RING][:, k * COLS:(k + 1) * COLS],
                                          start=(k == 0 and i == 0), stop=(k == KC - 1 and i == 2))
                        last.then_inc(bank_full[b], 1)
                all_read()

            def attention(l):
                n = unit_no["in", l, 7] + 1
                pe.wait_ge(v_out, 2 * NT * (l + 1))
                pe.wait_ge(cache_landed, 32 * (l + 1))
                steps = [(h, t) for h in range(H) for t in range(NT)]

                def values(s):
                    h, t = steps[s]
                    no = 20 * l + s
                    tiles = [0, 1, 2, 3, 5] if t < 4 else [4]
                    pe.wait_ge(a_ready, no + 1)
                    fill(("aT", l, s), 4)
                    for i in range(len(tiles)):
                        last = nc.tensor.transpose(bank(4, i * 128, (i + 1) * 128), probs[:, s % 2, 0, i * 128:(i + 1) * 128], ident)
                    last.then_inc(bank_full[4], 1)
                    pe.wait_ge(aT_ready, no + 1)
                    fill(("o", l, s), 6)
                    for i, kt in enumerate(tiles):
                        last = mm(bank(6, 0, V), aT[:, s % 2, i * 128:(i + 1) * 128], vt[:, kt, h * V:(h + 1) * V],
                                  start=(i == 0), stop=(i == len(tiles) - 1))
                    last.then_inc(bank_full[6], 1)

                for s, (h, t) in enumerate(steps):
                    pe.wait_ge(rope_ready, 2 * H * l + 2 * h + 2)
                    fill(("score", l, s), 0)
                    for m in range(2):
                        q = qT[64 * m:64 * m + 64, h, t * 128:(t + 1) * 128]
                        if t < 4:
                            for j in range(2):
                                last = mm(bank(2 * m + j, 0, HALF), q, kT[64 * m:64 * m + 64, h, j * HALF:(j + 1) * HALF],
                                          start=True, stop=True)
                        else:
                            last = mm(bank(2 * m, 0, T_CTX), q, kT[64 * m:64 * m + 64, h, T:T + T_CTX],
                                      start=True, stop=True)
                    last.then_inc(bank_full[0], 1)
                    for _ in range(ADA_STEPS[l][t]):
                        ada(n)
                        n += 1
                    if s:
                        values(s - 1)
                values(len(steps) - 1)
                assert n == unit_no["cos", l, 0], (l, n, unit_no["cos", l, 0])
                all_read()

            def fourier(l):
                for i, m in enumerate((c128, s128)):
                    fill(("m12", l, i), i)
                    mm(bank(i, 0, 512), m, w_fn[:, :], start=True, stop=True).then_inc(bank_full[i], 1)
                pe.wait_ge(m12_ready, 2 * (l + 1))
                for t in range(NT):
                    for g2 in range(2):
                        b = 2 + (2 * t + g2) % 6
                        fill(("z", l, t, g2), b)
                        for g in (2 * g2, 2 * g2 + 1):
                            last = mm(bank(b, 256 * (g % 2), 256 * (g % 2) + 256), fT[:, g, t * 128:(t + 1) * 128],
                                      m12[:, g, :, :].rearrange("p a e -> p (a e)"), start=True, stop=True)
                        last.then_inc(bank_full[b], 1)
                all_read()
                pe.wait_ge(o_ready, 20 * (l + 1) + l + 1)
                for h in range(H):
                    b = 2 * h
                    fill(("sub", l, h), b)
                    for t in range(NT):
                        last = nc.tensor.transpose(bank(b, t * 128, (t + 1) * 128), o_all[:, t, h * V:(h + 1) * V], ident)
                    last.then_inc(bank_full[b], 1)
                all_read()
                pe.wait_ge(zl_ready, 2 * NT * (l + 1))
                for i, name in enumerate(("cos", "sin")):
                    n = unit_no[name, l, 0]
                    pe.wait_ge(wl_ready, n + 1)
                    for g in range(G):
                        if i == 0:
                            fill(("mf", l, g), g)
                        for t in range(4):
                            for j, (zz, w) in enumerate(((z_h, wh), (z_h, wl), (z_l, wh))):
                                last = mm(bank(g, 0, T_LAT), zz[:, t, g, i * 128:(i + 1) * 128],
                                          w[n % RING][:, t * 512:(t + 1) * 512],
                                          start=(i == 0 and t == 0 and j == 0), stop=(i == 1 and t == 3 and j == 2),
                                          skip_group_check=True)
                        if i == 1:
                            last.then_inc(bank_full[g], 1)
                        elif g == G - 1:
                            last.then_inc(sums_used, 1)
                fill(("mfc", l), 4)
                for g in range(G):
                    for i in range(2):
                        for j, (zz, w) in enumerate(((z_h, dft_h), (z_h, dft_l), (z_l, dft_h))):
                            last = mm(bank(4, g * 128, (g + 1) * 128), zz[:, 4, g, i * 128:(i + 1) * 128],
                                      w[:, i * 128:(i + 1) * 128], start=(i == 0 and j == 0), stop=(i == 1 and j == 2))
                last.then_inc(bank_full[4], 1)
                all_read()

            def gate_rows(g):
                for cond in range(2):
                    pe.wait_ge(diag_ready, 2 * g + cond + 1)
                    for hf in range(2):
                        b = 6 + hf
                        fill(("gate_bc", g, cond, hf), b)
                        for c in range(4):
                            last = mm(bank(b, c * 128, (c + 1) * 128), ones[:, :], diag[:, 4 * hf + c, :],
                                      start=True, stop=True)
                        last.then_inc(bank_full[b], 1)

            def proj_out(l):
                gate_rows(2 * l)
                all_read()
                pe.wait_ge(mf_ready, 2 * G * (l + 1))
                pe.wait_ge(mxa_ready, H * (l + 1))
                for hf in range(2):
                    for kh in range(2):
                        n = unit_no["out", l, 2 * hf + kh]
                        pe.wait_ge(wl_ready, n + 1)
                        for t in range(NT):
                            b = (5 * hf + t) % 8
                            if kh == 0:
                                fill(("mix", l, hf, t), b)
                            for k in range(4):
                                for j, (xp, w) in enumerate(((mx_h, wh), (mx_h, wl), (mx_l, wh))):
                                    last = mm(bank(b, 0, 512), xp[:, 4 * kh + k, t * 128:(t + 1) * 128],
                                              w[n % RING][:, k * 512:(k + 1) * 512],
                                              start=(kh == 0 and k == 0 and j == 0), stop=(kh == 1 and k == 3 and j == 2),
                                              skip_group_check=True)
                            if kh == 1:
                                last.then_inc(bank_full[b], 1)
                            elif t == NT - 1:
                                last.then_inc(sums_used, 1)

            def hidden(l, key, n0, i, slots, k):
                for part, name in enumerate(("gate", "up")):
                    pe.wait_ge(wl_ready, n0 + part + 1 + i * k)
                    for j in range(2):
                        b = 2 * j
                        fill((key, name, j), b)
                        three([bank(b, 0, HALF), bank(b + 1, 0, HALF)],
                              lambda w, kk, j=j: w[:, kk * COLS + j * 128:kk * COLS + j * 128 + 128],
                              [(0, HALF), (HALF, T)], None, slots[part], range(KC)).then_inc(bank_full[b], 1)

            def down(l, key, n, i, slot, k):
                pe.wait_ge(wl_ready, n + 1 + i * k)
                pe.wait_ge(hid_ready, hid_base[l] + 2 + (i * 2 if k else 2 * (N_BLK[l] - 1)))
                for t in range(NT):
                    for hf in range(2):
                        r = 2 * t + hf
                        b = 4 + r % 4
                        fill((key, "down", r), b)
                        for f in range(2):
                            for j, (xp, w) in enumerate(((hid_h, wh), (hid_h, wl), (hid_l, wh))):
                                last = mm(bank(b, 0, 512), xp[:, f, t * 128:(t + 1) * 128],
                                          w[slot][:, f * D + hf * 512:f * D + hf * 512 + 512],
                                          start=(f == 0 and j == 0), stop=(f == 1 and j == 2))
                        last.then_inc(bank_full[b], 1)

            def channel(l):
                nb = N_BLK[l]
                gate_rows(2 * l + 1)
                pe.wait_ge(hn_ready, KC * (2 * l + 2))
                all_read()
                if l == 1:
                    fill(("router",), 0)
                    for t in range(NT):
                        for k in range(KC):
                            for j, (xp, w) in enumerate(((hn_h, rt_h), (hn_h, rt_l), (hn_l, rt_h))):
                                last = mm(bank(0, t * E, (t + 1) * E), xp[:, k, t * 128:(t + 1) * 128], w[:, k, :],
                                          start=(k == 0 and j == 0), stop=(k == KC - 1 and j == 2))
                    last.then_inc(bank_full[0], 1)
                    all_read()
                n0 = unit_no["gate", l, 0]
                hidden(l, ("first", l), n0, 0, [n0 % RING, (n0 + 1) % RING], 0)
                with pe.Fori(0, nb - 1) as i:
                    fills.enter(i, {0: 2, 2: 2, 4: 3, 5: 3, 6: 2, 7: 2})
                    hidden(l, ("body", l), n0 + 2, i, [(n0 + 2) % RING, n0 % RING], 3)
                    down(l, ("body", l), n0 + 4, i, (n0 + 1) % RING, 3)
                    fills.leave(nb - 1)
                n = unit_no["down", l, nb - 1]
                down(l, ("last", l), n, 0, n % RING, 0)

            pe.wait_ge(params_landed, 80)
            pe.wait_ge(pool_const, 2)
            fill(("lam",), 0)
            pe.wait_ge(lam_v, 1)
            mm(bank(0, 0, 2 * L), ones[0:64, :], lam2[:, :, :].rearrange("p l a -> p (l a)"),
               start=True, stop=True).then_inc(bank_full[0], 1)
            pe.wait_ge(cond_ready, 1)
            pe.wait_ge(dft_ready, 1)
            for u in range(8):
                ada(u)
            for l in range(L):
                turn_norm(l, "pre_a")
                proj_in(l)
                attention(l)
                fourier(l)
                proj_out(l)
                turn_norm(l, "pre_f")
                channel(l)

        def full(eng, key, i=0, back=0):
            b, first, k = fills.named[key]
            first -= back * k
            eng.wait_ge(bank_full[b], first + i * k if k else first)

        def multiplied(eng, n):
            kind, l, u = units[n]
            nb = N_BLK[l]
            if kind == "cos" or (kind == "out" and u % 2 == 0):
                eng.wait_ge(sums_used, 3 * l + {"cos": 1, "out": 2 + u // 2}[kind])
            elif kind == "ada":
                full(eng, ("ada_row", l, u))
            elif kind == "in":
                full(eng, ("in", l, 2 * u + 1) if u < 6 else ("val", l, u - 6, NT - 1))
            elif kind == "sin":
                full(eng, ("mf", l, G - 1))
            elif kind == "out":
                full(eng, ("mix", l, u // 2, NT - 1))
            elif kind == "down":
                full(eng, (("body", l) if u < nb - 1 else ("last", l), "down", 2 * NT - 1), u)
            else:
                full(eng, (("body", l) if u else ("first", l), kind, 1), u - 1)

        def free(ins, key):
            ins.then_inc(bank_free[fills.named[key][0]], 1)

        @block.sync
        def _(sp):
            sp.dma_start(consts[:, :], dram["consts"]).then_inc(params_landed, 16)
            sp.dma_start(vcol[:, :, :], dram["vcol"]).then_inc(params_landed, 16)
            sp.dma_start(lamt[:, :, :], dram["lam"]).then_inc(params_landed, 16)
            sp.dma_start(w_rt[:, :, :], dram["w_router"]).then_inc(params_landed, 16)
            sp.dma_start(w_fn[:, :], dram["w_fnet"][0]).then_inc(params_landed, 16)
            sp.dma_start(x[:, :, :], dram["x"]).then_inc(x_landed, 16)

            def unit(n, i=0, k=0, slot=None):
                s = n % RING
                if k or n >= RING:
                    sp.wait_ge(wl_ready, n - RING + 1 + i * k)
                src = dram["stream"][n] if not k else dram["stream"][bass.ds(n + i * k, 1)].rearrange("a p n -> p (a n)")
                sp.dma_start(raw[s][:, :], src).then_inc(raw_landed[s], 16)

            n = 0
            for l in range(L):
                first = unit_no["in", l, 0]
                while n < first + RING + 1:
                    unit(n)
                    n += 1
                multiplied(sp, first)
                sp.dma_start(kT[:, :, T_LAT:T], dram["cache_k"][l]).then_inc(cache_landed, 16)
                sp.dma_start(vt[:, NT, :], dram["cache_v"][l]).then_inc(cache_landed, 16)
                ready = unit_no["in", l, 7] + 1
                while n < ready + RING:
                    unit(n)
                    n += 1
                sp.wait_ge(k_out, H * (l + 1))
                sp.wait_ge(v_out, 2 * NT * (l + 1))
                sp.dma_start(out["new_k"][l], kT[:, :, T:T + T_CTX]).then_inc(stored, 16)
                sp.dma_start(out["new_v"][l], vt[:, 4, :]).then_inc(stored, 16)
                if l == 1:
                    sp.wait_ge(x_ready, 2 * NT)
                    sp.dma_start(w_fn[:, :], dram["w_fnet"][1]).then_inc(params_landed, 16)
                body = unit_no["gate", l, 0] + 2 + RING
                while n < body:
                    unit(n)
                    n += 1
                trips = (unit_no["down", l, N_BLK[l] - 1] - n) // RING
                with sp.Fori(0, trips) as i:
                    for j in range(RING):
                        unit(n + j, i, RING)
                n += trips * RING
                while n <= unit_no["down", l, N_BLK[l] - 1]:
                    unit(n)
                    n += 1
            for t in range(NT):
                sp.wait_ge(x_ready, NT * 3 + t + 1)
                sp.dma_start(out["y"][:, t, :], x[:, t, :]).then_inc(stored, 16)
            sp.wait_ge(stored, 16 * (2 * L + NT))

        @block.gpsimd
        def _(pool):
            nc.gpsimd.memset(ones[:, :], 1.0).then_inc(pool_const, 1)
            nc.gpsimd.memset(mhalf[:, :], -0.5).then_inc(pool_const, 1)
            pool.wait_ge(pool_const, 2)
            steps = [0]

            def split(n, i=0, k=0):
                s = n % RING
                pool.wait_ge(wh_ready, n + 1 + i * k)
                nc.gpsimd.tensor_tensor(wl[s][:, :], raw[s][:, :], wh[s][:, :].bitcast(F32), ALU.subtract).then_inc(wl_ready, 1)

            def rsqrt(l, kind, width, no, count=1):
                c = stat_col(l, kind, no)
                pool.wait_ge(ssq_ready, stat_no(l, kind, no))
                nc.gpsimd.tensor_scalar(msq[:, c:c + count], ssq[:, c:c + count], 1.0 / width, EPS, ALU.mult, ALU.add).then_inc(pool_step, 1)
                steps[0] += 1
                pool.wait_ge(pool_step, steps[0])
                nc.gpsimd.tensor_tensor(rstd[:, c:c + count], msq[:, c:c + count], mhalf[:, 0:count], ALU.pow).then_inc(rstd_ready, 1)

            n = 0

            def upto(n1):
                nonlocal n
                while n < n1:
                    split(n)
                    n += 1

            for l in range(L):
                if l == 0:
                    for t in range(NT):
                        rsqrt(0, "pre_a", D, t)
                upto(unit_no["in", l, 0])
                if l == 1:
                    pass
                upto(unit_no["cos", l, 0] + 2)
                rsqrt(l, "sub", V, 0, 20)
                upto(unit_no["gate", l, 0] + 2)
                for kind in ("post_a", "pre_f"):
                    for t in range(NT):
                        rsqrt(l, kind, D, t)
                last = unit_no["down", l, N_BLK[l] - 1]
                trips = (last + 1 - n) // RING
                with pool.Fori(0, trips) as i:
                    for j in range(RING):
                        split(n + j, i, RING)
                n += trips * RING
                upto(last + 1)
                if l + 1 < L:
                    upto(last + 3)
                for t in range(NT):
                    rsqrt(l, "post_f", D, t)
                if l + 1 < L:
                    for t in range(NT):
                        rsqrt(l + 1, "pre_a", D, t)

        @block.scalar
        def _(act):
            chain = [0]

            def split(n, i=0, k=0):
                s = n % RING
                act.wait_ge(raw_landed[s], 16 * (n // RING + 1) + i * 16 * (k // RING))
                if not k and n >= RING:
                    multiplied(act, n - RING)
                nc.scalar.copy(wh[s][:, :], raw[s][:, :]).then_inc(wh_ready, 1)

            def squares(l, kind, src):
                for t in range(NT):
                    if src is x:
                        upd = {"pre_a": 2 * l, "pre_f": 2 * l + 1}[kind]
                        if upd == 0:
                            act.wait_ge(x_landed, 16)
                        else:
                            act.wait_ge(x_ready, NT * (upd - 1) + t + 1)
                    c = stat_col(l, kind, t)
                    nc.scalar.activation(junk[:, t, :], src[:, t, :], ACT.Square, accum_out=ssq[:, c:c + 1]).then_inc(ssq_ready, 1)

            def norm_high(l, kind):
                m = 2 * l + (kind == "pre_f")
                for c in range(KC):
                    act.wait_ge(nrm_v_ready, KC * m + c + 1)
                    nc.scalar.copy(hn_h[:, c, :], nrm_v[:, c % 2, :]).then_inc(nrm_h_ready, 1)

            n = 0

            def ahead(stage):
                nonlocal n
                while n < min(stage + RING, N_UNITS):
                    split(n)
                    n += 1

            act.wait_ge(params_landed, 80)
            cs = cond_s[:, :, :]
            vc = vcol[:, 0, V_C:V_C + 16].rearrange("p (a c) -> p c a", a=2)
            nc.scalar.activation(cs, vc, ACT.Silu).then_inc(cond_act, 1)
            act.wait_ge(cond_act, 1)
            nc.scalar.copy(cond_p[:, :, 0:2], cs).then_inc(cond_act, 1)
            nc.scalar.copy(dft_h[:, :], consts[:, 256:512]).then_inc(act_const, 1)
            nc.scalar.copy(rt_h[:, :, :], w_rt[:, :, :]).then_inc(act_const, 1)
            full(act, ("lam",))
            free(nc.scalar.activation(lame[:, :, :].rearrange("p l a -> p (l a)"), bank(0, 0, 2 * L), ACT.Exp), ("lam",))
            squares(0, "pre_a", x)
            for u in range(8):
                ahead(u)
            for l in range(L):
                n_in = unit_no["in", l, 0]
                norm_high(l, "pre_a")
                for u in range(6):
                    ahead(n_in + u)
                    for j in range(2):
                        c = 2 * u + j
                        if c < 4:
                            full(act, ("in", l, c))
                            nc.scalar.copy(qT[:, c, :].rearrange("p (a n) -> p a n", a=2), pair(2 * (c % 4))).then_inc(q_out, 1)
                            act.wait_ge(q_out, H * l + c + 1)
                            act.nop().then_inc(bank_free[2 * (c % 4)], 1)
                        if c >= 8:
                            full(act, ("in", l, c))
                            nc.scalar.copy(fT[:, c - 8, :].rearrange("p (a n) -> p a n", a=2), pair(2 * (c % 4))).then_inc(f_out, 1)
                            act.wait_ge(f_out, G * l + c - 8 + 1)
                            act.nop().then_inc(bank_free[2 * (c % 4)], 1)
                for u in range(6, 8):
                    ahead(n_in + u)
                nu = n_in + 8

                def turned(s):
                    full(act, ("aT", l, s))
                    w = T if s % NT < 4 else 128
                    nc.scalar.copy(aT[:, s % 2, 0:w], bank(4, 0, w)).then_inc(aT_ready, 1)
                    act.wait_ge(aT_ready, 20 * l + s + 1)
                    act.nop().then_inc(bank_free[4], 1)

                for s in range(H * NT):
                    t = s % NT
                    act.wait_ge(nmax_ready, 20 * l + s + 1)
                    for m in range(2):
                        src = pair(2 * m) if t < 4 else bank(2 * m, 0, T_CTX)
                        dst = probs[:, s % 2, m, 0:T].rearrange("p (a n) -> p a n", a=2) if t < 4 else probs[:, s % 2, m, 0:T_CTX]
                        if s >= 2 and m == 0:
                            full(act, ("aT", l, s - 2))
                        nc.scalar.activation(dst, src, ACT.Exp, bias=nmx[:, m:m + 1], scale=SCALE,
                                             accum_out=ssum[:, m:m + 1]).then_inc(exp_ready, 1)
                    act.wait_ge(exp_ready, 40 * l + 2 * s + 2)
                    act.nop().then_inc(bank_free[0], 1)
                    for _ in range(ADA_STEPS[l][t]):
                        ahead(nu)
                        nu += 1
                    if s:
                        turned(s - 1)
                turned(H * NT - 1)
                for t in range(NT):
                    for g2 in range(2):
                        full(act, ("z", l, t, g2))
                        nc.scalar.copy(z_h[:, t, 2 * g2:2 * g2 + 2, :], bank(2 + (2 * t + g2) % 6, 0, 512).rearrange("p (g e) -> p g e", g=2)).then_inc(zh_ready, 1)
                for h in range(H):
                    act.wait_ge(sub_v_ready, H * l + h + 1)
                    nc.scalar.copy(mx_h[:, h, :], sub_v[:, h % 2, :]).then_inc(sub_h_ready, 1)
                ahead(unit_no["cos", l, 0])
                ahead(unit_no["sin", l, 0])
                for g in range(G):
                    full(act, ("mf", l, g))
                    nc.scalar.copy(mx_h[:, 4 + g, 0:T_LAT], bank(g, 0, T_LAT)).then_inc(mf_h_ready, 1)
                full(act, ("mfc", l))
                nc.scalar.copy(mx_h[:, 4:8, T_LAT:T], bank(4, 0, 512).rearrange("p (g n) -> p g n", g=4)).then_inc(mf_h_ready, 1)
                for u in range(4):
                    ahead(unit_no["out", l, u])
                for t in range(NT):
                    act.wait_ge(y_ready, NT * 2 * l + t + 1)
                    if t == 0:
                        multiplied(act, unit_no["out", l, 3])
                    c = stat_col(l, "post_a", t)
                    nc.scalar.activation(junk[:, t, :], acc[:, t, :], ACT.Square, accum_out=ssq[:, c:c + 1]).then_inc(ssq_ready, 1)
                squares(l, "pre_f", x)
                norm_high(l, "pre_f")
                nb = N_BLK[l]
                if l == 1:
                    act.wait_ge(gexp_ready, 1)
                    nc.scalar.activation(gexp[:, :], gdif[:, :], ACT.Exp).then_inc(gexp_ready, 1)

                def silu(key, i, first):
                    for j in range(2):
                        full(act, (key, "gate", j), i)
                        nc.scalar.activation(sg[:, j, :].rearrange("p (a n) -> p a n", a=2), pair(2 * j), ACT.Silu).then_inc(sg_ready, 1)

                def high(i, k):
                    for j in range(2):
                        act.wait_ge(hv_ready, hid_base[l] + j + 1 + (i * 2 + 2 if k else 0))
                        nc.scalar.copy(hid_h[:, j, :], sg[:, j, :]).then_inc(hid_h_ready, 1)

                n0 = unit_no["gate", l, 0]
                ahead(n0)
                silu(("first", l), 0, True)
                act.wait_ge(sg_ready, hid_base[l] + 2)
                act.nop().then_inc(bank_free[0], 1)
                act.nop().then_inc(bank_free[2], 1)
                high(0, 0)
                nn = n
                assert nn == n0 + 3
                with act.Fori(0, nb - 1) as i:
                    full(act, (("body", l), "up", 1), i, 1)
                    split(nn, i, RING)
                    act.wait_ge(hid_ready, hid_base[l] + 2 + i * 2)
                    silu(("body", l), i, False)
                    act.wait_ge(sg_ready, hid_base[l] + 4 + i * 2)
                    act.nop().then_inc(bank_free[0], 1)
                    act.nop().then_inc(bank_free[2], 1)
                    full(act, (("body", l), "down", 2 * NT - 1), i, 1)
                    split(nn + 1, i, RING)
                    split(nn + 2, i, RING)
                    full(act, (("body", l), "down", 2 * NT - 1), i)
                    high(i, 1)
                n = nn + RING * (nb - 1)
                assert n == unit_no["down", l, nb - 1] + 1
                if l + 1 < L:
                    ahead(n)
                for t in range(NT):
                    act.wait_ge(y_ready, NT * (2 * l + 1) + t + 1)
                    if t == 0:
                        multiplied(act, unit_no["down", l, nb - 1])
                    c = stat_col(l, "post_f", t)
                    nc.scalar.activation(junk[:, t, :], acc[:, t, :], ACT.Square, accum_out=ssq[:, c:c + 1]).then_inc(ssq_ready, 1)
                if l + 1 < L:
                    squares(l + 1, "pre_a", x)

        @block.vector
        def _(dve):
            v = nc.vector
            chain = [0]

            def link(ins):
                chain[0] += 1
                ins.then_inc(dve_step, 1)
                dve.wait_ge(dve_step, chain[0])

            def ada(l, u):
                full(dve, ("ada_row", l, u))
                v.tensor_copy(arow[:, :], ps[0:4, 7 * BANK:7 * BANK + COLS]).then_inc(arow_ready, 1)
                dve.wait_ge(arow_ready, 24 * l + u + 1)
                dve.nop().then_inc(bank_free[7], 1)
                full(dve, ("ada_col", l, u))
                v.tensor_tensor(modc[:, l, 2 * u:2 * u + 2, :], bank(7, 0, 4).rearrange("p (j a) -> p j a", j=2),
                                vcol[:, l, V_BADA + 2 * u:V_BADA + 2 * u + 2].unsqueeze(2).broadcast_to([128, 2, 2]),
                                ALU.add).then_inc(mod_ready, 1)
                dve.wait_ge(mod_ready, 24 * l + u + 1)
                dve.nop().then_inc(bank_free[7], 1)

            def norm(l, kind):
                m = 2 * l + (kind == "pre_f")
                sc, sh = (SC_A, SH_A) if kind == "pre_a" else (SC_F, SH_F)
                vg = V_GAPRE if kind == "pre_a" else V_GFPRE
                link(v.tensor_scalar(mulc[:, m, :, :], modc[:, l, sc * KC:(sc + 1) * KC, :], 1.0, None, ALU.add))
                link(v.tensor_tensor(mulc[:, m, :, :], mulc[:, m, :, :],
                                     vcol[:, l, vg:vg + KC].unsqueeze(2).broadcast_to([128, KC, 2]), ALU.mult))
                if m == 0:
                    dve.wait_ge(x_landed, 16)
                for t in range(NT):
                    dve.wait_ge(rstd_ready, stat_no(l, kind, t))
                    c = stat_col(l, kind, t)
                    v.tensor_scalar(z[:, t, :], x[:, t, :], rstd[:, c:c + 1], None, ALU.mult).then_inc(z_ready, 1)

                def low(c):
                    dve.wait_ge(nrm_h_ready, KC * m + c + 1)
                    v.tensor_tensor(hn_l[:, c, :], nrm_v[:, c % 2, :], hn_h[:, c, :].bitcast(F32), ALU.subtract).then_inc(hn_ready, 1)

                for c in range(KC):
                    b = 2 * (c % 4)
                    full(dve, ("turn", m, c))
                    if c >= 2:
                        dve.wait_ge(hn_ready, KC * m + c - 1)
                    link(v.tensor_scalar(nrm_v[:, c % 2, 0:T_LAT], bank(b, 0, T_LAT), mulc[:, m, c, 0:1],
                                         modc[:, l, sh * KC + c, 0:1], ALU.mult, ALU.add))
                    v.tensor_scalar(nrm_v[:, c % 2, T_LAT:T], bank(b, T_LAT, T), mulc[:, m, c, 1:2],
                                    modc[:, l, sh * KC + c, 1:2], ALU.mult, ALU.add).then_inc(nrm_v_ready, 1)
                    dve.wait_ge(nrm_v_ready, KC * m + c + 1)
                    dve.nop().then_inc(bank_free[b], 1)
                    if c:
                        low(c - 1)
                low(KC - 1)

            def attention(l):
                nu = 8 if l == 0 else 8
                todo = [(0, u) for u in range(8, 24)] + [(1, u) for u in range(8)] if l == 0 else [(1, u) for u in range(8, 24)]

                def drain_o(s):
                    h, t = divmod(s, NT)
                    full(dve, ("o", l, s))
                    v.tensor_copy(o_all[:, t, h * V:(h + 1) * V], bank(6, 0, V)).then_inc(o_ready, 1)
                    dve.wait_ge(o_ready, 21 * l + s + 1)
                    dve.nop().then_inc(bank_free[6], 1)

                for s in range(H * NT):
                    t = s % NT
                    w = T if t < 4 else T_CTX
                    full(dve, ("score", l, s))
                    if t < 4:
                        src = ps[:, 0:4 * BANK].rearrange("p (m a n) -> p m a n", m=2, a=2)[:, :, :, 0:HALF]
                        link(v.tensor_reduce(smx[:, :], src, AX.XY, ALU.max))
                    else:
                        src = ps[:, 0:4 * BANK].rearrange("p (m n) -> p m n", m=2)[:, :, 0:T_CTX]
                        link(v.tensor_reduce(smx[:, :], src, AX.X, ALU.max))
                    v.tensor_scalar(nmx[:, :], smx[:, :], -SCALE, None, ALU.mult).then_inc(nmax_ready, 1)
                    if s:
                        drain_o_prev = s - 2
                        if drain_o_prev >= 0:
                            drain_o(drain_o_prev)
                    dve.wait_ge(exp_ready, 40 * l + 2 * s + 2)
                    link(v.reciprocal(rsum[:, :], ssum[:, :]))
                    link(v.tensor_scalar(rneg[:, :], rsum[:, 1:2], nlam[:, l:l + 1], None, ALU.mult))
                    p0, p1 = probs[:, s % 2, 0, 0:w], probs[:, s % 2, 1, 0:w]
                    link(v.tensor_scalar(p0, p0, rsum[:, 0:1], None, ALU.mult))
                    v.scalar_tensor_tensor(out=p0, in0=p1, scalar=rneg[:, 0:1], in1=p0, op0=ALU.mult, op1=ALU.add).then_inc(a_ready, 1)
                    for _ in range(ADA_STEPS[l][t]):
                        ada(*todo.pop(0))
                assert not todo
                drain_o(H * NT - 2)
                drain_o(H * NT - 1)

            def fourier(l):
                for i in range(2):
                    if i == 0 and l == 1:
                        dve.wait_ge(params_landed, 96)
                    full(dve, ("m12", l, i))
                    v.tensor_scalar(m12[:, :, i, :], bank(i, 0, 512).rearrange("p (g e) -> p g e", g=G),
                                    1.0 if i == 0 else -1.0, None, ALU.mult).then_inc(m12_ready, 1)
                    dve.wait_ge(m12_ready, 2 * l + i + 1)
                    dve.nop().then_inc(bank_free[i], 1)
                link(v.tensor_tensor(o_sq[:, :, :], o_all[:, :, :], o_all[:, :, :], ALU.mult))
                c = stat_col(l, "sub")
                v.tensor_reduce(ssq[:, c:c + 20], o_sq[:, :, :].rearrange("p t (h e) -> p (t h) e", h=H), AX.X, ALU.add).then_inc(ssq_ready, 1)
                dve.wait_ge(ssq_ready, stat_no(l, "sub"))
                for t in range(NT):
                    for g2 in range(2):
                        r = 2 * t + g2
                        dve.wait_ge(zh_ready, 10 * l + r + 1)
                        v.tensor_tensor(z_l[:, t, 2 * g2:2 * g2 + 2, :], bank(2 + r % 6, 0, 512).rearrange("p (g e) -> p g e", g=2),
                                        z_h[:, t, 2 * g2:2 * g2 + 2, :].bitcast(F32), ALU.subtract).then_inc(zl_ready, 1)
                        dve.wait_ge(zl_ready, 10 * l + r + 1)
                        dve.nop().then_inc(bank_free[2 + r % 6], 1)
                dve.wait_ge(rstd_ready, stat_no(l, "sub"))
                o3 = o_all[:, :, :].rearrange("p t (h e) -> p (t h) e", h=H)
                v.tensor_tensor(o3, o3, rstd[:, c:c + 20].unsqueeze(2).broadcast_to([128, 20, V]), ALU.mult).then_inc(o_ready, 1)

                def low(h):
                    dve.wait_ge(sub_h_ready, H * l + h + 1)
                    v.tensor_tensor(mx_l[:, h, :], sub_v[:, h % 2, :], mx_h[:, h, :].bitcast(F32), ALU.subtract).then_inc(mxa_ready, 1)

                for h in range(H):
                    full(dve, ("sub", l, h))
                    if h >= 2:
                        dve.wait_ge(mxa_ready, H * l + h - 1)
                    v.tensor_scalar(sub_v[:, h % 2, :], bank(2 * h, 0, T), gsub[:, l:l + 1], None, ALU.mult).then_inc(sub_v_ready, 1)
                    dve.wait_ge(sub_v_ready, H * l + h + 1)
                    dve.nop().then_inc(bank_free[2 * h], 1)
                    if h:
                        low(h - 1)
                low(H - 1)
                dve.wait_ge(mxa_ready, H * (l + 1))
                for g in range(G):
                    dve.wait_ge(mf_h_ready, 5 * l + g + 1)
                    v.tensor_tensor(mx_l[:, 4 + g, 0:T_LAT], bank(g, 0, T_LAT), mx_h[:, 4 + g, 0:T_LAT].bitcast(F32), ALU.subtract).then_inc(mf_ready, 1)
                    dve.wait_ge(mf_ready, 2 * G * l + g + 1)
                    dve.nop().then_inc(bank_free[g], 1)
                dve.wait_ge(mf_h_ready, 5 * l + 5)
                v.tensor_tensor(mx_l[:, 4:8, T_LAT:T], bank(4, 0, 512).rearrange("p (g n) -> p g n", g=4),
                                mx_h[:, 4:8, T_LAT:T].bitcast(F32), ALU.subtract).then_inc(mf_ready, 4)
                dve.wait_ge(mf_ready, 2 * G * (l + 1))
                dve.nop().then_inc(bank_free[4], 1)

            def gate_rows(g):
                l, f = divmod(g, 2)
                vec, gain = ((GT_A, V_GAPOST), (GT_F, V_GFPOST))[f]
                link(v.tensor_tensor(gcol[:, :, :], modc[:, l, vec * KC:(vec + 1) * KC, :],
                                     vcol[:, l, gain:gain + KC].unsqueeze(2).broadcast_to([128, KC, 2]), ALU.mult))
                for cond in range(2):
                    for c in range(KC):
                        ins = v.tensor_scalar(diag[:, c, :], ident, gcol[:, c, cond:cond + 1], None, ALU.mult)
                    ins.then_inc(diag_ready, 1)
                    for hf in range(2):
                        full(dve, ("gate_bc", g, cond, hf))
                        v.tensor_copy(gate_bc[:, cond, hf * 512:(hf + 1) * 512], bank(6 + hf, 0, 512)).then_inc(gate_ready, 1)
                        dve.wait_ge(gate_ready, 4 * g + 2 * cond + hf + 1)
                        dve.nop().then_inc(bank_free[6 + hf], 1)

            def residual(l, kind):
                r = 2 * l + (kind == "post_f")
                for t in range(NT):
                    dve.wait_ge(rstd_ready, stat_no(l, kind, t))
                    c = stat_col(l, kind, t)
                    link(v.scalar_tensor_tensor(out=acc[:, t, :], in0=acc[:, t, :], scalar=rstd[:, c:c + 1],
                                                in1=gate_bc[:, 0 if t < 4 else 1, :], op0=ALU.mult, op1=ALU.mult))
                    v.tensor_tensor(x[:, t, :], x[:, t, :], acc[:, t, :], ALU.add).then_inc(x_ready, 1)
                    dve.wait_ge(x_ready, NT * r + t + 1)

            def products(l, key, i, k):
                for j in range(2):
                    full(dve, (key, "up", j), i)
                    view = sg[:, j, :].rearrange("p (a n) -> p a n", a=2)
                    v.tensor_tensor(view, view, pair(2 * j), ALU.mult).then_inc(hv_ready, 1)
                base = hid_base[l]
                dve.wait_ge(hv_ready, base + 2 + (i * 2 + 2 if k else 0))
                dve.nop().then_inc(bank_free[0], 1)
                dve.nop().then_inc(bank_free[2], 1)

            def low_hidden(l, i, k):
                base = hid_base[l]
                for j in range(2):
                    dve.wait_ge(hid_h_ready, base + j + 1 + (i * 2 + 2 if k else 0))
                    v.tensor_tensor(hid_l[:, j, :], sg[:, j, :], hid_h[:, j, :].bitcast(F32), ALU.subtract).then_inc(hid_ready, 1)

            def add_down(l, key, i, k):
                for r in range(2 * NT):
                    t, hf = divmod(r, 2)
                    full(dve, (key, "down", r), i)
                    a = acc[:, t, hf * 512:(hf + 1) * 512]
                    src = bank(4 + r % 4, 0, 512)
                    if l == 0:
                        ins = v.tensor_tensor(a, a, src, ALU.add)
                    else:
                        blk = i if k else N_BLK[1] - 1
                        g = gates_b[:, t, :, :].rearrange("p e q -> p (e q)")
                        g = g[:, bass.ds(blk, 1)] if k else g[:, blk:blk + 1]
                        ins = v.scalar_tensor_tensor(out=a, in0=src, scalar=g, in1=a, op0=ALU.mult, op1=ALU.add)
                    ins.then_inc(bank_free[4 + r % 4], 1)

            params = 80
            dve.wait_ge(params_landed, params)
            lt = lamt[:, :, :].rearrange("p l (a b) -> p l a b", a=2)
            v.tensor_tensor(lam2[:, :, :], lt[:, :, :, 0], lt[:, :, :, 1], ALU.mult).then_inc(lam_v, 1)
            dve.wait_ge(cond_act, 2)
            v.tensor_tensor(cond_p[:, :, 2:4], cond_s[:, :, :], cond_p[:, :, 0:2].bitcast(F32), ALU.subtract).then_inc(cond_ready, 1)
            dve.wait_ge(act_const, 2)
            v.tensor_tensor(dft_l[:, :], consts[:, 256:512], dft_h[:, :].bitcast(F32), ALU.subtract).then_inc(dft_ready, 1)
            v.tensor_tensor(rt_l[:, :, :], w_rt[:, :, :], rt_h[:, :, :].bitcast(F32), ALU.subtract).then_inc(dft_ready, 1)
            dve.wait_ge(bank_free[0], 1)
            link(v.tensor_tensor(nlam[:, :], lame[:, :, 1], lame[:, :, 0], ALU.subtract))
            for l in range(L):
                lam_init = 0.8 - 0.6 * math.exp(-0.3 * l)
                link(v.tensor_scalar(nlam[:, l:l + 1], nlam[:, l:l + 1], -lam_init, None, ALU.add))
                link(v.tensor_scalar(gsub[:, l:l + 1], vcol[:, l, V_SUB:V_SUB + 1], 1.0 - lam_init, None, ALU.mult))
            for u in range(8):
                ada(0, u)
            for l in range(L):
                norm(l, "pre_a")
                for c in range(4, 8):
                    b = 2 * (c % 4)
                    full(dve, ("in", l, c))
                    v.tensor_copy(kT[:, c - 4, 0:HALF], bank(b, 0, HALF)).then_inc(dve_step, 1)
                    v.tensor_copy(kT[:, c - 4, HALF:T_LAT], bank(b + 1, 0, T_LAT - HALF)).then_inc(dve_step, 1)
                    chain[0] += 2
                    dve.wait_ge(dve_step, chain[0])
                    v.tensor_copy(kT[:, c - 4, T:T + T_CTX], bank(b + 1, T_LAT - HALF, HALF)).then_inc(k_out, 1)
                    dve.wait_ge(k_out, H * l + c - 3)
                    dve.nop().then_inc(bank_free[b], 1)
                for c in range(2 * H):
                    full(dve, ("rot", l, c))
                    a = (qT if c % 2 == 0 else kT)[:, c // 2, 0:T_LAT]
                    link(v.tensor_tensor(rope_t[:, :], bank(c, 0, T_LAT), sin_r, ALU.mult))
                    dve.nop().then_inc(bank_free[c], 1)
                    link(v.tensor_tensor(a, a, cos_r, ALU.mult))
                    v.tensor_tensor(a, a, rope_t[:, :], ALU.add).then_inc(rope_ready, 1)
                    dve.wait_ge(rope_ready, 2 * H * l + c + 1)
                for u in range(2):
                    for t in range(NT):
                        full(dve, ("val", l, u, t))
                        v.tensor_copy(vt[:, t, u * 256:(u + 1) * 256], bank((5 * u + t) % 8, 0, 256)).then_inc(v_out, 1)
                        dve.wait_ge(v_out, 2 * NT * l + 5 * u + t + 1)
                        dve.nop().then_inc(bank_free[(5 * u + t) % 8], 1)
                attention(l)
                fourier(l)
                gate_rows(2 * l)
                for hf in range(2):
                    for t in range(NT):
                        full(dve, ("mix", l, hf, t))
                        b = (5 * hf + t) % 8
                        v.tensor_copy(acc[:, t, hf * 512:(hf + 1) * 512], bank(b, 0, 512)).then_inc(y_ready if hf else dve_step, 1)
                        if hf == 0:
                            chain[0] += 1
                            dve.wait_ge(dve_step, chain[0])
                        else:
                            dve.wait_ge(y_ready, NT * 2 * l + t + 1)
                        dve.nop().then_inc(bank_free[b], 1)
                residual(l, "post_a")
                norm(l, "pre_f")
                link(v.memset(acc[:, :, :], 0.0))
                gate_rows(2 * l + 1)
                if l == 1:
                    full(dve, ("router",))
                    link(v.tensor_copy(logit[:, :, :].rearrange("p t e -> p (t e)"), bank(0, 0, NT * E)))
                    dve.nop().then_inc(bank_free[0], 1)
                    for t in range(NT):
                        link(v.max(top8[:, t, :], logit[:, t, :]))
                        link(v.max_index(idx8[:, t, :], top8[:, t, :], logit[:, t, :]))
                    link(v.tensor_copy(idxf[:, :, :], idx8[:, :, 0:2]))
                    v.tensor_tensor(gdif[:, :], top8[:, :, 1], top8[:, :, 0], ALU.subtract).then_inc(gexp_ready, 1)
                    dve.wait_ge(gexp_ready, 2)
                    link(v.tensor_scalar(gden[:, :], gexp[:, :], 1.0, None, ALU.add))
                    link(v.reciprocal(g12[:, :, 0], gden[:, :]))
                    link(v.tensor_tensor(g12[:, :, 1], g12[:, :, 0], gexp[:, :], ALU.mult))
                    for t in range(NT):
                        link(v.tensor_scalar(gates[:, t, :], iota8, idxf[:, t, 0:1], g12[:, t, 0:1], ALU.is_equal, ALU.mult))
                        link(v.tensor_scalar(gsel[:, t, :], iota8, idxf[:, t, 1:2], g12[:, t, 1:2], ALU.is_equal, ALU.mult))
                    link(v.tensor_tensor(gates[:, :, :], gates[:, :, :], gsel[:, :, :], ALU.add))
                    link(v.tensor_copy(gates_b[:, :, :, :].rearrange("p t e q -> p (t e) q"),
                                       gates[:, :, :].rearrange("p t e -> p (t e)").unsqueeze(2).broadcast_to([128, NT * E, N_BLK[1] // E])))
                nb = N_BLK[l]
                dve.wait_ge(sg_ready, hid_base[l] + 2)
                products(l, ("first", l), 0, 0)
                low_hidden(l, 0, 0)
                with dve.Fori(0, nb - 1) as i:
                    dve.wait_ge(sg_ready, hid_base[l] + 4 + i * 2)
                    products(l, ("body", l), i, 1)
                    add_down(l, ("body", l), i, 1)
                    low_hidden(l, i, 1)
                add_down(l, ("last", l), 0, 0)
                b0 = fills.named[(("last", l), "down", 0)]
                for t in range(NT):
                    r = 2 * t + 1
                    dve.wait_ge(bank_free[4 + r % 4], fills.named[(("last", l), "down", r)][1])
                    dve.wait_ge(bank_free[4 + (r - 1) % 4], fills.named[(("last", l), "down", r - 1)][1])
                    dve.nop().then_inc(y_ready, 1)
                residual(l, "post_f")


def dft(n):
    j = np.outer(np.arange(n), np.arange(n)) % n
    return (np.cos(2 * np.pi * j / n) / math.sqrt(n)).astype(np.float32), (np.sin(2 * np.pi * j / n) / math.sqrt(n)).astype(np.float32)


def shape_constants():
    c, s = dft(128)
    rot = np.zeros((128, 128), np.float32)
    for d in range(128):
        b, r = divmod(d, 16)
        if b % 2 == 0:
            rot[d + 16, d] = -1.0
        else:
            rot[d - 16, d] = 1.0
    grid_w, half = 64, QK // 2
    inv = (1.0 / (np.float32(10000.0) ** (np.arange(0, half, 2, dtype=np.float32) / np.float32(half)))).astype(np.float32)
    pos = np.arange(T_LAT)
    tabs = []
    for p in (pos // grid_w, pos % grid_w):
        a = p.astype(np.float32)[:, None] * inv[None, :]
        tabs += [a, a]
    ang = np.concatenate(tabs, axis=1)
    ang = np.concatenate([ang, ang], axis=1).T
    iota = np.tile(np.arange(8, dtype=np.float32), (128, 1))
    sel = np.zeros((128, 2), np.float32)
    for r in range(4):
        sel[r, r % 2] = 1.0
    consts = np.concatenate([np.eye(128, dtype=np.float32), rot, c, s, np.cos(ang), np.sin(ang), iota, sel], axis=1)
    c5, s5 = dft(T_LAT)
    lay = lambda a: a.reshape(4, 128, T_LAT).transpose(1, 0, 2).reshape(128, UNIT)
    return np.ascontiguousarray(consts.astype(np.float32)), lay(c5), lay(s5)


def kernel(x_prompt, x_sample, cache_k, cache_v, c, c_ctx, g_attn_pre, g_attn_post, g_ffn_pre, g_ffn_post,
           w_ada, b_ada, w_in, lam_params, g_subln, w_fnet, w_out, w_gate, w_up, w_down, w_router,
           e_gate, e_up, e_down):
    import concourse.bacc as bacc
    from concourse.bass_utils import run_bass_kernel_spmd

    A = np.asarray
    consts, cos5, sin5 = shape_constants()

    def wide(w, u):
        return A(w)[:, u * COLS:(u + 1) * COLS].reshape(KC, 128, COLS).transpose(1, 0, 2).reshape(128, UNIT)

    def rows(w, r, n):
        w = A(w)[r:r + n]
        return w.reshape(n // 128, 128, w.shape[1]).transpose(1, 0, 2).reshape(128, UNIT)

    in_cols = [0, 1, 2, 3, 6, 7, 4, 5]
    units = plan_units()
    stream = np.empty((len(units), 128, UNIT), np.float32)
    for n, (kind, l, u) in enumerate(units):
        e, q = divmod(u, F_EXP // COLS)
        if kind == "ada":
            stream[n] = wide(w_ada[l], u)
        elif kind == "in":
            stream[n] = wide(w_in[l], in_cols[u])
        elif kind == "cos":
            stream[n] = cos5
        elif kind == "sin":
            stream[n] = sin5
        elif kind == "out":
            stream[n] = rows(A(w_out[l])[:, (u // 2) * 512:(u // 2 + 1) * 512], (u % 2) * 512, 512)
        elif kind == "gate":
            stream[n] = wide(w_gate[0], u) if l == 0 else wide(e_gate[0][e], q)
        elif kind == "up":
            stream[n] = wide(w_up[0], u) if l == 0 else wide(e_up[0][e], q)
        else:
            stream[n] = rows(w_down[0], u * COLS, COLS) if l == 0 else rows(e_down[0][e], q * COLS, COLS)
    vrows = np.zeros((L, 128, 128), np.float32)
    for l in range(L):
        parts = [b_ada[l], g_attn_pre[l], g_attn_post[l], g_ffn_pre[l], g_ffn_post[l], c[0], c_ctx, g_subln[l]]
        flat = np.concatenate([A(p).reshape(-1, 128) for p in parts], axis=0)
        vrows[l, :flat.shape[0]] = flat
    x_all = np.concatenate([A(x_sample)[0], A(x_prompt)[0]], axis=0)
    arrays = {
        "stream": stream,
        "consts": consts,
        "vcol": vrows.transpose(2, 0, 1),
        "x": x_all.reshape(NT, 128, D).transpose(1, 0, 2),
        "lam": A(lam_params).transpose(2, 0, 1),
        "w_router": A(w_router)[0].reshape(KC, 128, E).transpose(1, 0, 2),
        "w_fnet": A(w_fnet).transpose(0, 2, 1, 3).reshape(L, 128, G * 128),
        "cache_k": A(cache_k)[0].reshape(L, PAST, H, 2 * QK).transpose(0, 3, 2, 1),
        "cache_v": A(cache_v)[0].reshape(L, PAST, H * V),
    }
    arrays = {k: np.ascontiguousarray(a) for k, a in arrays.items()}
    nc = bacc.Bacc("TRN2", target_bir_lowering=False, num_devices=1)
    dram = {k: nc.dram_tensor(k, a.shape, F32, kind="ExternalInput").ap() for k, a in arrays.items()}
    shapes = {"y": (128, NT, D), "new_k": (L, 128, H, T_CTX), "new_v": (L, 128, H * V)}
    out = {k: nc.dram_tensor(k, s, F32, kind="ExternalOutput").ap() for k, s in shapes.items()}
    build(nc, dram, out)
    r = run_bass_kernel_spmd(nc, [arrays], core_ids=[0]).results[0]
    y = A(r["y"]).transpose(1, 0, 2).reshape(T, D)
    new_k = A(r["new_k"]).transpose(0, 3, 2, 1).reshape(1, L, T_CTX, H, 2, QK)
    new_v = A(r["new_v"]).reshape(1, L, T_CTX, H, V)
    return (np.ascontiguousarray(y[T_LAT:])[None], np.ascontiguousarray(y[:T_LAT])[None],
            np.ascontiguousarray(new_k), np.ascontiguousarray(new_v))
```

```python
import math
from contextlib import ExitStack

import numpy as np
import concourse.bass as bass
from concourse import mybir
from concourse.alu_op_type import AluOpType as ALU

F32 = mybir.dt.float32
F32R = mybir.dt.float32r
U32 = mybir.dt.uint32
I32 = mybir.dt.int32
ACT = mybir.ActivationFunctionType
AX = mybir.AxisListType

D = 1024
KC = D // 128
L = 2
T_LAT, T_CTX, PAST = 512, 128, 128
T = T_LAT + T_CTX
NT = T // 128
H, QK, V = 4, 64, 128
G = 4
F_DENSE, F_EXP, E = 2816, 1024, 8
UNIT = 2048
RING = 3
COLS = UNIT // KC
N_BLK = F_DENSE // COLS
EXP_BLK = F_EXP // COLS
SLOTS = 256
ROUNDS = -(-T // SLOTS)
EXP_UNITS = [("gate", 0), ("up", 0), ("gate", 1), ("up", 1), ("down", 0), ("gate", 2), ("up", 2), ("down", 1),
             ("gate", 3), ("up", 3), ("down", 2), ("down", 3)]
N_EU = len(EXP_UNITS)
EPS = 1e-6
FAR = 1048576.0
SCALE = QK ** -0.5
HALF = T // 2
BANK = 512
ADA_STEPS = ((1, 1, 1, 1, 2), (1, 1, 1, 1, 0))
SH_A, SC_A, GT_A, SH_F, SC_F, GT_F = range(6)
V_BADA, V_GAPRE, V_GAPOST, V_GFPRE, V_GFPOST, V_C, V_CTX, V_SUB = 0, 48, 56, 64, 72, 80, 88, 96


def plan_units():
    units = [("ada", 0, u) for u in range(8)]
    ada = [[("ada", 0, u) for u in range(8, 24)] + [("ada", 1, u) for u in range(8)],
           [("ada", 1, u) for u in range(8, 24)]]
    for l in range(L):
        units += [("in", l, u) for u in range(8)]
        units += ada[l]
        units += [("cos", l, 0), ("sin", l, 0)]
        units += [("out", l, u) for u in range(4)]
        if l == 0:
            units += [("gate", l, 0), ("up", l, 0)]
            for b in range(1, N_BLK):
                units += [("gate", l, b), ("up", l, b), ("down", l, b - 1)]
            units += [("down", l, N_BLK - 1)]
        else:
            units += [(kind, l, e * EXP_BLK + q) for e in range(E) for kind, q in EXP_UNITS]
    return units


def stat_no(l, kind, t=0):
    if kind == "pre_a" and l == 0:
        return t + 1
    if kind == "sub":
        return l * 21 + 6
    base = {"post_a": 6 + 21 * l, "pre_f": 6 + 21 * l, "post_f": 16 + 21 * l, "pre_a": 16}[kind]
    if kind == "post_f" and l == L - 1:
        return base + t + 1
    if kind[:4] == "post":
        return base + max(2 * t - 1, 0) + 1
    return base + min(2 * t + 2, 2 * NT - 1) + 1


def stat_col(l, kind, t=0):
    return l * 40 + {"pre_a": 0, "sub": 20, "post_a": 5, "pre_f": 10, "post_f": 15}[kind] + t


class Fills:

    def __init__(self):
        self.total = [0] * 8
        self.named = {}
        self.i, self.per = None, None

    def enter(self, i, per):
        self.i, self.per, self.at = i, per, list(self.total)

    def leave(self, n):
        for b, k in self.per.items():
            assert self.total[b] - self.at[b] == k, (b, k, self.total[b] - self.at[b])
        assert all(self.total[b] == self.at[b] for b in range(8) if b not in self.per)
        for b, k in self.per.items():
            self.total[b] = self.at[b] + n * k
        self.i = None

    def next(self, key, b):
        before, k = self.total[b], self.per.get(b, 0) if self.i is not None else 0
        self.total[b] += 1
        self.named[key] = (b, before + 1, k)
        return before if not k else before + self.i * k


def build(nc, dram, out):
    units = plan_units()
    unit_no = {u: n for n, u in enumerate(units)}
    N_STATIC = unit_no["gate", 1, 0]

    with ExitStack() as ctx:
        def sem(name):
            return ctx.enter_context(nc.semaphore(name))

        top = [(nc.sbuf_base + 31) // 32 * 32]

        def at(name, shape, dt, offset):
            return nc.alloc_sbuf_tensor_at(name, shape, dt, offset=offset)

        def sb(name, shape, dt=F32):
            off = top[0]
            top[0] += (int(np.prod(shape[1:])) * 4 + 31) // 32 * 32
            return at(name, shape, dt, off)

        x_off = top[0]
        x = sb("x", [128, NT, D])
        ehid_h = at("ehid_h", [128, 2, SLOTS], F32R, x_off)
        ehid_l = at("ehid_l", [128, 2, SLOTS], F32R, x_off + 2048)
        esg = at("esg", [128, 2, SLOTS], F32, x_off + 4096)
        y_h = at("y_h", [128, 2, D], F32R, x_off + 6144)
        act_off = top[0]
        hn_h = sb("hn_h", [128, KC, T], F32R)
        hn_l = sb("hn_l", [128, KC, T], F32R)
        half_kc = KC // 2 * T * 4
        mx_h = at("mx_h", [128, KC, T], F32R, act_off)
        mx_l = at("mx_l", [128, KC, T], F32R, act_off + 2 * half_kc)
        junk = at("junk", [128, NT, D], F32, act_off)
        o_all = at("o_all", [128, NT, H * V], F32, act_off + half_kc)
        probs = at("probs", [128, 2, 2, T], F32, act_off + 3 * half_kc)
        o_sq = at("o_sq", [128, NT, H * V], F32, act_off + 3 * half_kc)
        eacc = at("eacc", [128, NT, D], F32, act_off)
        xg = at("xg", [128, KC, 2, SLOTS], F32R, act_off + 20480)
        y_l = [at("y_l0", [128, D], F32R, act_off + 36864), at("y_l1", [128, D], F32R, x_off + 14336)]
        raw = [sb(f"raw{s}", [128, UNIT]) for s in range(RING)]
        wh = [sb(f"wh{s}", [128, UNIT], F32R) for s in range(RING)]
        wl = [sb(f"wl{s}", [128, UNIT], F32R) for s in range(RING)]
        m_off = top[0]
        top[0] += 51200
        fT = at("fT", [128, G, T], F32, m_off)
        qT = at("qT", [128, H, T], F32, m_off + 10240)
        kT = at("kT", [128, H, T + PAST], F32, m_off + 20480)
        vt = at("vt", [128, NT + 1, H * V], F32, m_off + 32768)
        rope_t = at("rope_t", [128, T_LAT], F32, m_off + 45056)
        aT = at("aT", [128, 2, T], F32, m_off + 45056)
        z_h = at("z_h", [128, NT, G, 256], F32R, m_off + 10240)
        z_l = at("z_l", [128, NT, G, 256], F32R, m_off + 30720)
        sub_v = at("sub_v", [128, 2, T], F32, act_off + 3 * half_kc)
        nrm_v = at("nrm_v", [128, 2, T], F32, m_off)
        sg = at("sg", [128, 2, T], F32, m_off)
        hid_h = at("hid_h", [128, 2, T], F32R, m_off + 5120)
        hid_l = at("hid_l", [128, 2, T], F32R, m_off + 10240)
        acc = at("acc", [128, NT, D], F32, m_off + 25600)
        z = at("z", [128, NT, D], F32, m_off + 25600)
        ht_h = at("ht_h", [128, NT, D], F32R, m_off)
        ht_l = at("ht_l", [128, NT, D], F32R, m_off + 20480)
        junk2 = at("junk2", [128, NT, D], F32, m_off)
        pick = at("pick", [128, NT, SLOTS], F32R, m_off + 40960)
        pickT = at("pickT", [128, 2, T], F32R, m_off + 46080)
        gate_off = top[0]
        gate_bc = sb("gate_bc", [128, 2, D])
        w_fn = at("w_fn", [128, G * 128], F32, gate_off)
        m12 = at("m12", [128, G, 2, 128], F32, gate_off + 2048)
        NCONST = 4 * 128 + 2 * T_LAT + 8 + SLOTS + 128 + 2
        const_off = top[0]
        consts = sb("consts", [128, NCONST])
        ident, rot, c128, s128 = (consts[:, 128 * i:128 * (i + 1)] for i in range(4))
        cos_r, sin_r = consts[:, 512:512 + T_LAT], consts[:, 512 + T_LAT:512 + 2 * T_LAT]
        iota8 = consts[:, 512 + 2 * T_LAT:512 + 2 * T_LAT + 8]
        iota_s = consts[:, 520 + 2 * T_LAT:520 + 2 * T_LAT + SLOTS]
        tri = consts[:, 520 + 2 * T_LAT + SLOTS:520 + 2 * T_LAT + SLOTS + 128]
        sel4 = consts[0:4, NCONST - 2:NCONST]
        dft_h = sb("dft_h", [128, 2 * 128], F32R)
        dft_l = sb("dft_l", [128, 2 * 128], F32R)
        ones = sb("ones", [128, 128])
        vcol = sb("vcol", [128, L, 128])
        modc = sb("modc", [128, L, 48, 2])
        mulc = sb("mulc", [128, 2 * L, KC, 2])
        arow = sb("arow", [4, COLS])
        cond_s = sb("cond_s", [128, KC, 2])
        cond_p = sb("cond_p", [128, KC, 4], F32R)
        ssq = sb("ssq", [128, L * 40])
        msq = sb("msq", [128, L * 40])
        rstd = sb("rstd", [128, L * 40])
        mhalf = sb("mhalf", [128, 20])
        lamt = sb("lamt", [64, L, 4])
        lam2 = sb("lam2", [64, L, 2])
        lame = sb("lame", [128, L, 2])
        nlam = sb("nlam", [128, L])
        gsub = sb("gsub", [128, L])
        smx = sb("smx", [128, 2])
        nmx = sb("nmx", [128, 2])
        ssum = sb("ssum", [128, 2])
        rsum = sb("rsum", [128, 2])
        rneg = sb("rneg", [128, 1])
        gcol = sb("gcol", [128, KC, 2])
        w_rt = sb("w_rt", [128, KC, E])
        rt_h = sb("rt_h", [128, KC, E], F32R)
        rt_l = sb("rt_l", [128, KC, E], F32R)
        logit = sb("logit", [128, NT, E])
        top8 = sb("top8", [128, NT, 8])
        idx8 = sb("idx8", [128, NT, 8], U32)
        idxf = sb("idxf", [128, NT, 2])
        gdif = sb("gdif", [128, NT])
        gexp = sb("gexp", [128, NT])
        gden = sb("gden", [128, NT])
        g12 = sb("g12", [128, NT, 2])
        gsel = sb("gsel", [128, NT, E])
        gates = sb("gates", [128, NT, E])
        sel = sb("sel", [128, NT, E])
        csel = sb("csel", [128, NT, E])
        tsel = sb("tsel", [128, E])
        pos = sb("pos", [128, NT, E])
        slot_x = at("slot_x", [128, NT, ROUNDS * E + 1], F32, const_off + 2048)
        gate_x = at("gate_x", [128, NT, ROUNDS * E + 1], F32, const_off + 2048 + 1024)
        total = sb("total", [128, E])
        most = sb("most", [128, 3])
        trips_f = sb("trips_f", [128, 3])
        trips_i = sb("trips_i", [128, 3], I32)
        left_f = sb("left_f", [128, ROUNDS * E])
        left_i = sb("left_i", [128, ROUNDS * E], I32)
        slot_c = sb("slot_c", [128, NT])
        gate_c = sb("gate_c", [128, NT])
        gslot = sb("gslot", [128, 2])
        x_wait = nc.dram_tensor("x_wait", (128, NT, D), F32, kind="Internal").ap()
        assert top[0] <= nc.sbuf_usable_end, top[0]

        ps = ctx.enter_context(nc.psum_tensor("ps", [128, 8 * BANK], F32))

        def bank(b, lo, hi):
            return ps[:, b * BANK + lo:b * BANK + hi]

        def pair(b):
            return ps[:, b * BANK:(b + 2) * BANK].rearrange("p (a n) -> p a n", a=2)[:, :, 0:HALF]

        raw_landed = [sem(f"raw_landed{s}") for s in range(RING)]
        wh_ready, wl_ready = sem("wh_ready"), sem("wl_ready")
        sums_used = sem("sums_used")
        bank_full = [sem(f"bank_full{b}") for b in range(8)]
        bank_free = [sem(f"bank_free{b}") for b in range(8)]
        params_landed, x_landed = sem("params_landed"), sem("x_landed")
        cache_landed, stored = sem("cache_landed"), sem("stored")
        pool_const, pool_step = sem("pool_const"), sem("pool_step")
        cond_act, cond_ready = sem("cond_act"), sem("cond_ready")
        act_const = sem("act_const")
        dft_ready = sem("dft_ready")
        arow_ready, mod_ready, mul_ready = sem("arow_ready"), sem("mod_ready"), sem("mul_ready")
        ssq_ready, rstd_ready = sem("ssq_ready"), sem("rstd_ready")
        z_ready = sem("z_ready")
        nrm_v_ready, nrm_h_ready, hn_ready = sem("nrm_v_ready"), sem("nrm_h_ready"), sem("hn_ready")
        q_out, k_out, f_out, v_out = sem("q_out"), sem("k_out"), sem("f_out"), sem("v_out")
        rope_ready = sem("rope_ready")
        nmax_ready, exp_ready, a_ready, aT_ready = sem("nmax_ready"), sem("exp_ready"), sem("a_ready"), sem("aT_ready")
        o_ready = sem("o_ready")
        sub_v_ready, sub_h_ready, mxa_ready = sem("sub_v_ready"), sem("sub_h_ready"), sem("mxa_ready")
        m12_ready = sem("m12_ready")
        zh_ready, zl_ready = sem("zh_ready"), sem("zl_ready")
        mf_h_ready, mf_ready = sem("mf_h_ready"), sem("mf_ready")
        y_ready, x_ready = sem("y_ready"), sem("x_ready")
        gcol_ready, gate_ready = sem("gcol_ready"), sem("gate_ready")
        lam_v, lam_e = sem("lam_v"), sem("lam_e")
        sg_ready, hv_ready, hid_h_ready, hid_ready = sem("sg_ready"), sem("hv_ready"), sem("hid_h_ready"), sem("hid_ready")
        acc_zero = sem("acc_zero")
        gexp_ready = sem("gexp_ready")
        ht_h_ready, ht_l_ready = sem("ht_h_ready"), sem("ht_l_ready")
        sel_ready, trips_ready, x_saved, x_back = sem("sel_ready"), sem("trips_ready"), sem("x_saved"), sem("x_back")
        pick_ready, pickT_ready, gslot_ready = sem("pick_ready"), sem("pickT_ready"), sem("gslot_ready")
        xg_act, xg_dve = sem("xg_act"), sem("xg_dve")
        esg_ready, ehv_ready, ehid_h_ready, ehid_ready = sem("esg_ready"), sem("ehv_ready"), sem("ehid_h_ready"), sem("ehid_ready")
        yh_ready, yl_ready = sem("yh_ready"), sem("yl_ready")
        dve_step = sem("dve_step")
        act_step = sem("act_step")
        slot_ready = sem("slot_ready")

        fills = Fills()
        block = ctx.enter_context(nc.Block())


        @block.tensor
        def _(pe):
            mm = nc.tensor.matmul

            def fill(key, b):
                before = fills.next(key, b)
                if not (isinstance(before, int) and before == 0):
                    pe.wait_ge(bank_free[b], before)

            def all_read():
                for b in range(8):
                    if fills.total[b]:
                        pe.wait_ge(bank_free[b], fills.total[b])

            def three(outs, w_of, x_of, sl, ks):
                for k in ks:
                    for hi, xs in ((wh, (hn_h, hn_l)), (wl, (hn_h,))):
                        for xp in xs:
                            for o, xc in zip(outs, x_of):
                                last = mm(o, w_of(hi[sl], k), xp[:, k, xc[0]:xc[1]],
                                          start=(k == 0 and hi is wh and xp is hn_h),
                                          stop=(k == KC - 1 and hi is wl))
                return last

            def ada(n):
                _, l, u = units[n]
                s = n % RING
                pe.wait_ge(wl_ready, n + 1)
                fill(("ada_row", l, u), 7)
                for k in range(KC):
                    for w in (wh, wl):
                        last = mm(ps[0:4, 7 * BANK:7 * BANK + COLS], cond_p[:, k, :], w[s][:, k * COLS:(k + 1) * COLS],
                                  start=(k == 0 and w is wh), stop=(k == KC - 1 and w is wl))
                last.then_inc(bank_full[7], 1)

            def ada_turn(n):
                _, l, u = units[n]
                pe.wait_ge(arow_ready, l * 24 + u + 1)
                fill(("ada_col", l, u), 7)
                for j in range(2):
                    last = mm(bank(7, 2 * j, 2 * j + 2), arow[:, j * 128:(j + 1) * 128], sel4,
                              start=True, stop=True)
                last.then_inc(bank_full[7], 1)

            def turn_norm(l, kind, product=None):
                all_read()
                m = 2 * l + (kind == "pre_f")
                pe.wait_ge(z_ready, NT * (m + 1))

                def turn(c):
                    b = 4 + 2 * (c % 2)
                    fill(("turn", m, c), b)
                    for t in range(NT):
                        last = nc.tensor.transpose(bank(b, t * 128, (t + 1) * 128), z[:, t, c * 128:(c + 1) * 128], ident)
                    last.then_inc(bank_full[b], 1)

                turn(0)
                turn(1)
                for c in range(KC):
                    if c + 2 < KC:
                        turn(c + 2)
                    pe.wait_ge(hn_ready, KC * m + c + 1)
                    if product:
                        product(c)
                pe.wait_ge(bank_free[4], fills.total[4])
                pe.wait_ge(bank_free[6], fills.total[6])

            def first_products(n, keys):
                def product(k):
                    if k == 0:
                        pe.wait_ge(wl_ready, n + 1)
                        fill(keys[0], 0)
                        fill(keys[1], 2)
                    for j, b in ((0, 0), (1, 2)):
                        last = three([bank(b, 0, HALF), bank(b + 1, 0, HALF)],
                                     lambda w, kk, j=j: w[:, kk * COLS + j * 128:kk * COLS + j * 128 + 128],
                                     [(0, HALF), (HALF, T)], n % RING, [k])
                        if k == KC - 1:
                            last.then_inc(bank_full[b], 1)
                return product

            def proj_in(l):
                for u in range(1, 6):
                    n = unit_no["in", l, u]
                    pe.wait_ge(wl_ready, n + 1)
                    for j in range(2):
                        c = 2 * u + j
                        b = 2 * (c % 4)
                        fill(("in", l, c), b)
                        three([bank(b, 0, HALF), bank(b + 1, 0, HALF)],
                              lambda w, k, j=j: w[:, k * COLS + j * 128:k * COLS + j * 128 + 128],
                              [(0, HALF), (HALF, T)], n % RING, range(KC)).then_inc(bank_full[b], 1)
                all_read()
                for c in range(2 * H):
                    pe.wait_ge(q_out if c % 2 == 0 else k_out, H * l + c // 2 + 1)
                    fill(("rot", l, c), c)
                    mm(bank(c, 0, T_LAT), rot, (qT if c % 2 == 0 else kT)[:, c // 2, 0:T_LAT],
                       start=True, stop=True).then_inc(bank_full[c], 1)
                for u in range(6, 8):
                    n = unit_no["in", l, u]
                    pe.wait_ge(wl_ready, n + 1)
                    for t in range(NT):
                        b = (5 * (u - 6) + t) % 8
                        fill(("val", l, u - 6, t), b)
                        for k in range(KC):
                            for i, (xp, w) in enumerate(((hn_h, wh), (hn_h, wl), (hn_l, wh))):
                                last = mm(bank(b, 0, COLS), xp[:, k, t * 128:(t + 1) * 128],
                                          w[n % RING][:, k * COLS:(k + 1) * COLS],
                                          start=(k == 0 and i == 0), stop=(k == KC - 1 and i == 2))
                        last.then_inc(bank_full[b], 1)
                all_read()

            def attention(l):
                n = unit_no["in", l, 7] + 1
                pe.wait_ge(v_out, 2 * NT * (l + 1))
                pe.wait_ge(cache_landed, 32 * (l + 1))
                steps = [(h, t) for h in range(H) for t in range(NT)]
                turn = None

                def values(s):
                    h, t = steps[s]
                    no = 20 * l + s
                    tiles = [0, 1, 2, 3, 5] if t < 4 else [4]
                    pe.wait_ge(a_ready, no + 1)
                    fill(("aT", l, s), 4)
                    for i in range(len(tiles)):
                        last = nc.tensor.transpose(bank(4, i * 128, (i + 1) * 128), probs[:, s % 2, 0, i * 128:(i + 1) * 128], ident)
                    last.then_inc(bank_full[4], 1)
                    pe.wait_ge(aT_ready, no + 1)
                    fill(("o", l, s), 6)
                    for i, kt in enumerate(tiles):
                        last = mm(bank(6, 0, V), aT[:, s % 2, i * 128:(i + 1) * 128], vt[:, kt, h * V:(h + 1) * V],
                                  start=(i == 0), stop=(i == len(tiles) - 1))
                    last.then_inc(bank_full[6], 1)

                for s, (h, t) in enumerate(steps):
                    pe.wait_ge(rope_ready, 2 * H * l + 2 * h + 2)
                    fill(("score", l, s), 0)
                    for m in range(2):
                        q = qT[64 * m:64 * m + 64, h, t * 128:(t + 1) * 128]
                        if t < 4:
                            for j in range(2):
                                last = mm(bank(2 * m + j, 0, HALF), q, kT[64 * m:64 * m + 64, h, j * HALF:(j + 1) * HALF],
                                          start=True, stop=True)
                        else:
                            last = mm(bank(2 * m, 0, T_CTX), q, kT[64 * m:64 * m + 64, h, T:T + T_CTX],
                                      start=True, stop=True)
                    last.then_inc(bank_full[0], 1)
                    if turn is not None:
                        ada_turn(turn)
                        turn = None
                    if s:
                        values(s - 1)
                    for a in range(ADA_STEPS[l][t]):
                        if a:
                            ada_turn(n - 1)
                        ada(n)
                        turn = n
                        n += 1
                if turn is not None:
                    ada_turn(turn)
                values(len(steps) - 1)
                assert n == unit_no["cos", l, 0], (l, n, unit_no["cos", l, 0])
                all_read()

            def fourier(l):
                for i, m in enumerate((c128, s128)):
                    fill(("m12", l, i), i)
                    mm(bank(i, 0, 512), m, w_fn[:, :], start=True, stop=True).then_inc(bank_full[i], 1)
                pe.wait_ge(m12_ready, 2 * (l + 1))
                for t in range(NT):
                    for g2 in range(2):
                        b = 2 + (2 * t + g2) % 6
                        fill(("z", l, t, g2), b)
                        for g in (2 * g2, 2 * g2 + 1):
                            last = mm(bank(b, 256 * (g % 2), 256 * (g % 2) + 256), fT[:, g, t * 128:(t + 1) * 128],
                                      m12[:, g, :, :].rearrange("p a e -> p (a e)"), start=True, stop=True)
                        last.then_inc(bank_full[b], 1)
                all_read()
                pe.wait_ge(o_ready, 20 * (l + 1) + l + 1)
                for h in range(H):
                    b = 2 * h
                    fill(("sub", l, h), b)
                    for t in range(NT):
                        last = nc.tensor.transpose(bank(b, t * 128, (t + 1) * 128), o_all[:, t, h * V:(h + 1) * V], ident)
                    last.then_inc(bank_full[b], 1)
                all_read()
                gate_rows(2 * l)
                pe.wait_ge(zl_ready, 2 * NT * (l + 1))
                for i, name in enumerate(("cos", "sin")):
                    n = unit_no[name, l, 0]
                    pe.wait_ge(wl_ready, n + 1)
                    for g in range(G):
                        if i == 0:
                            fill(("mf", l, g), g)
                        for t in range(4):
                            for j, (zz, w) in enumerate(((z_h, wh), (z_h, wl), (z_l, wh))):
                                last = mm(bank(g, 0, T_LAT), zz[:, t, g, i * 128:(i + 1) * 128],
                                          w[n % RING][:, t * 512:(t + 1) * 512],
                                          start=(i == 0 and t == 0 and j == 0), stop=(i == 1 and t == 3 and j == 2),
                                          skip_group_check=True)
                        if i == 1:
                            last.then_inc(bank_full[g], 1)
                        elif g == G - 1:
                            last.then_inc(sums_used, 1)
                fill(("mfc", l), 4)
                for g in range(G):
                    for i in range(2):
                        for j, (zz, w) in enumerate(((z_h, dft_h), (z_h, dft_l), (z_l, dft_h))):
                            last = mm(bank(4, g * 128, (g + 1) * 128), zz[:, 4, g, i * 128:(i + 1) * 128],
                                      w[:, i * 128:(i + 1) * 128], start=(i == 0 and j == 0), stop=(i == 1 and j == 2))
                last.then_inc(bank_full[4], 1)
                all_read()

            def gate_rows(g):
                pe.wait_ge(gcol_ready, g + 1)
                for cond in range(2):
                    for hf in range(2):
                        b = 4 + 2 * cond + hf
                        fill(("gate_bc", g, cond, hf), b)
                        for c in range(4):
                            last = mm(bank(b, c * 128, (c + 1) * 128), gcol[:, 4 * hf + c, cond:cond + 1].broadcast_to([128, 128]),
                                      ident, start=True, stop=True)
                        last.then_inc(bank_full[b], 1)

            def proj_out(l):
                pe.wait_ge(mf_ready, 2 * G * (l + 1))
                pe.wait_ge(mxa_ready, H * (l + 1))
                for hf in range(2):
                    for kh in range(2):
                        n = unit_no["out", l, 2 * hf + kh]
                        pe.wait_ge(wl_ready, n + 1)
                        for t in range(NT):
                            b = (5 * hf + t) % 8
                            if kh == 0:
                                fill(("mix", l, hf, t), b)
                            for k in range(4):
                                for j, (xp, w) in enumerate(((mx_h, wh), (mx_h, wl), (mx_l, wh))):
                                    last = mm(bank(b, 0, 512), xp[:, 4 * kh + k, t * 128:(t + 1) * 128],
                                              w[n % RING][:, k * 512:(k + 1) * 512],
                                              start=(kh == 0 and k == 0 and j == 0), stop=(kh == 1 and k == 3 and j == 2),
                                              skip_group_check=True)
                            if kh == 1:
                                last.then_inc(bank_full[b], 1)
                            elif t == NT - 1:
                                last.then_inc(sums_used, 1)

            def hidden(l, key, n0, i, slots, k):
                for part, name in enumerate(("gate", "up")):
                    if key[0] == "first" and part == 0:
                        continue
                    pe.wait_ge(wl_ready, n0 + part + 1 + i * k)
                    for j in range(2):
                        b = 2 * j
                        fill((key, name, j), b)
                        three([bank(b, 0, HALF), bank(b + 1, 0, HALF)],
                              lambda w, kk, j=j: w[:, kk * COLS + j * 128:kk * COLS + j * 128 + 128],
                              [(0, HALF), (HALF, T)], slots[part], range(KC)).then_inc(bank_full[b], 1)

            def down(l, key, n, i, slot, k):
                pe.wait_ge(wl_ready, n + 1 + i * k)
                pe.wait_ge(hid_ready, 2 + (i * 2 if k else 2 * (N_BLK - 1)))
                for t in range(NT):
                    for hf in range(2):
                        r = 2 * t + hf
                        b = 4 + r % 4
                        fill((key, "down", r), b)
                        for f in range(2):
                            for j, (xp, w) in enumerate(((hid_h, wh), (hid_h, wl), (hid_l, wh))):
                                last = mm(bank(b, 0, 512), xp[:, f, t * 128:(t + 1) * 128],
                                          w[slot][:, f * D + hf * 512:f * D + hf * 512 + 512],
                                          start=(f == 0 and j == 0), stop=(f == 1 and j == 2))
                        last.then_inc(bank_full[b], 1)

            def dense():
                l, nb = 0, N_BLK
                gate_rows(1)
                n0 = unit_no["gate", l, 0]
                hidden(l, ("first", l), n0, 0, [n0 % RING, (n0 + 1) % RING], 0)
                with pe.Fori(0, nb - 1) as i:
                    fills.enter(i, {0: 2, 2: 2, 4: 3, 5: 3, 6: 2, 7: 2})
                    hidden(l, ("body", l), n0 + 2, i, [(n0 + 2) % RING, n0 % RING], 3)
                    down(l, ("body", l), n0 + 4, i, (n0 + 1) % RING, 3)
                    fills.leave(nb - 1)
                n = unit_no["down", l, nb - 1]
                down(l, ("last", l), n, 0, n % RING, 0)

            def gather(key, chunks):
                for c in chunks:
                    b = c % 4
                    fill((key, "xg", c), b)
                    for i, src in enumerate((ht_h, ht_l)):
                        for t in range(NT):
                            last = mm(bank(b, i * SLOTS, (i + 1) * SLOTS), src[:, t, c * 128:(c + 1) * 128], pick[:, t, :],
                                      start=(t == 0), stop=(t == NT - 1))
                    last.then_inc(bank_full[b], 1)

            def experts():
                fill(("router",), 0)
                for t in range(NT):
                    for k in range(KC):
                        for j, (xp, w) in enumerate(((hn_h, rt_h), (hn_h, rt_l), (hn_l, rt_h))):
                            last = mm(bank(0, t * E, (t + 1) * E), xp[:, k, t * 128:(t + 1) * 128], w[:, k, :],
                                      start=(k == 0 and j == 0), stop=(k == KC - 1 and j == 2))
                last.then_inc(bank_full[0], 1)
                for i, src in enumerate((hn_h, hn_l)):
                    for t in range(NT):
                        b = 2 * ((2 * t + i + 1) % 4)
                        fill(("ht", i, t), b)
                        for c in range(KC):
                            last = nc.tensor.transpose(bank(b, c * 128, (c + 1) * 128),
                                                       src[:, c, t * 128:(t + 1) * 128].bitcast(F32), ident)
                        last.then_inc(bank_full[b], 1)
                all_read()
                gate_rows(3)
                pe.wait_ge(sel_ready, 1)
                fill(("pos",), 0)
                mm(bank(0, 0, NT * E), tri, sel[:, :, :].rearrange("p t e -> p (t e)"), start=True, stop=False)
                mm(bank(0, 0, NT * E), ones[:, :], csel[:, :, :].rearrange("p t e -> p (t e)"), start=False, stop=True)
                mm(bank(0, NT * E, (NT + 1) * E), ones[:, :], tsel[:, :], start=True, stop=True).then_inc(bank_full[0], 1)
                pe.wait_ge(ht_h_ready, NT)
                pe.wait_ge(ht_l_ready, NT)
                pe.wait_ge(pick_ready, 1)
                gather("ahead", range(KC))

                def turn(i, tiles):
                    pe.wait_ge(xg_act, 4 + i * 4)
                    pe.wait_ge(xg_dve, 4 + i * 4)
                    for j, (kind, q) in enumerate(EXP_UNITS):
                        w_h, w_l = wh[(N_STATIC + j) % RING], wl[(N_STATIC + j) % RING]
                        pe.wait_ge(wl_ready, N_STATIC + j + 1 + i * N_EU)
                        if kind != "down":
                            b = 2 * (q % 2) + (kind == "up")
                            fill(("exp", kind, q), b)
                            for f in range(2):
                                for k in range(KC):
                                    cols = slice(k * COLS + f * 128, k * COLS + f * 128 + 128)
                                    for p, (w, part) in enumerate(((w_h, 0), (w_h, 1), (w_l, 0))):
                                        last = mm(bank(b, f * SLOTS, (f + 1) * SLOTS), w[:, cols], xg[:, k, part, :],
                                                  start=(k == 0 and p == 0), stop=(k == KC - 1 and p == 2))
                            last.then_inc(bank_full[b], 1)
                        else:
                            pe.wait_ge(ehid_ready, q + 1 + i * EXP_BLK)
                            for st in range(tiles):
                                for hf in range(2):
                                    b = 4 + 2 * st + hf
                                    if q == 0:
                                        fill(("y", st, hf), b)
                                    for f in range(2):
                                        for p, (xp, w) in enumerate(((ehid_h, w_h), (ehid_h, w_l), (ehid_l, w_h))):
                                            last = mm(bank(b, 0, 512), xp[:, f, st * 128:(st + 1) * 128],
                                                      w[:, f * D + hf * 512:f * D + hf * 512 + 512],
                                                      start=(q == 0 and f == 0 and p == 0),
                                                      stop=(q == EXP_BLK - 1 and f == 1 and p == 2), skip_group_check=True)
                                    if q == EXP_BLK - 1:
                                        last.then_inc(bank_full[b], 1)
                            if q < EXP_BLK - 1:
                                last.then_inc(sums_used, 1)
                            elif tiles == 1:
                                for hf in range(2):
                                    fill(("y", 1, hf), 6 + hf)
                                    pe.nop().then_inc(bank_full[6 + hf], 1)
                        if j == 1:
                            for st, b in ((0, 2), (1, 3)):
                                fill(("pickT", st), b)
                                for t in range(4):
                                    last = nc.tensor.transpose(bank(b, t * 128, (t + 1) * 128),
                                                               pick[:, t, st * 128:(st + 1) * 128].bitcast(F32), ident)
                                last.then_inc(bank_full[b], 1)
                            fill(("pickT", 2), 4)
                            for st in range(2):
                                last = nc.tensor.transpose(bank(4, st * 128, (st + 1) * 128),
                                                           pick[:, 4, st * 128:(st + 1) * 128].bitcast(F32), ident)
                            last.then_inc(bank_full[4], 1)
                            fill(("gslot",), 5)
                            for st in range(2):
                                for t in range(NT):
                                    last = mm(bank(5, st, st + 1), pick[:, t, st * 128:(st + 1) * 128].bitcast(F32),
                                              gate_c[:, t:t + 1], start=(t == 0), stop=(t == NT - 1))
                            last.then_inc(bank_full[5], 1)
                        if (kind, q) == ("down", EXP_BLK - 2):
                            pe.wait_ge(pick_ready, 2 + i)
                            gather("next", range(0, KC // 2))
                    gather("next", range(KC // 2, KC))
                    pe.wait_ge(pickT_ready, 3 + i * 3)
                    pe.wait_ge(yl_ready, 4 + i * 4)
                    for r in range(2 * NT):
                        t, hf = divmod(r, 2)
                        fill(("scatter", r), r % 4)
                        for st in range(tiles):
                            for p, yy in enumerate((y_h[:, st, :], y_l[st][:, :])):
                                last = mm(bank(r % 4, 0, 512), pickT[:, st, t * 128:(t + 1) * 128],
                                          yy[:, hf * 512:(hf + 1) * 512],
                                          start=(st == 0 and p == 0), stop=(st == tiles - 1 and p == 1))
                        last.then_inc(bank_full[r % 4], 1)

                pe.wait_ge(trips_ready, 1)
                trips = pe.value_load(trips_i[0:1, 0:1], min_val=E, max_val=ROUNDS * E)
                with pe.Fori(0, trips) as i:
                    fills.enter(i, {0: 7, 1: 7, 2: 7, 3: 7, 4: 2, 5: 2, 6: 1, 7: 1})
                    left = pe.value_load(left_i[0:1, bass.ds(i, 1)], min_val=-T, max_val=T)
                    before = list(fills.total)
                    with pe.If(left > 128):
                        turn(i, 2)
                    with pe.Else():
                        fills.total = list(before)
                        turn(i, 1)
                    fills.leave(1)

            pe.wait_ge(params_landed, 80)
            pe.wait_ge(pool_const, 2)
            fill(("lam",), 0)
            pe.wait_ge(lam_v, 1)
            mm(bank(0, 0, 2 * L), ones[0:64, :], lam2[:, :, :].rearrange("p l a -> p (l a)"),
               start=True, stop=True).then_inc(bank_full[0], 1)
            pe.wait_ge(cond_ready, 1)
            pe.wait_ge(dft_ready, 1)
            for u in range(8):
                ada(u)
                ada_turn(u)
            for l in range(L):
                turn_norm(l, "pre_a", first_products(unit_no["in", l, 0], [("in", l, 0), ("in", l, 1)]))
                proj_in(l)
                attention(l)
                fourier(l)
                proj_out(l)
                first = first_products(unit_no["gate", 0, 0], [(("first", 0), "gate", j) for j in range(2)])
                turn_norm(l, "pre_f", first if l == 0 else None)
                (dense, experts)[l]()

        def full(eng, key, i=0, back=0):
            b, first, k = fills.named[key]
            first -= back * k
            eng.wait_ge(bank_full[b], first + i * k if k else first)

        def multiplied(eng, n):
            kind, l, u = units[n]
            nb = N_BLK
            if kind == "cos" or (kind == "out" and u % 2 == 0):
                eng.wait_ge(sums_used, 3 * l + {"cos": 1, "out": 2 + u // 2}[kind])
            elif kind == "ada":
                full(eng, ("ada_row", l, u))
            elif kind == "in":
                full(eng, ("in", l, 2 * u + 1) if u < 6 else ("val", l, u - 6, NT - 1))
            elif kind == "sin":
                full(eng, ("mf", l, G - 1))
            elif kind == "out":
                full(eng, ("mix", l, u // 2, NT - 1))
            elif kind == "down":
                full(eng, (("body", l) if u < nb - 1 else ("last", l), "down", 2 * NT - 1), u)
            else:
                full(eng, (("body", l) if u else ("first", l), kind, 1), u - 1)

        def free(ins, key):
            ins.then_inc(bank_free[fills.named[key][0]], 1)

        @block.sync
        def _(sp):
            sp.dma_start(consts[:, :], dram["consts"]).then_inc(params_landed, 16)
            sp.dma_start(vcol[:, :, :], dram["vcol"]).then_inc(params_landed, 16)
            sp.dma_start(lamt[:, :, :], dram["lam"]).then_inc(params_landed, 16)
            sp.dma_start(w_rt[:, :, :], dram["w_router"]).then_inc(params_landed, 16)
            sp.dma_start(w_fn[:, :], dram["w_fnet"][0]).then_inc(params_landed, 16)
            sp.dma_start(x[:, :, :], dram["x"]).then_inc(x_landed, 16)

            def unit(n, i=0, k=0, slot=None):
                s = n % RING
                if k or n >= RING:
                    sp.wait_ge(wl_ready, n - RING + 1 + i * k)
                src = dram["stream"][n] if not k else dram["stream"][bass.ds(n + i * k, 1)].rearrange("a p n -> p (a n)")
                sp.dma_start(raw[s][:, :], src).then_inc(raw_landed[s], 16)

            def expert(e, turn):
                for j in range(N_EU):
                    m = N_STATIC + j
                    sp.wait_ge(wl_ready, m - RING + 1 + turn * N_EU)
                    sp.dma_start(raw[m % RING][:, :], dram["stream"][bass.ds(m + e * N_EU, 1)].rearrange("a p n -> p (a n)")).then_inc(raw_landed[m % RING], 16)

            n = 0
            for l in range(L):
                first = unit_no["in", l, 0]
                while n < first + RING + 1:
                    unit(n)
                    n += 1
                multiplied(sp, first)
                sp.dma_start(kT[:, :, T_LAT:T], dram["cache_k"][l]).then_inc(cache_landed, 16)
                sp.dma_start(vt[:, NT, :], dram["cache_v"][l]).then_inc(cache_landed, 16)
                ready = unit_no["in", l, 7] + 1
                while n < ready + RING:
                    unit(n)
                    n += 1
                sp.wait_ge(k_out, H * (l + 1))
                sp.wait_ge(v_out, 2 * NT * (l + 1))
                sp.dma_start(out["new_k"][l], kT[:, :, T:T + T_CTX]).then_inc(stored, 16)
                sp.dma_start(out["new_v"][l], vt[:, 4, :]).then_inc(stored, 16)
                if l == 1:
                    sp.wait_ge(x_ready, 2 * NT)
                    sp.dma_start(w_fn[:, :], dram["w_fnet"][1]).then_inc(params_landed, 16)
                if l == 1:
                    break
                body = unit_no["gate", l, 0] + 2 + RING
                while n < body:
                    unit(n)
                    n += 1
                last = unit_no["down", l, N_BLK - 1]
                trips = (last - n) // RING
                with sp.Fori(0, trips) as i:
                    for j in range(RING):
                        unit(n + j, i, RING)
                n += trips * RING
                while n <= last:
                    unit(n)
                    n += 1
            while n < N_STATIC:
                unit(n)
                n += 1
            with sp.Fori(0, E) as e:
                expert(e, e)
            sp.wait_ge(trips_ready, 1)
            rounds = sp.value_load(trips_i[0:1, 1:2], min_val=1, max_val=ROUNDS)
            with sp.If(rounds > 1):
                with sp.Fori(1, rounds) as r:
                    with sp.Fori(0, E) as e:
                        expert(e, r * E + e)
            for t in range(NT):
                sp.wait_ge(x_ready, NT * 3 + t + 1)
                sp.dma_start(out["y"][:, t, :], x[:, t, :]).then_inc(stored, 16)
            sp.wait_ge(stored, 16 * (2 * L + NT))

        @block.gpsimd
        def _(pool):
            nc.gpsimd.memset(ones[:, :], 1.0).then_inc(pool_const, 1)
            nc.gpsimd.memset(mhalf[:, :], -0.5).then_inc(pool_const, 1)
            pool.wait_ge(pool_const, 2)
            steps = [0]

            def split(n, i=0, k=0):
                s = n % RING
                pool.wait_ge(wh_ready, n + 1 + i * k)
                nc.gpsimd.tensor_tensor(wl[s][:, :], raw[s][:, :], wh[s][:, :].bitcast(F32), ALU.subtract).then_inc(wl_ready, 1)

            def rsqrt(l, kind, width, no, count=1):
                c = stat_col(l, kind, no)
                pool.wait_ge(ssq_ready, stat_no(l, kind, no))
                nc.gpsimd.tensor_scalar(msq[:, c:c + count], ssq[:, c:c + count], 1.0 / width, EPS, ALU.mult, ALU.add).then_inc(pool_step, 1)
                steps[0] += 1
                pool.wait_ge(pool_step, steps[0])
                nc.gpsimd.tensor_tensor(rstd[:, c:c + count], msq[:, c:c + count], mhalf[:, 0:count], ALU.pow).then_inc(rstd_ready, 1)

            def two_norms(first, second):
                for t in range(NT + 1):
                    if t < NT:
                        rsqrt(*first, D, t)
                    if t:
                        rsqrt(*second, D, t - 1)

            n = 0

            def upto(n1):
                nonlocal n
                while n < n1:
                    split(n)
                    n += 1

            for l in range(L):
                if l == 0:
                    for t in range(NT):
                        rsqrt(0, "pre_a", D, t)
                upto(unit_no["in", l, 0])
                upto(unit_no["cos", l, 0] + 2)
                rsqrt(l, "sub", V, 0, 20)
                upto(min(unit_no["gate", l, 0] + 1, N_STATIC))
                two_norms((l, "post_a"), (l, "pre_f"))
                if l == 0:
                    upto(unit_no["gate", l, 0] + 2)
                    full(pool, ("turn", 1, KC - 1))
                    nc.gpsimd.memset(acc[:, :, :], 0.0).then_inc(acc_zero, 1)
                if l == 0:
                    last = unit_no["down", l, N_BLK - 1]
                    trips = (last + 1 - n) // RING
                    with pool.Fori(0, trips) as i:
                        for j in range(RING):
                            split(n + j, i, RING)
                    n += trips * RING
                    upto(last + 2)
                else:
                    pool.wait_ge(trips_ready, 1)
                    trips = pool.value_load(trips_i[0:1, 0:1], min_val=E, max_val=ROUNDS * E)
                    with pool.Fori(0, trips) as i:
                        for j in range(N_EU):
                            split(n + j, i, N_EU)
                if l + 1 < L:
                    two_norms((l, "post_f"), (l + 1, "pre_a"))
                else:
                    for t in range(NT):
                        rsqrt(l, "post_f", D, t)

        @block.scalar
        def _(act):
            chain = [0]

            def split(n, i=0, k=0):
                s = n % RING
                act.wait_ge(raw_landed[s], 16 * (n // RING + 1) + i * (16 * (k // RING)))
                if not k and n >= RING:
                    multiplied(act, n - RING)
                nc.scalar.copy(wh[s][:, :], raw[s][:, :]).then_inc(wh_ready, 1)

            def square(l, kind, src, t, to):
                c = stat_col(l, kind, t)
                nc.scalar.activation(to[:, t, :], src[:, t, :], ACT.Square, accum_out=ssq[:, c:c + 1]).then_inc(ssq_ready, 1)

            def two_norms(first, second, to):
                r = 2 * first[0] + (first[1] == "post_f")
                for t in range(NT + 1):
                    if t < NT:
                        act.wait_ge(y_ready, NT * r + t + 1)
                        square(*first, acc, t, to)
                    if t:
                        act.wait_ge(x_ready, NT * r + t)
                        square(*second, x, t - 1, to)

            def norm_high(l, kind):
                m = 2 * l + (kind == "pre_f")
                sh = SH_A if kind == "pre_a" else SH_F
                for c in range(KC):
                    b = fills.named["turn", m, c][0]
                    full(act, ("turn", m, c))
                    if c >= 2:
                        act.wait_ge(hn_ready, KC * m + c - 1)
                    for cond, (lo, hi) in enumerate(((0, T_LAT), (T_LAT, T))):
                        nc.scalar.activation(nrm_v[:, c % 2, lo:hi], ps[:, b * BANK + lo:b * BANK + hi], ACT.Identity,
                                             bias=modc[:, l, sh * KC + c, cond:cond + 1], scale=mulc[:, m, c, cond:cond + 1]).then_inc(nrm_v_ready, 1)
                    act.wait_ge(nrm_v_ready, 2 * (KC * m + c + 1))
                    nc.scalar.copy(hn_h[:, c, :], nrm_v[:, c % 2, :]).then_inc(nrm_h_ready, 1)
                    act.nop().then_inc(bank_free[b], 1)

            n = 0

            def ahead(stage):
                nonlocal n
                while n < min(stage + RING, N_STATIC):
                    split(n)
                    n += 1

            act.wait_ge(params_landed, 80)
            cs = cond_s[:, :, :]
            vc = vcol[:, 0, V_C:V_C + 16].rearrange("p (a c) -> p c a", a=2)
            nc.scalar.activation(cs, vc, ACT.Silu).then_inc(cond_act, 1)
            act.wait_ge(cond_act, 1)
            nc.scalar.copy(cond_p[:, :, 0:2], cs).then_inc(cond_act, 1)
            nc.scalar.copy(dft_h[:, :], consts[:, 256:512]).then_inc(act_const, 1)
            nc.scalar.copy(rt_h[:, :, :], w_rt[:, :, :]).then_inc(act_const, 1)
            full(act, ("lam",))
            free(nc.scalar.activation(lame[:, :, :].rearrange("p l a -> p (l a)"), bank(0, 0, 2 * L), ACT.Exp), ("lam",))
            act.wait_ge(x_landed, 16)
            for t in range(NT):
                square(0, "pre_a", x, t, junk)
            for u in range(8):
                ahead(u)
            for l in range(L):
                n_in = unit_no["in", l, 0]
                norm_high(l, "pre_a")
                for u in range(6):
                    ahead(n_in + u)
                    for j in range(2):
                        c = 2 * u + j
                        if c < 4:
                            full(act, ("in", l, c))
                            nc.scalar.copy(qT[:, c, :].rearrange("p (a n) -> p a n", a=2), pair(2 * (c % 4))).then_inc(q_out, 1)
                            act.wait_ge(q_out, H * l + c + 1)
                            act.nop().then_inc(bank_free[2 * (c % 4)], 1)
                        if c >= 8:
                            full(act, ("in", l, c))
                            nc.scalar.copy(fT[:, c - 8, :].rearrange("p (a n) -> p a n", a=2), pair(2 * (c % 4))).then_inc(f_out, 1)
                            act.wait_ge(f_out, G * l + c - 8 + 1)
                            act.nop().then_inc(bank_free[2 * (c % 4)], 1)
                for u in range(6, 8):
                    ahead(n_in + u)
                nu = n_in + 8

                def turned(s):
                    full(act, ("aT", l, s))
                    w = T if s % NT < 4 else 128
                    nc.scalar.copy(aT[:, s % 2, 0:w], bank(4, 0, w)).then_inc(aT_ready, 1)
                    act.wait_ge(aT_ready, 20 * l + s + 1)
                    act.nop().then_inc(bank_free[4], 1)

                for s in range(H * NT):
                    t = s % NT
                    if s:
                        turned(s - 1)
                    act.wait_ge(nmax_ready, 20 * l + s + 1)
                    for m in range(2):
                        src = pair(2 * m) if t < 4 else bank(2 * m, 0, T_CTX)
                        dst = probs[:, s % 2, m, 0:T].rearrange("p (a n) -> p a n", a=2) if t < 4 else probs[:, s % 2, m, 0:T_CTX]
                        if s >= 2 and m == 0:
                            full(act, ("aT", l, s - 2))
                        nc.scalar.activation(dst, src, ACT.Exp, bias=nmx[:, m:m + 1], scale=SCALE,
                                             accum_out=ssum[:, m:m + 1]).then_inc(exp_ready, 1)
                    act.wait_ge(exp_ready, 40 * l + 2 * s + 2)
                    act.nop().then_inc(bank_free[0], 1)
                    for _ in range(ADA_STEPS[l][t]):
                        ahead(nu)
                        nu += 1
                turned(H * NT - 1)
                for t in range(NT):
                    for g2 in range(2):
                        full(act, ("z", l, t, g2))
                        nc.scalar.copy(z_h[:, t, 2 * g2:2 * g2 + 2, :], bank(2 + (2 * t + g2) % 6, 0, 512).rearrange("p (g e) -> p g e", g=2)).then_inc(zh_ready, 1)
                for h in range(H):
                    act.wait_ge(sub_v_ready, H * l + h + 1)
                    nc.scalar.copy(mx_h[:, h, :], sub_v[:, h % 2, :]).then_inc(sub_h_ready, 1)
                ahead(unit_no["cos", l, 0])
                ahead(unit_no["sin", l, 0])
                for g in range(G):
                    full(act, ("mf", l, g))
                    nc.scalar.copy(mx_h[:, 4 + g, 0:T_LAT], bank(g, 0, T_LAT)).then_inc(mf_h_ready, 1)
                full(act, ("mfc", l))
                nc.scalar.copy(mx_h[:, 4:8, T_LAT:T], bank(4, 0, 512).rearrange("p (g n) -> p g n", g=4)).then_inc(mf_h_ready, 1)
                for u in range(4):
                    ahead(unit_no["out", l, u])
                two_norms((l, "post_a"), (l, "pre_f"), junk2)
                norm_high(l, "pre_f")
                nb = N_BLK
                if l == 1:
                    break

                def silu(key, i, first):
                    for j in range(2):
                        full(act, (key, "gate", j), i)
                        nc.scalar.activation(sg[:, j, :].rearrange("p (a n) -> p a n", a=2), pair(2 * j), ACT.Silu).then_inc(sg_ready, 1)

                def high(i, k):
                    for j in range(2):
                        act.wait_ge(hv_ready, j + 1 + (i * 2 + 2 if k else 0))
                        nc.scalar.copy(hid_h[:, j, :], sg[:, j, :]).then_inc(hid_h_ready, 1)

                n0 = unit_no["gate", l, 0]
                ahead(n0)
                silu(("first", l), 0, True)
                act.wait_ge(sg_ready, 2)
                act.nop().then_inc(bank_free[0], 1)
                act.nop().then_inc(bank_free[2], 1)
                high(0, 0)
                nn = n
                assert nn == n0 + 3
                with act.Fori(0, nb - 1) as i:
                    full(act, (("body", l), "up", 1), i, 1)
                    split(nn, i, RING)
                    act.wait_ge(hid_ready, 2 + i * 2)
                    silu(("body", l), i, False)
                    act.wait_ge(sg_ready, 4 + i * 2)
                    act.nop().then_inc(bank_free[0], 1)
                    act.nop().then_inc(bank_free[2], 1)
                    full(act, (("body", l), "down", 2 * NT - 1), i, 1)
                    split(nn + 1, i, RING)
                    split(nn + 2, i, RING)
                    full(act, (("body", l), "down", 2 * NT - 1), i)
                    high(i, 1)
                n = nn + RING * (nb - 1)
                assert n == unit_no["down", l, nb - 1] + 1
                ahead(n - 1)
                multiplied(act, unit_no["up", l, nb - 1])
                two_norms((l, "post_f"), (l + 1, "pre_a"), junk)

            act.wait_ge(x_ready, 3 * NT)
            act.dma_start(x_wait, x[:, :, :]).then_inc(x_saved, 16)
            for t in range(NT):
                full(act, ("ht", 0, t))
                b = fills.named["ht", 0, t][0]
                nc.scalar.copy(ht_h[:, t, :], ps[:, b * BANK:b * BANK + D]).then_inc(ht_h_ready, 1)
                act.wait_ge(ht_h_ready, t + 1)
                act.nop().then_inc(bank_free[b], 1)
            act.wait_ge(gexp_ready, 1)
            nc.scalar.activation(gexp[:, :], gdif[:, :], ACT.Exp).then_inc(gexp_ready, 1)

            def picked(key, chunks, i):
                for c in chunks:
                    if c % 2 == 0:
                        full(act, (key, "xg", c), i)
                        base = 4 if key == "next" else 0
                        nc.scalar.copy(xg[:, c, :, :].rearrange("p a n -> p (a n)"), bank(c % 4, 0, 2 * SLOTS)).then_inc(xg_act, 1)
                        act.wait_ge(xg_act, base + c // 2 + 1 + i * 4)
                        act.nop().then_inc(bank_free[c % 4], 1)

            picked("ahead", range(KC), 0)
            act.wait_ge(x_saved, 16)
            act.wait_ge(trips_ready, 1)
            last = act.value_load(trips_i[0:1, 2:3], min_val=E - 1, max_val=ROUNDS * E - 1)

            def exp_split(j, i):
                m = N_STATIC + j
                act.wait_ge(raw_landed[m % RING], 16 * (m // RING + 1) + i * (16 * N_EU // RING))
                nc.scalar.copy(wh[m % RING][:, :], raw[m % RING][:, :]).then_inc(wh_ready, 1)

            sums = 3 * L
            def turn(i, more):
                for q in range(EXP_BLK):
                    full(act, ("exp", "gate", q), i)
                    if q:
                        act.wait_ge(ehid_ready, q + i * EXP_BLK)
                    nc.scalar.activation(esg[:, :, :].rearrange("p a n -> p (a n)"), bank(2 * (q % 2), 0, 2 * SLOTS), ACT.Silu).then_inc(esg_ready, 1)
                    act.wait_ge(esg_ready, q + 1 + i * EXP_BLK)
                    act.nop().then_inc(bank_free[2 * (q % 2)], 1)
                    exp_split((3, 5, 8, 11)[q], i)
                    if q < EXP_BLK - 1 or more:
                        full(act, ("exp", "up", q), i)
                        exp_split((4, 6, 9, N_EU)[q], i)
                    if q:
                        act.wait_ge(sums_used, sums + q + i * (EXP_BLK - 1))
                    if 0 < q < EXP_BLK - 1:
                        exp_split((None, 7, 10)[q], i)
                    act.wait_ge(ehv_ready, q + 1 + i * EXP_BLK)
                    nc.scalar.copy(ehid_h[:, :, :], esg[:, :, :]).then_inc(ehid_h_ready, 1)
                if more:
                    exp_split(N_EU + 1, i)
                picked("next", range(0, KC // 2), i)
                act.wait_ge(gslot_ready, 1 + i)
                for st in range(2):
                    for hf in range(2):
                        full(act, ("y", st, hf), i)
                        nc.scalar.activation(y_h[:, st, hf * 512:(hf + 1) * 512], bank(4 + 2 * st + hf, 0, 512), ACT.Copy,
                                             scale=gslot[:, st:st + 1]).then_inc(yh_ready, 1)
                if more:
                    exp_split(N_EU + 2, i)
                picked("next", range(KC // 2, KC), i)

            for j in range(RING):
                exp_split(j, 0)
            with act.Fori(0, last) as i:
                turn(i, True)
            turn(last, False)
            act.wait_ge(y_ready, 4 * NT)
            act.dma_start(x[:, :, :], x_wait).then_inc(x_back, 16)
            for t in range(NT):
                c = stat_col(1, "post_f", t)
                nc.scalar.activation(junk2[:, t, :], eacc[:, t, :], ACT.Square, accum_out=ssq[:, c:c + 1]).then_inc(ssq_ready, 1)

        @block.vector
        def _(dve):
            v = nc.vector
            chain = [0]

            def link(ins):
                chain[0] += 1
                ins.then_inc(dve_step, 1)
                dve.wait_ge(dve_step, chain[0])

            def ada_row(l, u):
                full(dve, ("ada_row", l, u))
                v.tensor_copy(arow[:, :], ps[0:4, 7 * BANK:7 * BANK + COLS]).then_inc(arow_ready, 1)
                dve.wait_ge(arow_ready, 24 * l + u + 1)
                dve.nop().then_inc(bank_free[7], 1)

            def ada_col(l, u):
                full(dve, ("ada_col", l, u))
                v.tensor_tensor(modc[:, l, 2 * u:2 * u + 2, :], bank(7, 0, 4).rearrange("p (j a) -> p j a", j=2),
                                vcol[:, l, V_BADA + 2 * u:V_BADA + 2 * u + 2].unsqueeze(2).broadcast_to([128, 2, 2]),
                                ALU.add).then_inc(mod_ready, 1)
                dve.wait_ge(mod_ready, 24 * l + u + 1)
                dve.nop().then_inc(bank_free[7], 1)

            def modulation(l, kind):
                m = 2 * l + (kind == "pre_f")
                sc, vg = (SC_A, V_GAPRE) if kind == "pre_a" else (SC_F, V_GFPRE)
                link(v.tensor_scalar(mulc[:, m, :, :], modc[:, l, sc * KC:(sc + 1) * KC, :], 1.0, None, ALU.add))
                link(v.tensor_tensor(mulc[:, m, :, :], mulc[:, m, :, :],
                                     vcol[:, l, vg:vg + KC].unsqueeze(2).broadcast_to([128, KC, 2]), ALU.mult))

            def normalise(l, kind, t):
                dve.wait_ge(rstd_ready, stat_no(l, kind, t))
                c = stat_col(l, kind, t)
                v.tensor_scalar(z[:, t, :], x[:, t, :], rstd[:, c:c + 1], None, ALU.mult).then_inc(z_ready, 1)

            def norm_low(l, kind):
                m = 2 * l + (kind == "pre_f")
                for c in range(KC):
                    dve.wait_ge(nrm_h_ready, KC * m + c + 1)
                    v.tensor_tensor(hn_l[:, c, :], nrm_v[:, c % 2, :], hn_h[:, c, :].bitcast(F32), ALU.subtract).then_inc(hn_ready, 1)

            def tail(first, second, produce):
                r = 2 * first[0] + (first[1] == "post_f")
                for t in range(NT + 2):
                    if t < NT:
                        produce(t)
                    if 1 <= t <= NT:
                        residual(*first, t - 1)
                    if t >= 2:
                        normalise(*second, t - 2)

            def attention(l):
                col = None
                todo = [(0, u) for u in range(8, 24)] + [(1, u) for u in range(8)] if l == 0 else [(1, u) for u in range(8, 24)]

                def drain_o(s):
                    h, t = divmod(s, NT)
                    full(dve, ("o", l, s))
                    v.tensor_copy(o_all[:, t, h * V:(h + 1) * V], bank(6, 0, V)).then_inc(o_ready, 1)
                    dve.wait_ge(o_ready, 21 * l + s + 1)
                    dve.nop().then_inc(bank_free[6], 1)

                for s in range(H * NT):
                    t = s % NT
                    w = T if t < 4 else T_CTX
                    full(dve, ("score", l, s))
                    if t < 4:
                        src = ps[:, 0:4 * BANK].rearrange("p (m a n) -> p m a n", m=2, a=2)[:, :, :, 0:HALF]
                        link(v.tensor_reduce(smx[:, :], src, AX.XY, ALU.max))
                    else:
                        src = ps[:, 0:4 * BANK].rearrange("p (m n) -> p m n", m=2)[:, :, 0:T_CTX]
                        link(v.tensor_reduce(smx[:, :], src, AX.X, ALU.max))
                    v.tensor_scalar(nmx[:, :], smx[:, :], -SCALE, None, ALU.mult).then_inc(nmax_ready, 1)
                    if col:
                        ada_col(*col)
                        col = None
                    if s:
                        drain_o(s - 1)
                    dve.wait_ge(exp_ready, 40 * l + 2 * s + 2)
                    link(v.reciprocal(rsum[:, :], ssum[:, :]))
                    link(v.tensor_scalar(rneg[:, :], rsum[:, 1:2], nlam[:, l:l + 1], None, ALU.mult))
                    p0, p1 = probs[:, s % 2, 0, 0:w], probs[:, s % 2, 1, 0:w]
                    link(v.tensor_scalar(p0, p0, rsum[:, 0:1], None, ALU.mult))
                    v.scalar_tensor_tensor(out=p0, in0=p1, scalar=rneg[:, 0:1], in1=p0, op0=ALU.mult, op1=ALU.add).then_inc(a_ready, 1)
                    for a in range(ADA_STEPS[l][t]):
                        if a:
                            ada_col(*col)
                        col = todo.pop(0)
                        ada_row(*col)
                assert not todo
                if col:
                    ada_col(*col)
                drain_o(H * NT - 1)

            def fourier(l):
                for i in range(2):
                    if i == 0 and l == 1:
                        dve.wait_ge(params_landed, 96)
                    full(dve, ("m12", l, i))
                    v.tensor_scalar(m12[:, :, i, :], bank(i, 0, 512).rearrange("p (g e) -> p g e", g=G),
                                    1.0 if i == 0 else -1.0, None, ALU.mult).then_inc(m12_ready, 1)
                    dve.wait_ge(m12_ready, 2 * l + i + 1)
                    dve.nop().then_inc(bank_free[i], 1)
                gate_column(2 * l)
                link(v.tensor_tensor(o_sq[:, :, :], o_all[:, :, :], o_all[:, :, :], ALU.mult))
                c = stat_col(l, "sub")
                v.tensor_reduce(ssq[:, c:c + 20], o_sq[:, :, :].rearrange("p t (h e) -> p (t h) e", h=H), AX.X, ALU.add).then_inc(ssq_ready, 1)
                dve.wait_ge(ssq_ready, stat_no(l, "sub"))
                for t in range(NT):
                    for g2 in range(2):
                        r = 2 * t + g2
                        dve.wait_ge(zh_ready, 10 * l + r + 1)
                        v.tensor_tensor(z_l[:, t, 2 * g2:2 * g2 + 2, :], bank(2 + r % 6, 0, 512).rearrange("p (g e) -> p g e", g=2),
                                        z_h[:, t, 2 * g2:2 * g2 + 2, :].bitcast(F32), ALU.subtract).then_inc(zl_ready, 1)
                        dve.wait_ge(zl_ready, 10 * l + r + 1)
                        dve.nop().then_inc(bank_free[2 + r % 6], 1)
                dve.wait_ge(rstd_ready, stat_no(l, "sub"))
                o3 = o_all[:, :, :].rearrange("p t (h e) -> p (t h) e", h=H)
                v.tensor_tensor(o3, o3, rstd[:, c:c + 20].unsqueeze(2).broadcast_to([128, 20, V]), ALU.mult).then_inc(o_ready, 1)

                def low(h):
                    dve.wait_ge(sub_h_ready, H * l + h + 1)
                    v.tensor_tensor(mx_l[:, h, :], sub_v[:, h % 2, :], mx_h[:, h, :].bitcast(F32), ALU.subtract).then_inc(mxa_ready, 1)

                for h in range(H):
                    full(dve, ("sub", l, h))
                    if h >= 2:
                        dve.wait_ge(mxa_ready, H * l + h - 1)
                    v.tensor_scalar(sub_v[:, h % 2, :], bank(2 * h, 0, T), gsub[:, l:l + 1], None, ALU.mult).then_inc(sub_v_ready, 1)
                    dve.wait_ge(sub_v_ready, H * l + h + 1)
                    dve.nop().then_inc(bank_free[2 * h], 1)
                    if h:
                        low(h - 1)
                low(H - 1)
                gate_rows(2 * l)
                dve.wait_ge(mxa_ready, H * (l + 1))
                for g in range(G):
                    dve.wait_ge(mf_h_ready, 5 * l + g + 1)
                    v.tensor_tensor(mx_l[:, 4 + g, 0:T_LAT], bank(g, 0, T_LAT), mx_h[:, 4 + g, 0:T_LAT].bitcast(F32), ALU.subtract).then_inc(mf_ready, 1)
                    dve.wait_ge(mf_ready, 2 * G * l + g + 1)
                    dve.nop().then_inc(bank_free[g], 1)
                dve.wait_ge(mf_h_ready, 5 * l + 5)
                v.tensor_tensor(mx_l[:, 4:8, T_LAT:T], bank(4, 0, 512).rearrange("p (g n) -> p g n", g=4),
                                mx_h[:, 4:8, T_LAT:T].bitcast(F32), ALU.subtract).then_inc(mf_ready, 4)
                dve.wait_ge(mf_ready, 2 * G * (l + 1))
                dve.nop().then_inc(bank_free[4], 1)

            def gate_column(g):
                l, f = divmod(g, 2)
                vec, gain = ((GT_A, V_GAPOST), (GT_F, V_GFPOST))[f]
                v.tensor_tensor(gcol[:, :, :], modc[:, l, vec * KC:(vec + 1) * KC, :],
                                vcol[:, l, gain:gain + KC].unsqueeze(2).broadcast_to([128, KC, 2]), ALU.mult).then_inc(gcol_ready, 1)

            def gate_rows(g):
                for cond in range(2):
                    for hf in range(2):
                        full(dve, ("gate_bc", g, cond, hf))
                        v.tensor_copy(gate_bc[:, cond, hf * 512:(hf + 1) * 512], bank(4 + 2 * cond + hf, 0, 512)).then_inc(gate_ready, 1)
                dve.wait_ge(gate_ready, 4 * (g + 1))
                for b in range(4, 8):
                    dve.nop().then_inc(bank_free[b], 1)

            def residual(l, kind, t):
                r = 2 * l + (kind == "post_f")
                y = eacc if (l, kind) == (1, "post_f") else acc
                dve.wait_ge(rstd_ready, stat_no(l, kind, t))
                c = stat_col(l, kind, t)
                link(v.scalar_tensor_tensor(out=y[:, t, :], in0=y[:, t, :], scalar=rstd[:, c:c + 1],
                                            in1=gate_bc[:, 0 if t < 4 else 1, :], op0=ALU.mult, op1=ALU.mult))
                v.tensor_tensor(x[:, t, :], x[:, t, :], y[:, t, :], ALU.add).then_inc(x_ready, 1)

            def products(l, key, i, k):
                for j in range(2):
                    full(dve, (key, "up", j), i)
                    view = sg[:, j, :].rearrange("p (a n) -> p a n", a=2)
                    v.tensor_tensor(view, view, pair(2 * j), ALU.mult).then_inc(hv_ready, 1)
                dve.wait_ge(hv_ready, 2 + (i * 2 + 2 if k else 0))
                dve.nop().then_inc(bank_free[0], 1)
                dve.nop().then_inc(bank_free[2], 1)

            def low_hidden(l, i, k):
                for j in range(2):
                    dve.wait_ge(hid_h_ready, j + 1 + (i * 2 + 2 if k else 0))
                    v.tensor_tensor(hid_l[:, j, :], sg[:, j, :], hid_h[:, j, :].bitcast(F32), ALU.subtract).then_inc(hid_ready, 1)

            def add_down(l, key, i, k, rs):
                for r in rs:
                    t, hf = divmod(r, 2)
                    full(dve, (key, "down", r), i)
                    a = acc[:, t, hf * 512:(hf + 1) * 512]
                    v.tensor_tensor(a, a, bank(4 + r % 4, 0, 512), ALU.add).then_inc(bank_free[4 + r % 4], 1)

            def route():
                full(dve, ("router",))
                link(v.tensor_copy(logit[:, :, :].rearrange("p t e -> p (t e)"), bank(0, 0, NT * E)))
                dve.nop().then_inc(bank_free[0], 1)
                for t in range(NT):
                    link(v.max(top8[:, t, :], logit[:, t, :]))
                    link(v.max_index(idx8[:, t, :], top8[:, t, :], logit[:, t, :]))
                link(v.tensor_copy(idxf[:, :, :], idx8[:, :, 0:2]))
                v.tensor_tensor(gdif[:, :], top8[:, :, 1], top8[:, :, 0], ALU.subtract).then_inc(gexp_ready, 1)
                io = iota8.unsqueeze(1).broadcast_to([128, NT, E])
                link(v.tensor_tensor(sel[:, :, :], io, idxf[:, :, 0:1].broadcast_to([128, NT, E]), ALU.is_equal))
                link(v.tensor_tensor(gsel[:, :, :], io, idxf[:, :, 1:2].broadcast_to([128, NT, E]), ALU.is_equal))
                dve.wait_ge(gexp_ready, 2)
                link(v.tensor_scalar(gden[:, :], gexp[:, :], 1.0, None, ALU.add))
                link(v.reciprocal(g12[:, :, 0], gden[:, :]))
                link(v.tensor_tensor(g12[:, :, 1], g12[:, :, 0], gexp[:, :], ALU.mult))
                link(v.tensor_tensor(gates[:, :, :], sel[:, :, :], g12[:, :, 0:1].broadcast_to([128, NT, E]), ALU.mult))
                link(v.tensor_tensor(pos[:, :, :], gsel[:, :, :], g12[:, :, 1:2].broadcast_to([128, NT, E]), ALU.mult))
                link(v.tensor_tensor(gates[:, :, :], gates[:, :, :], pos[:, :, :], ALU.add))
                link(v.tensor_tensor(sel[:, :, :], sel[:, :, :], gsel[:, :, :], ALU.add))
                link(v.memset(csel[:, 0, :], 0.0))
                for t in range(1, NT):
                    link(v.tensor_tensor(csel[:, t, :], csel[:, t - 1, :], sel[:, t - 1, :], ALU.add))
                v.tensor_tensor(tsel[:, :], csel[:, NT - 1, :], sel[:, NT - 1, :], ALU.add).then_inc(sel_ready, 1)
                for t in range(NT):
                    full(dve, ("ht", 1, t))
                    b = fills.named["ht", 1, t][0]
                    v.tensor_copy(ht_l[:, t, :], ps[:, b * BANK:b * BANK + D]).then_inc(ht_l_ready, 1)
                    dve.wait_ge(ht_l_ready, t + 1)
                    dve.nop().then_inc(bank_free[b], 1)
                full(dve, ("pos",))
                link(v.tensor_scalar(pos[:, :, :].rearrange("p t e -> p (t e)"), bank(0, 0, NT * E), FAR, None, ALU.add))
                link(v.tensor_copy(total[:, :], bank(0, NT * E, (NT + 1) * E)))
                link(v.tensor_reduce(most[:, 0:1], total[:, :], AX.X, ALU.max))
                dve.nop().then_inc(bank_free[0], 1)
                link(v.tensor_tensor(pos[:, :, :], pos[:, :, :], sel[:, :, :], ALU.mult))
                for r in range(ROUNDS):
                    link(v.tensor_scalar(slot_x[:, :, r * E:(r + 1) * E], pos[:, :, :], -FAR - r * SLOTS, None, ALU.add))
                    link(v.tensor_copy(gate_x[:, :, r * E:(r + 1) * E], gates[:, :, :]))
                link(v.memset(slot_x[:, :, ROUNDS * E:], -FAR))
                link(v.memset(gate_x[:, :, ROUNDS * E:], 0.0))
                pick_first()
                for r in range(1, ROUNDS):
                    link(v.tensor_scalar(most[:, r:r + 1], most[:, 0:1], float(r * SLOTS), None, ALU.is_gt))
                link(v.tensor_reduce(trips_f[:, 1:2], most[:, 1:ROUNDS], AX.X, ALU.add))
                link(v.tensor_scalar(trips_f[:, 1:2], trips_f[:, 1:2], 1.0, None, ALU.add))
                link(v.tensor_scalar(trips_f[:, 0:1], trips_f[:, 1:2], float(E), None, ALU.mult))
                link(v.tensor_scalar(trips_f[:, 2:3], trips_f[:, 0:1], -1.0, None, ALU.add))
                for r in range(ROUNDS):
                    link(v.tensor_scalar(left_f[:, r * E:(r + 1) * E], total[:, :], -float(r * SLOTS), None, ALU.add))
                link(v.tensor_copy(left_i[:, :], left_f[:, :]))
                v.tensor_copy(trips_i[:, :], trips_f[:, :]).then_inc(trips_ready, 1)

            def pick_first():
                link(v.tensor_copy(slot_c[:, :], slot_x[:, :, 0]))
                link(v.tensor_copy(gate_c[:, :], gate_x[:, :, 0]))
                for t in range(NT):
                    ins = v.tensor_scalar(pick[:, t, :], iota_s, slot_c[:, t:t + 1], None, ALU.is_equal)
                ins.then_inc(pick_ready, 1)

            def picked(key, chunks, i):
                for c in chunks:
                    if c % 2:
                        full(dve, (key, "xg", c), i)
                        base = 4 if key == "next" else 0
                        v.tensor_copy(xg[:, c, :, :].rearrange("p a n -> p (a n)"), bank(c % 4, 0, 2 * SLOTS)).then_inc(xg_dve, 1)
                        dve.wait_ge(xg_dve, base + c // 2 + 1 + i * 4)
                        dve.nop().then_inc(bank_free[c % 4], 1)

            def experts():
                picked("ahead", range(KC), 0)
                link(v.memset(eacc[:, :, :], 0.0))
                dve.wait_ge(trips_ready, 1)
                trips = dve.value_load(trips_i[0:1, 0:1], min_val=E, max_val=ROUNDS * E)
                with dve.Fori(0, trips) as i:
                    for q in range(EXP_BLK):
                        full(dve, ("exp", "up", q), i)
                        dve.wait_ge(esg_ready, q + 1 + i * EXP_BLK)
                        sg2 = esg[:, :, :].rearrange("p a n -> p (a n)")
                        v.tensor_tensor(sg2, sg2, bank(2 * (q % 2) + 1, 0, 2 * SLOTS), ALU.mult).then_inc(ehv_ready, 1)
                        dve.wait_ge(ehv_ready, q + 1 + i * EXP_BLK)
                        dve.nop().then_inc(bank_free[2 * (q % 2) + 1], 1)
                        if q == 0:
                            for st in range(2):
                                full(dve, ("pickT", st), i)
                                v.tensor_copy(pickT[:, st, 0:T_LAT], bank(2 + st, 0, T_LAT)).then_inc(pickT_ready, 1)
                                dve.wait_ge(pickT_ready, st + 1 + i * 3)
                                dve.nop().then_inc(bank_free[2 + st], 1)
                            full(dve, ("pickT", 2), i)
                            v.tensor_copy(pickT[:, :, T_LAT:T], bank(4, 0, 256).rearrange("p (a n) -> p a n", a=2)).then_inc(pickT_ready, 1)
                            dve.wait_ge(pickT_ready, 3 + i * 3)
                            dve.nop().then_inc(bank_free[4], 1)
                            full(dve, ("gslot",), i)
                            v.tensor_copy(gslot[:, :], bank(5, 0, 2)).then_inc(gslot_ready, 1)
                            dve.wait_ge(gslot_ready, 1 + i)
                            dve.nop().then_inc(bank_free[5], 1)
                        dve.wait_ge(ehid_h_ready, q + 1 + i * EXP_BLK)
                        v.tensor_tensor(ehid_l[:, :, :], esg[:, :, :], ehid_h[:, :, :].bitcast(F32), ALU.subtract).then_inc(ehid_ready, 1)
                        if q == 0:
                            v.tensor_copy(slot_c[:, :], slot_x[:, :, bass.ds(i + 1, 1)].rearrange("p t a -> p (t a)")).then_inc(slot_ready, 1)
                            v.tensor_copy(gate_c[:, :], gate_x[:, :, bass.ds(i + 1, 1)].rearrange("p t a -> p (t a)")).then_inc(slot_ready, 1)
                            dve.wait_ge(slot_ready, 2 + i * 2)
                            for t in range(NT):
                                ins = v.tensor_scalar(pick[:, t, :], iota_s, slot_c[:, t:t + 1], None, ALU.is_equal)
                            ins.then_inc(pick_ready, 1)
                    picked("next", range(0, KC // 2), i)
                    for st in range(2):
                        for hf in range(2):
                            b = 4 + 2 * st + hf
                            r = 2 * st + hf
                            dve.wait_ge(yh_ready, r + 1 + i * 4)
                            v.scalar_tensor_tensor(out=y_l[st][:, hf * 512:(hf + 1) * 512], in0=bank(b, 0, 512), scalar=gslot[:, st:st + 1],
                                                   in1=y_h[:, st, hf * 512:(hf + 1) * 512].bitcast(F32), op0=ALU.mult, op1=ALU.subtract).then_inc(yl_ready, 1)
                            dve.wait_ge(yl_ready, r + 1 + i * 4)
                            dve.nop().then_inc(bank_free[b], 1)
                    picked("next", range(KC // 2, KC), i)
                    for r in range(2 * NT):
                        t, hf = divmod(r, 2)
                        full(dve, ("scatter", r), i)
                        a = eacc[:, t, hf * 512:(hf + 1) * 512]
                        v.tensor_tensor(a, a, bank(r % 4, 0, 512), ALU.add).then_inc(bank_free[r % 4], 1)
                dve.drain().then_inc(y_ready, NT)
                dve.wait_ge(x_back, 16)

            params = 80
            dve.wait_ge(params_landed, params)
            lt = lamt[:, :, :].rearrange("p l (a b) -> p l a b", a=2)
            v.tensor_tensor(lam2[:, :, :], lt[:, :, :, 0], lt[:, :, :, 1], ALU.mult).then_inc(lam_v, 1)
            dve.wait_ge(cond_act, 2)
            v.tensor_tensor(cond_p[:, :, 2:4], cond_s[:, :, :], cond_p[:, :, 0:2].bitcast(F32), ALU.subtract).then_inc(cond_ready, 1)
            dve.wait_ge(act_const, 2)
            v.tensor_tensor(dft_l[:, :], consts[:, 256:512], dft_h[:, :].bitcast(F32), ALU.subtract).then_inc(dft_ready, 1)
            v.tensor_tensor(rt_l[:, :, :], w_rt[:, :, :], rt_h[:, :, :].bitcast(F32), ALU.subtract).then_inc(dft_ready, 1)
            dve.wait_ge(bank_free[0], 1)
            link(v.tensor_tensor(nlam[:, :], lame[:, :, 1], lame[:, :, 0], ALU.subtract))
            for l in range(L):
                lam_init = 0.8 - 0.6 * math.exp(-0.3 * l)
                link(v.tensor_scalar(nlam[:, l:l + 1], nlam[:, l:l + 1], -lam_init, None, ALU.add))
                link(v.tensor_scalar(gsub[:, l:l + 1], vcol[:, l, V_SUB:V_SUB + 1], 1.0 - lam_init, None, ALU.mult))
            for u in range(8):
                ada_row(0, u)
                ada_col(0, u)
            modulation(0, "pre_a")
            dve.wait_ge(x_landed, 16)
            for t in range(NT):
                normalise(0, "pre_a", t)
            for l in range(L):
                norm_low(l, "pre_a")
                for c in range(4, 8):
                    b = 2 * (c % 4)
                    full(dve, ("in", l, c))
                    v.tensor_copy(kT[:, c - 4, 0:HALF], bank(b, 0, HALF)).then_inc(dve_step, 1)
                    v.tensor_copy(kT[:, c - 4, HALF:T_LAT], bank(b + 1, 0, T_LAT - HALF)).then_inc(dve_step, 1)
                    chain[0] += 2
                    dve.wait_ge(dve_step, chain[0])
                    v.tensor_copy(kT[:, c - 4, T:T + T_CTX], bank(b + 1, T_LAT - HALF, HALF)).then_inc(k_out, 1)
                    dve.wait_ge(k_out, H * l + c - 3)
                    dve.nop().then_inc(bank_free[b], 1)
                for c in range(2 * H):
                    full(dve, ("rot", l, c))
                    a = (qT if c % 2 == 0 else kT)[:, c // 2, 0:T_LAT]
                    link(v.tensor_tensor(rope_t[:, :], bank(c, 0, T_LAT), sin_r, ALU.mult))
                    dve.nop().then_inc(bank_free[c], 1)
                    link(v.tensor_tensor(a, a, cos_r, ALU.mult))
                    v.tensor_tensor(a, a, rope_t[:, :], ALU.add).then_inc(rope_ready, 1)
                    dve.wait_ge(rope_ready, 2 * H * l + c + 1)
                for u in range(2):
                    for t in range(NT):
                        full(dve, ("val", l, u, t))
                        v.tensor_copy(vt[:, t, u * 256:(u + 1) * 256], bank((5 * u + t) % 8, 0, 256)).then_inc(v_out, 1)
                        dve.wait_ge(v_out, 2 * NT * l + 5 * u + t + 1)
                        dve.nop().then_inc(bank_free[(5 * u + t) % 8], 1)
                attention(l)
                fourier(l)
                modulation(l, "pre_f")

                def mixed(hf, t):
                    full(dve, ("mix", l, hf, t))
                    b = (5 * hf + t) % 8
                    v.tensor_copy(acc[:, t, hf * 512:(hf + 1) * 512], bank(b, 0, 512)).then_inc(y_ready if hf else dve_step, 1)
                    if hf == 0:
                        chain[0] += 1
                        dve.wait_ge(dve_step, chain[0])
                    else:
                        dve.wait_ge(y_ready, NT * 2 * l + t + 1)
                    dve.nop().then_inc(bank_free[b], 1)

                for t in range(NT):
                    mixed(0, t)
                tail((l, "post_a"), (l, "pre_f"), lambda t: mixed(1, t))
                gate_column(2 * l + 1)
                norm_low(l, "pre_f")
                if l == 1:
                    route()
                    gate_rows(3)
                    experts()
                    for t in range(NT):
                        residual(1, "post_f", t)
                    break
                gate_rows(1)
                nb = N_BLK
                dve.wait_ge(sg_ready, 2)
                products(l, ("first", l), 0, 0)
                low_hidden(l, 0, 0)
                dve.wait_ge(acc_zero, 1)
                with dve.Fori(0, nb - 1) as i:
                    dve.wait_ge(sg_ready, 4 + i * 2)
                    products(l, ("body", l), i, 1)
                    add_down(l, ("body", l), i, 1, range(2 * NT))
                    low_hidden(l, i, 1)
                modulation(l + 1, "pre_a")

                def summed(t):
                    rs = (2 * t, 2 * t + 1)
                    add_down(l, ("last", l), 0, 0, rs)
                    for r in rs:
                        dve.wait_ge(bank_free[4 + r % 4], fills.named[(("last", l), "down", r)][1])
                    dve.nop().then_inc(y_ready, 1)

                tail((l, "post_f"), (l + 1, "pre_a"), summed)


def dft(n):
    j = np.outer(np.arange(n), np.arange(n)) % n
    return (np.cos(2 * np.pi * j / n) / math.sqrt(n)).astype(np.float32), (np.sin(2 * np.pi * j / n) / math.sqrt(n)).astype(np.float32)


def shape_constants():
    c, s = dft(128)
    rot = np.zeros((128, 128), np.float32)
    for d in range(128):
        b, r = divmod(d, 16)
        if b % 2 == 0:
            rot[d + 16, d] = -1.0
        else:
            rot[d - 16, d] = 1.0
    grid_w, half = 64, QK // 2
    inv = (1.0 / (np.float32(10000.0) ** (np.arange(0, half, 2, dtype=np.float32) / np.float32(half)))).astype(np.float32)
    pos = np.arange(T_LAT)
    tabs = []
    for p in (pos // grid_w, pos % grid_w):
        a = p.astype(np.float32)[:, None] * inv[None, :]
        tabs += [a, a]
    ang = np.concatenate(tabs, axis=1)
    ang = np.concatenate([ang, ang], axis=1).T
    iota = np.tile(np.concatenate([np.arange(8), np.arange(SLOTS)]).astype(np.float32), (128, 1))
    tri = np.triu(np.ones((128, 128), np.float32), 1)
    sel = np.zeros((128, 2), np.float32)
    for r in range(4):
        sel[r, r % 2] = 1.0
    consts = np.concatenate([np.eye(128, dtype=np.float32), rot, c, s, np.cos(ang), np.sin(ang), iota, tri, sel], axis=1)
    c5, s5 = dft(T_LAT)
    lay = lambda a: a.reshape(4, 128, T_LAT).transpose(1, 0, 2).reshape(128, UNIT)
    return np.ascontiguousarray(consts.astype(np.float32)), lay(c5), lay(s5)


def kernel(x_prompt, x_sample, cache_k, cache_v, c, c_ctx, g_attn_pre, g_attn_post, g_ffn_pre, g_ffn_post,
           w_ada, b_ada, w_in, lam_params, g_subln, w_fnet, w_out, w_gate, w_up, w_down, w_router,
           e_gate, e_up, e_down):
    import concourse.bacc as bacc
    from concourse.bass_utils import run_bass_kernel_spmd

    A = np.asarray
    consts, cos5, sin5 = shape_constants()

    def wide(w, u):
        return A(w)[:, u * COLS:(u + 1) * COLS].reshape(KC, 128, COLS).transpose(1, 0, 2).reshape(128, UNIT)

    def rows(w, r, n):
        w = A(w)[r:r + n]
        return w.reshape(n // 128, 128, w.shape[1]).transpose(1, 0, 2).reshape(128, UNIT)

    in_cols = [0, 1, 2, 3, 6, 7, 4, 5]
    units = plan_units()
    stream = np.empty((len(units), 128, UNIT), np.float32)
    for n, (kind, l, u) in enumerate(units):
        e, q = divmod(u, EXP_BLK)
        if kind == "ada":
            stream[n] = wide(w_ada[l], u)
        elif kind == "in":
            stream[n] = wide(w_in[l], in_cols[u])
        elif kind == "cos":
            stream[n] = cos5
        elif kind == "sin":
            stream[n] = sin5
        elif kind == "out":
            stream[n] = rows(A(w_out[l])[:, (u // 2) * 512:(u // 2 + 1) * 512], (u % 2) * 512, 512)
        elif kind == "gate":
            stream[n] = wide(w_gate[0], u) if l == 0 else wide(e_gate[0][e], q)
        elif kind == "up":
            stream[n] = wide(w_up[0], u) if l == 0 else wide(e_up[0][e], q)
        else:
            stream[n] = rows(w_down[0], u * COLS, COLS) if l == 0 else rows(e_down[0][e], q * COLS, COLS)
    vrows = np.zeros((L, 128, 128), np.float32)
    for l in range(L):
        parts = [b_ada[l], g_attn_pre[l], g_attn_post[l], g_ffn_pre[l], g_ffn_post[l], c[0], c_ctx, g_subln[l]]
        flat = np.concatenate([A(p).reshape(-1, 128) for p in parts], axis=0)
        vrows[l, :flat.shape[0]] = flat
    x_all = np.concatenate([A(x_sample)[0], A(x_prompt)[0]], axis=0)
    arrays = {
        "stream": stream,
        "consts": consts,
        "vcol": vrows.transpose(2, 0, 1),
        "x": x_all.reshape(NT, 128, D).transpose(1, 0, 2),
        "lam": A(lam_params).transpose(2, 0, 1),
        "w_router": A(w_router)[0].reshape(KC, 128, E).transpose(1, 0, 2),
        "w_fnet": A(w_fnet).transpose(0, 2, 1, 3).reshape(L, 128, G * 128),
        "cache_k": A(cache_k)[0].reshape(L, PAST, H, 2 * QK).transpose(0, 3, 2, 1),
        "cache_v": A(cache_v)[0].reshape(L, PAST, H * V),
    }
    arrays = {k: np.ascontiguousarray(a) for k, a in arrays.items()}
    nc = bacc.Bacc("TRN2", target_bir_lowering=False, num_devices=1)
    dram = {k: nc.dram_tensor(k, a.shape, F32, kind="ExternalInput").ap() for k, a in arrays.items()}
    shapes = {"y": (128, NT, D), "new_k": (L, 128, H, T_CTX), "new_v": (L, 128, H * V)}
    out = {k: nc.dram_tensor(k, s, F32, kind="ExternalOutput").ap() for k, s in shapes.items()}
    build(nc, dram, out)
    r = run_bass_kernel_spmd(nc, [arrays], core_ids=[0]).results[0]
    y = A(r["y"]).transpose(1, 0, 2).reshape(T, D)
    new_k = A(r["new_k"]).transpose(0, 3, 2, 1).reshape(1, L, T_CTX, H, 2, QK)
    new_v = A(r["new_v"]).reshape(1, L, T_CTX, H, V)
    return (np.ascontiguousarray(y[T_LAT:])[None], np.ascontiguousarray(y[:T_LAT])[None],
            np.ascontiguousarray(new_k), np.ascontiguousarray(new_v))
```

```python
import math
from contextlib import ExitStack

import numpy as np
import concourse.bass as bass
from concourse import mybir
from concourse.alu_op_type import AluOpType as ALU

F32 = mybir.dt.float32
F32R = mybir.dt.float32r
U32 = mybir.dt.uint32
I32 = mybir.dt.int32
ACT = mybir.ActivationFunctionType
AX = mybir.AxisListType

D = 1024
KC = D // 128
L = 2
T_LAT, T_CTX, PAST = 512, 128, 128
T = T_LAT + T_CTX
NT = T // 128
H, QK, V = 4, 64, 128
G = 4
F_DENSE, F_EXP, E = 2816, 1024, 8
UNIT = 2048
RING = 3
FIRST = 8
COLS = UNIT // KC
N_BLK = F_DENSE // COLS
EXP_BLK = F_EXP // COLS
SLOTS = 256
ROUNDS = -(-T // SLOTS)
EXP_UNITS = [("gate", 0), ("up", 0), ("gate", 1), ("up", 1), ("down", 0), ("gate", 2), ("up", 2), ("down", 1),
             ("gate", 3), ("up", 3), ("down", 2), ("down", 3)]
N_EU = len(EXP_UNITS)
EPS = 1e-6
FAR = 1048576.0
SCALE = QK ** -0.5
HALF = T // 2
BANK = 512
ADA_STEPS = ((1, 1, 1, 1, 2), (1, 1, 1, 1, 0))
SH_A, SC_A, GT_A, SH_F, SC_F, GT_F = range(6)
V_BADA, V_GAPRE, V_GAPOST, V_GFPRE, V_GFPOST, V_C, V_CTX, V_SUB = 0, 48, 56, 64, 72, 80, 88, 96


def plan_units():
    units = [("ada", 0, u) for u in range(FIRST)]
    ada = [[("ada", 0, u) for u in range(8, 24)] + [("ada", 1, u) for u in range(8)],
           [("ada", 1, u) for u in range(8, 24)]]
    for l in range(L):
        units += [("in", l, u) for u in range(8)]
        units += ada[l]
        units += [("cos", l, 0), ("sin", l, 0)]
        units += [("out", l, u) for u in range(4)]
        if l == 0:
            units += [("gate", l, 0), ("up", l, 0)]
            for b in range(1, N_BLK):
                units += [("gate", l, b), ("up", l, b), ("down", l, b - 1)]
            units += [("down", l, N_BLK - 1)]
        else:
            units += [(kind, l, e * EXP_BLK + q) for e in range(E) for kind, q in EXP_UNITS]
    return units


def stat_no(l, kind, t=0):
    if kind == "pre_a" and l == 0:
        return t + 1
    if kind == "sub":
        return l * 21 + 6
    base = {"post_a": 6 + 21 * l, "pre_f": 6 + 21 * l, "post_f": 16 + 21 * l, "pre_a": 16}[kind]
    if kind == "post_f" and l == L - 1:
        return base + t + 1
    if kind[:4] == "post":
        return base + max(2 * t - 1, 0) + 1
    return base + min(2 * t + 2, 2 * NT - 1) + 1


def stat_col(l, kind, t=0):
    return l * 40 + {"pre_a": 0, "sub": 20, "post_a": 5, "pre_f": 10, "post_f": 15}[kind] + t


class Fills:

    def __init__(self):
        self.total = [0] * 8
        self.named = {}
        self.i, self.per = None, None

    def enter(self, i, per):
        self.i, self.per, self.at = i, per, list(self.total)

    def leave(self, n):
        for b, k in self.per.items():
            assert self.total[b] - self.at[b] == k, (b, k, self.total[b] - self.at[b])
        assert all(self.total[b] == self.at[b] for b in range(8) if b not in self.per)
        for b, k in self.per.items():
            self.total[b] = self.at[b] + n * k
        self.i = None

    def next(self, key, b):
        before, k = self.total[b], self.per.get(b, 0) if self.i is not None else 0
        self.total[b] += 1
        self.named[key] = (b, before + 1, k)
        return before if not k else before + self.i * k


def build(nc, dram, out):
    units = plan_units()
    unit_no = {u: n for n, u in enumerate(units)}
    N_STATIC = unit_no["gate", 1, 0]

    with ExitStack() as ctx:
        def sem(name):
            return ctx.enter_context(nc.semaphore(name))

        top = [(nc.sbuf_base + 31) // 32 * 32]

        def at(name, shape, dt, offset):
            return nc.alloc_sbuf_tensor_at(name, shape, dt, offset=offset)

        def sb(name, shape, dt=F32):
            off = top[0]
            top[0] += (int(np.prod(shape[1:])) * 4 + 31) // 32 * 32
            return at(name, shape, dt, off)

        x_off = top[0]
        x = sb("x", [128, NT, D])
        ehid_h = at("ehid_h", [128, 2, SLOTS], F32R, x_off)
        ehid_l = at("ehid_l", [128, 2, SLOTS], F32R, x_off + 2048)
        esg = at("esg", [128, 2, SLOTS], F32, x_off + 4096)
        y_h = at("y_h", [128, 2, D], F32R, x_off + 6144)
        act_off = top[0]
        hn_h = sb("hn_h", [128, KC, T], F32R)
        hn_l = sb("hn_l", [128, KC, T], F32R)
        half_kc = KC // 2 * T * 4
        mx_h = at("mx_h", [128, KC, T], F32R, act_off)
        mx_l = at("mx_l", [128, KC, T], F32R, act_off + 2 * half_kc)
        junk = at("junk", [128, NT, D], F32, act_off)
        o_all = at("o_all", [128, NT, H * V], F32, act_off + half_kc)
        probs = at("probs", [128, 2, 2, T], F32, act_off + 3 * half_kc)
        o_sq = at("o_sq", [128, NT, H * V], F32, act_off + 3 * half_kc)
        eacc = at("eacc", [128, NT, D], F32, act_off)
        xg = at("xg", [128, KC, 2, SLOTS], F32R, act_off + 20480)
        y_l = [at("y_l0", [128, D], F32R, act_off + 36864), at("y_l1", [128, D], F32R, x_off + 14336)]
        raw = [sb(f"raw{s}", [128, UNIT]) for s in range(RING)]
        wh = [sb(f"wh{s}", [128, UNIT], F32R) for s in range(RING)]
        wl = [sb(f"wl{s}", [128, UNIT], F32R) for s in range(RING)]
        m_off = top[0]
        top[0] += 51200
        fT = at("fT", [128, G, T], F32, m_off)
        qT = at("qT", [128, H, T], F32, m_off + 10240)
        kT = at("kT", [128, H, T + PAST], F32, m_off + 20480)
        vt = at("vt", [128, NT + 1, H * V], F32, m_off + 32768)
        rope_t = at("rope_t", [128, T_LAT], F32, m_off + 45056)
        aT = at("aT", [128, 2, T], F32, m_off + 45056)
        z_h = at("z_h", [128, NT, G, 256], F32R, m_off + 10240)
        z_l = at("z_l", [128, NT, G, 256], F32R, m_off + 30720)
        o_norm = at("o_norm", [128, NT, H * V], F32, m_off)
        sub_v = at("sub_v", [128, 2, T], F32, m_off + 10240)
        nrm_v = at("nrm_v", [128, 2, T], F32, m_off)
        sg = at("sg", [128, 2, T], F32, m_off)
        hid_h = at("hid_h", [128, 2, T], F32R, m_off + 5120)
        hid_l = at("hid_l", [128, 2, T], F32R, m_off + 10240)
        acc = at("acc", [128, NT, D], F32, m_off + 25600)
        z = at("z", [128, NT, D], F32, m_off + 25600)
        ht_h = at("ht_h", [128, NT, D], F32R, m_off)
        ht_l = at("ht_l", [128, NT, D], F32R, m_off + 20480)
        junk2 = at("junk2", [128, NT, D], F32, m_off)
        pick = at("pick", [128, NT, SLOTS], F32R, m_off + 40960)
        pickT = at("pickT", [128, 2, T], F32R, m_off + 46080)
        gate_off = top[0]
        gate_bc = sb("gate_bc", [128, 2, D])
        w_fn = at("w_fn", [128, G * 128], F32, gate_off)
        m12 = at("m12", [128, G, 2, 128], F32, gate_off + 2048)
        NCONST = 4 * 128 + 2 * T_LAT + 8 + SLOTS + 128 + 2
        const_off = top[0]
        consts = sb("consts", [128, NCONST])
        ident, rot, c128, s128 = (consts[:, 128 * i:128 * (i + 1)] for i in range(4))
        cos_r, sin_r = consts[:, 512:512 + T_LAT], consts[:, 512 + T_LAT:512 + 2 * T_LAT]
        iota8 = consts[:, 512 + 2 * T_LAT:512 + 2 * T_LAT + 8]
        iota_s = consts[:, 520 + 2 * T_LAT:520 + 2 * T_LAT + SLOTS]
        tri = consts[:, 520 + 2 * T_LAT + SLOTS:520 + 2 * T_LAT + SLOTS + 128]
        sel4 = consts[0:4, NCONST - 2:NCONST]
        dft_h = sb("dft_h", [128, 2 * 128], F32R)
        dft_l = sb("dft_l", [128, 2 * 128], F32R)
        ones = sb("ones", [128, 128])
        vcol = sb("vcol", [128, L, 128])
        modc = sb("modc", [128, L, 48, 2])
        mulc = sb("mulc", [128, 2 * L, KC, 2])
        arow = sb("arow", [4, COLS])
        cond_s = sb("cond_s", [128, KC, 2])
        cond_p = sb("cond_p", [128, KC, 4], F32R)
        ssq = sb("ssq", [128, L * 40])
        msq = sb("msq", [128, L * 40])
        rstd = sb("rstd", [128, L * 40])
        mhalf = sb("mhalf", [128, 20])
        lamt = sb("lamt", [64, L, 4])
        lam2 = sb("lam2", [64, L, 2])
        lame = sb("lame", [128, L, 2])
        nlam = sb("nlam", [128, L])
        gsub = sb("gsub", [128, L])
        smx = sb("smx", [128, 2])
        nmx = sb("nmx", [128, 2])
        ssum = sb("ssum", [128, 2])
        rsum = sb("rsum", [128, 2])
        rneg = sb("rneg", [128, 1])
        gcol = sb("gcol", [128, KC, 2])
        w_rt = sb("w_rt", [128, KC, E])
        rt_h = sb("rt_h", [128, KC, E], F32R)
        rt_l = sb("rt_l", [128, KC, E], F32R)
        logit = sb("logit", [128, NT, E])
        top8 = sb("top8", [128, NT, 8])
        idx8 = sb("idx8", [128, NT, 8], U32)
        idxf = sb("idxf", [128, NT, 2])
        gdif = sb("gdif", [128, NT])
        gexp = sb("gexp", [128, NT])
        gden = sb("gden", [128, NT])
        g12 = sb("g12", [128, NT, 2])
        gsel = sb("gsel", [128, NT, E])
        gates = sb("gates", [128, NT, E])
        sel = sb("sel", [128, NT, E])
        csel = sb("csel", [128, NT, E])
        tsel = sb("tsel", [128, E])
        pos = sb("pos", [128, NT, E])
        slot_x = at("slot_x", [128, NT, ROUNDS * E + 1], F32, const_off + 2048)
        gate_x = at("gate_x", [128, NT, ROUNDS * E + 1], F32, const_off + 2048 + 1024)
        total = sb("total", [128, E])
        lgT = at("lgT", [E, T], F32, const_off + 2048)
        most = sb("most", [128, 3])
        trips_f = sb("trips_f", [128, 3])
        trips_i = sb("trips_i", [128, 3], I32)
        left_f = sb("left_f", [128, ROUNDS * E])
        left_i = sb("left_i", [128, ROUNDS * E], I32)
        slot_c = sb("slot_c", [128, NT])
        gate_c = sb("gate_c", [128, NT])
        gslot = sb("gslot", [128, 2])
        x_wait = nc.dram_tensor("x_wait", (128, NT, D), F32, kind="Internal").ap()
        assert top[0] <= nc.sbuf_usable_end, top[0]

        ps = ctx.enter_context(nc.psum_tensor("ps", [128, 8 * BANK], F32))

        def bank(b, lo, hi):
            return ps[:, b * BANK + lo:b * BANK + hi]

        def pair(b):
            return ps[:, b * BANK:(b + 2) * BANK].rearrange("p (a n) -> p a n", a=2)[:, :, 0:HALF]

        raw_landed = [sem(f"raw_landed{s}") for s in range(RING)]
        wh_ready, wl_ready = sem("wh_ready"), sem("wl_ready")
        wl_first = sem("wl_first")
        sums_used = sem("sums_used")
        bank_full = [sem(f"bank_full{b}") for b in range(8)]
        bank_free = [sem(f"bank_free{b}") for b in range(8)]
        params_landed = sem("params_landed")
        cache_landed, stored = sem("cache_landed"), sem("stored")
        pool_const, pool_step = sem("pool_const"), sem("pool_step")
        cond_act, cond_ready = sem("cond_act"), sem("cond_ready")
        act_const = sem("act_const")
        dft_ready = sem("dft_ready")
        arow_ready, mod_ready, mul_ready = sem("arow_ready"), sem("mod_ready"), sem("mul_ready")
        ssq_ready, rstd_ready = sem("ssq_ready"), sem("rstd_ready")
        z_ready = sem("z_ready")
        nrm_c_ready = sem("nrm_c_ready")
        nrm_v_ready, nrm_h_ready, hn_ready = sem("nrm_v_ready"), sem("nrm_h_ready"), sem("hn_ready")
        q_out, k_out, f_out, v_out = sem("q_out"), sem("k_out"), sem("f_out"), sem("v_out")
        rope_ready = sem("rope_ready")
        nmax_ready, exp_ready, a_ready, aT_ready = sem("nmax_ready"), sem("exp_ready"), sem("a_ready"), sem("aT_ready")
        o_ready = sem("o_ready")
        sub_v_ready, sub_h_ready, mxa_ready = sem("sub_v_ready"), sem("sub_h_ready"), sem("mxa_ready")
        m12_ready = sem("m12_ready")
        zh_ready, zl_ready = sem("zh_ready"), sem("zl_ready")
        mf_h_ready, mf_ready = sem("mf_h_ready"), sem("mf_ready")
        y_ready, x_ready = sem("y_ready"), sem("x_ready")
        gcol_ready, gate_ready = sem("gcol_ready"), sem("gate_ready")
        lam_v = sem("lam_v")
        sg_ready, hv_ready, hid_h_ready, hid_ready = sem("sg_ready"), sem("hv_ready"), sem("hid_h_ready"), sem("hid_ready")
        acc_zero = sem("acc_zero")
        lgT_ready, gexp_ready = sem("lgT_ready"), sem("gexp_ready")
        ht_ready = sem("ht_ready")
        sel_ready, trips_ready, x_saved = sem("sel_ready"), sem("trips_ready"), sem("x_saved")
        x_here = [sem(f"x_here{t}") for t in range(NT)]
        pick_ready, pickT_ready, gslot_ready = sem("pick_ready"), sem("pickT_ready"), sem("gslot_ready")
        xg_act, xg_dve = sem("xg_act"), sem("xg_dve")
        esg_ready, ehv_ready, ehid_h_ready, ehid_ready = sem("esg_ready"), sem("ehv_ready"), sem("ehid_h_ready"), sem("ehid_ready")
        yh_ready, yl_ready = sem("yh_ready"), sem("yl_ready")
        dve_step = sem("dve_step")
        slot_ready = sem("slot_ready")

        fills = Fills()
        block = ctx.enter_context(nc.Block())


        vector_low = (0, 2, 4)

        def low_made(eng, n):
            if n in vector_low:
                eng.wait_ge(wl_first, n // 2 + 1)
            else:
                eng.wait_ge(wl_ready, n + 1)

        @block.tensor
        def _(pe):
            mm = nc.tensor.matmul

            def fill(key, b):
                before = fills.next(key, b)
                if not (isinstance(before, int) and before == 0):
                    pe.wait_ge(bank_free[b], before)

            def all_read():
                for b in range(8):
                    if fills.total[b]:
                        pe.wait_ge(bank_free[b], fills.total[b])

            def three(outs, w_of, x_of, sl, ks):
                for k in ks:
                    for hi, xs in ((wh, (hn_h, hn_l)), (wl, (hn_h,))):
                        for xp in xs:
                            for o, xc in zip(outs, x_of):
                                last = mm(o, w_of(hi[sl], k), xp[:, k, xc[0]:xc[1]],
                                          start=(k == 0 and hi is wh and xp is hn_h),
                                          stop=(k == KC - 1 and hi is wl))
                return last

            def ada(n, b=7):
                _, l, u = units[n]
                s = n % RING
                low_made(pe, n)
                fill(("ada_row", l, u), b)
                for k in range(KC):
                    for w in (wh, wl):
                        last = mm(ps[0:4, b * BANK:b * BANK + COLS], cond_p[:, k, :], w[s][:, k * COLS:(k + 1) * COLS],
                                  start=(k == 0 and w is wh), stop=(k == KC - 1 and w is wl))
                last.then_inc(bank_full[b], 1)

            def ada_turn(n, b=7):
                _, l, u = units[n]
                pe.wait_ge(arow_ready, l * 24 + u + 1)
                if b == 7:
                    fills.next(("ada_col", l, u), b)
                else:
                    fill(("ada_col", l, u), b)
                for j in range(2):
                    last = mm(bank(b, BANK - 4 + 2 * j, BANK - 2 + 2 * j), arow[:, j * 128:(j + 1) * 128], sel4,
                              start=True, stop=True)
                last.then_inc(bank_full[b], 1)

            def turn_norm(l, kind, product):
                all_read()
                m = 2 * l + (kind == "pre_f")

                def turn(c):
                    b = 4 + 2 * (c % 2)
                    fill(("turn", m, c), b)
                    for t in range(NT):
                        if c == 0:
                            pe.wait_ge(z_ready, NT * m + t + 1)
                        last = nc.tensor.transpose(bank(b, t * 128, (t + 1) * 128), z[:, t, c * 128:(c + 1) * 128], ident)
                    last.then_inc(bank_full[b], 1)

                turn(0)
                turn(1)
                for c in range(KC):
                    if c + 2 < KC:
                        turn(c + 2)
                    pe.wait_ge(hn_ready, KC * m + c + 1)
                    product(c)
                pe.wait_ge(bank_free[4], fills.total[4])
                pe.wait_ge(bank_free[6], fills.total[6])

            def first_products(n, keys):
                def product(k):
                    if k == 0:
                        pe.wait_ge(wl_ready, n + 1)
                        fill(keys[0], 0)
                        fill(keys[1], 2)
                    for j, b in ((0, 0), (1, 2)):
                        last = three([bank(b, 0, HALF), bank(b + 1, 0, HALF)],
                                     lambda w, kk, j=j: w[:, kk * COLS + j * 128:kk * COLS + j * 128 + 128],
                                     [(0, HALF), (HALF, T)], n % RING, [k])
                        if k == KC - 1:
                            last.then_inc(bank_full[b], 1)
                return product

            def router_products(k):
                if k == 0:
                    fill(("router",), 0)
                for w, xp in ((rt_h, hn_h), (rt_l, hn_h), (rt_h, hn_l)):
                    for j in range(2):
                        last = mm(bank(j, 0, HALF)[0:E], w[:, k, :], xp[:, k, j * HALF:(j + 1) * HALF],
                                  start=(k == 0 and w is rt_h and xp is hn_h), stop=(k == KC - 1 and xp is hn_l))
                if k == KC - 1:
                    last.then_inc(bank_full[0], 1)

            def proj_in(l):
                for u in range(1, 6):
                    n = unit_no["in", l, u]
                    pe.wait_ge(wl_ready, n + 1)
                    for j in range(2):
                        c = 2 * u + j
                        b = 2 * (c % 4)
                        fill(("in", l, c), b)
                        three([bank(b, 0, HALF), bank(b + 1, 0, HALF)],
                              lambda w, k, j=j: w[:, k * COLS + j * 128:k * COLS + j * 128 + 128],
                              [(0, HALF), (HALF, T)], n % RING, range(KC)).then_inc(bank_full[b], 1)
                all_read()
                for c in range(2 * H):
                    pe.wait_ge(q_out if c % 2 == 0 else k_out, H * l + c // 2 + 1)
                    fill(("rot", l, c), c)
                    mm(bank(c, 0, T_LAT), rot, (qT if c % 2 == 0 else kT)[:, c // 2, 0:T_LAT],
                       start=True, stop=True).then_inc(bank_full[c], 1)
                for u in range(6, 8):
                    n = unit_no["in", l, u]
                    pe.wait_ge(wl_ready, n + 1)
                    for t in range(NT):
                        b = (5 * (u - 6) + t) % 8
                        fill(("val", l, u - 6, t), b)
                        for k in range(KC):
                            for i, (xp, w) in enumerate(((hn_h, wh), (hn_h, wl), (hn_l, wh))):
                                last = mm(bank(b, 0, COLS), xp[:, k, t * 128:(t + 1) * 128],
                                          w[n % RING][:, k * COLS:(k + 1) * COLS],
                                          start=(k == 0 and i == 0), stop=(k == KC - 1 and i == 2))
                        last.then_inc(bank_full[b], 1)
                all_read()

            def attention(l):
                n = unit_no["in", l, 7] + 1
                pe.wait_ge(v_out, 2 * NT * (l + 1))
                pe.wait_ge(cache_landed, 32 * (l + 1))
                steps = [(h, t) for h in range(H) for t in range(NT)]
                turn = None

                def turn_probs(s):
                    no = 20 * l + s
                    tiles = 5 if s % NT < 4 else 1
                    pe.wait_ge(a_ready, no + 1)
                    fill(("aT", l, s), 4)
                    for i in range(tiles):
                        last = nc.tensor.transpose(bank(4, i * 128, (i + 1) * 128), probs[:, s % 2, 0, i * 128:(i + 1) * 128], ident)
                    last.then_inc(bank_full[4], 1)

                def values(s):
                    h, t = steps[s]
                    tiles = [0, 1, 2, 3, 5] if t < 4 else [4]
                    pe.wait_ge(aT_ready, 20 * l + s + 1)
                    fill(("o", l, s), 6)
                    for i, kt in enumerate(tiles):
                        last = mm(bank(6, 0, V), aT[:, s % 2, i * 128:(i + 1) * 128], vt[:, kt, h * V:(h + 1) * V],
                                  start=(i == 0), stop=(i == len(tiles) - 1))
                    last.then_inc(bank_full[6], 1)

                for s, (h, t) in enumerate(steps):
                    pe.wait_ge(rope_ready, 2 * H * l + 2 * h + 2)
                    fill(("score", l, s), 0)
                    for m in range(2):
                        q = qT[64 * m:64 * m + 64, h, t * 128:(t + 1) * 128]
                        if t < 4:
                            for j in range(2):
                                last = mm(bank(2 * m + j, 0, HALF), q, kT[64 * m:64 * m + 64, h, j * HALF:(j + 1) * HALF],
                                          start=True, stop=True)
                        else:
                            last = mm(bank(2 * m, 0, T_CTX), q, kT[64 * m:64 * m + 64, h, T:T + T_CTX],
                                      start=True, stop=True)
                    last.then_inc(bank_full[0], 1)
                    if s:
                        turn_probs(s - 1)
                    for a in range(ADA_STEPS[l][t]):
                        ada(n)
                        if turn is not None:
                            ada_turn(turn)
                        turn = n
                        n += 1
                        if s and a == 0:
                            values(s - 1)
                    if s and ADA_STEPS[l][t] == 0:
                        values(s - 1)
                if turn is not None:
                    ada_turn(turn)
                turn_probs(len(steps) - 1)
                values(len(steps) - 1)
                assert n == unit_no["cos", l, 0], (l, n, unit_no["cos", l, 0])
                all_read()

            def channel_transform(l):
                if l == 1:
                    pe.wait_ge(params_landed, 96)
                for i, m in enumerate((c128, s128)):
                    b = (0, 7)[i]
                    fill(("m12", l, i), b)
                    mm(bank(b, 0, 512), m, w_fn[:, :], start=True, stop=True).then_inc(bank_full[b], 1)

            def fourier(l):
                pe.wait_ge(m12_ready, 2 * (l + 1))
                for t in range(NT):
                    for g2 in range(2):
                        b = 2 + (2 * t + g2) % 6
                        fill(("z", l, t, g2), b)
                        for g in (2 * g2, 2 * g2 + 1):
                            last = mm(bank(b, 256 * (g % 2), 256 * (g % 2) + 256), fT[:, g, t * 128:(t + 1) * 128],
                                      m12[:, g, :, :].rearrange("p a e -> p (a e)"), start=True, stop=True)
                        last.then_inc(bank_full[b], 1)
                for i, name in enumerate(("cos", "sin")):
                    n = unit_no[name, l, 0]
                    pe.wait_ge(wl_ready, n + 1)
                    for g in range(G):
                        if i == 0:
                            fill(("mf", l, g), g)
                        for t in range(4):
                            if i == 0:
                                pe.wait_ge(zl_ready, 2 * NT * l + 2 * t + g // 2 + 1)
                            for j, (zz, w) in enumerate(((z_h, wh), (z_h, wl), (z_l, wh))):
                                last = mm(bank(g, 0, T_LAT), zz[:, t, g, i * 128:(i + 1) * 128],
                                          w[n % RING][:, t * 512:(t + 1) * 512],
                                          start=(i == 0 and t == 0 and j == 0), stop=(i == 1 and t == 3 and j == 2),
                                          skip_group_check=True)
                        if i == 1:
                            last.then_inc(bank_full[g], 1)
                        elif g == G - 1:
                            last.then_inc(sums_used, 1)
                    if i == 0:
                        gate_rows(2 * l)
                pe.wait_ge(zl_ready, 2 * NT * (l + 1))
                fill(("mfc", l), 4)
                for g in range(G):
                    for i in range(2):
                        for j, (zz, w) in enumerate(((z_h, dft_h), (z_h, dft_l), (z_l, dft_h))):
                            last = mm(bank(4, g * 128, (g + 1) * 128), zz[:, 4, g, i * 128:(i + 1) * 128],
                                      w[:, i * 128:(i + 1) * 128], start=(i == 0 and j == 0), stop=(i == 1 and j == 2))
                last.then_inc(bank_full[4], 1)
                pe.wait_ge(o_ready, 21 * (l + 1))
                for h in range(H):
                    b = (6, 0, 2, 4)[h]
                    pe.wait_ge(bank_free[b + 1], fills.total[b + 1])
                    fill(("sub", l, h), b)
                    for t in range(NT):
                        last = nc.tensor.transpose(bank(b, t * 128, (t + 1) * 128), o_norm[:, t, h * V:(h + 1) * V], ident)
                    last.then_inc(bank_full[b], 1)

            def gate_rows(g):
                pe.wait_ge(gcol_ready, g + 1)
                for cond in range(2):
                    for hf in range(2):
                        b = 4 + 2 * cond + hf
                        fill(("gate_bc", g, cond, hf), b)
                        for c in range(4):
                            last = mm(bank(b, c * 128, (c + 1) * 128), gcol[:, 4 * hf + c, cond:cond + 1].broadcast_to([128, 128]),
                                      ident, start=True, stop=True)
                        last.then_inc(bank_full[b], 1)

            def proj_out(l):
                pe.wait_ge(mf_ready, 2 * G * (l + 1))
                for hf in range(2):
                    for kh in range(2):
                        n = unit_no["out", l, 2 * hf + kh]
                        pe.wait_ge(wl_ready, n + 1)
                        if kh == 1:
                            pe.wait_ge(mxa_ready, H * (l + 1))
                        for t in range(NT):
                            b = (5 * hf + t) % 8
                            if kh == 0:
                                fill(("mix", l, hf, t), b)
                            for k in range(4):
                                for j, (xp, w) in enumerate(((mx_h, wh), (mx_h, wl), (mx_l, wh))):
                                    last = mm(bank(b, 0, 512), xp[:, 4 * (1 - kh) + k, t * 128:(t + 1) * 128],
                                              w[n % RING][:, k * 512:(k + 1) * 512],
                                              start=(kh == 0 and k == 0 and j == 0), stop=(kh == 1 and k == 3 and j == 2),
                                              skip_group_check=True)
                            if kh == 1:
                                last.then_inc(bank_full[b], 1)
                            elif t == NT - 1:
                                last.then_inc(sums_used, 1)

            def hidden(l, key, n0, i, slots, k):
                for part, name in enumerate(("gate", "up")):
                    if key[0] == "first" and part == 0:
                        continue
                    pe.wait_ge(wl_ready, n0 + part + 1 + i * k)
                    for j in range(2):
                        b = 2 * j
                        fill((key, name, j), b)
                        three([bank(b, 0, HALF), bank(b + 1, 0, HALF)],
                              lambda w, kk, j=j: w[:, kk * COLS + j * 128:kk * COLS + j * 128 + 128],
                              [(0, HALF), (HALF, T)], slots[part], range(KC)).then_inc(bank_full[b], 1)

            def down(l, key, n, i, slot, k):
                pe.wait_ge(wl_ready, n + 1 + i * k)
                pe.wait_ge(hid_ready, 2 + (i * 2 if k else 2 * (N_BLK - 1)))
                for t in range(NT):
                    for hf in range(2):
                        r = 2 * t + hf
                        b = 4 + r % 4
                        fill((key, "down", r), b)
                        for f in range(2):
                            for j, (xp, w) in enumerate(((hid_h, wh), (hid_h, wl), (hid_l, wh))):
                                last = mm(bank(b, 0, 512), xp[:, f, t * 128:(t + 1) * 128],
                                          w[slot][:, f * D + hf * 512:f * D + hf * 512 + 512],
                                          start=(f == 0 and j == 0), stop=(f == 1 and j == 2))
                        last.then_inc(bank_full[b], 1)

            def dense():
                l, nb = 0, N_BLK
                gate_rows(1)
                n0 = unit_no["gate", l, 0]
                hidden(l, ("first", l), n0, 0, [n0 % RING, (n0 + 1) % RING], 0)
                with pe.Fori(0, nb - 1) as i:
                    fills.enter(i, {0: 2, 2: 2, 4: 3, 5: 3, 6: 2, 7: 2})
                    hidden(l, ("body", l), n0 + 2, i, [(n0 + 2) % RING, n0 % RING], 3)
                    down(l, ("body", l), n0 + 4, i, (n0 + 1) % RING, 3)
                    fills.leave(nb - 1)
                n = unit_no["down", l, nb - 1]
                down(l, ("last", l), n, 0, n % RING, 0)

            def gather(key, chunks):
                for c in chunks:
                    b = c % 4
                    fill((key, "xg", c), b)
                    for i, src in enumerate((ht_h, ht_l)):
                        for t in range(NT):
                            last = mm(bank(b, i * SLOTS, (i + 1) * SLOTS), src[:, t, c * 128:(c + 1) * 128], pick[:, t, :],
                                      start=(t == 0), stop=(t == NT - 1))
                    last.then_inc(bank_full[b], 1)

            def experts():
                def turn_back(t):
                    for i, src in enumerate((hn_h, hn_l)):
                        b = 2 + 2 * ((2 * t + i) % 3)
                        fill(("ht", i, t), b)
                        for c in range(KC):
                            last = nc.tensor.transpose(bank(b, c * 128, (c + 1) * 128),
                                                       src[:, c, t * 128:(t + 1) * 128].bitcast(F32), ident)
                        last.then_inc(bank_full[b], 1)

                pe.wait_ge(lgT_ready, 1)
                fill(("logits",), 0)
                for t in range(NT):
                    last = nc.tensor.transpose(bank(0, t * E, (t + 1) * E), lgT[0:E, t * 128:(t + 1) * 128], ident[0:E, 0:E])
                last.then_inc(bank_full[0], 1)
                for i in range(NT):
                    turn_back(i)
                all_read()
                gate_rows(3)
                pe.wait_ge(sel_ready, 1)
                fill(("pos",), 0)
                mm(bank(0, 0, NT * E), tri, sel[:, :, :].rearrange("p t e -> p (t e)"), start=True, stop=False)
                mm(bank(0, 0, NT * E), ones[:, :], csel[:, :, :].rearrange("p t e -> p (t e)"), start=False, stop=True)
                mm(bank(0, NT * E, (NT + 1) * E), ones[:, :], tsel[:, :], start=True, stop=True).then_inc(bank_full[0], 1)
                pe.wait_ge(ht_ready, 2 * NT)
                pe.wait_ge(pick_ready, 1)
                gather("ahead", range(KC))

                def turn_hidden(i, q, tiles):
                    pe.wait_ge(ehv_ready, q + 1 + i * EXP_BLK)
                    b = 2 * (q % 2)
                    fill(("hidden", q), b)
                    for f in range(2):
                        for st in range(tiles):
                            last = nc.tensor.transpose(bank(b, f * SLOTS + st * 128, f * SLOTS + (st + 1) * 128),
                                                       esg[:, st, f * 128:(f + 1) * 128], ident)
                    last.then_inc(bank_full[b], 1)

                def turn(i, tiles):
                    pe.wait_ge(xg_act, 4 + i * 4)
                    pe.wait_ge(xg_dve, 4 + i * 4)
                    for j, (kind, q) in enumerate(EXP_UNITS):
                        w_h, w_l = wh[(N_STATIC + j) % RING], wl[(N_STATIC + j) % RING]
                        pe.wait_ge(wl_ready, N_STATIC + j + 1 + i * N_EU)
                        if kind != "down":
                            b = 2 * (q % 2) + (kind == "up")
                            fill(("exp", kind, q), b)
                            for st in range(tiles):
                                for k in range(KC):
                                    for p, (w, part) in enumerate(((w_h, 0), (w_l, 0), (w_h, 1))):
                                        last = mm(bank(b, st * COLS, (st + 1) * COLS), xg[:, k, part, st * 128:(st + 1) * 128],
                                                  w[:, k * COLS:(k + 1) * COLS],
                                                  start=(k == 0 and p == 0), stop=(k == KC - 1 and p == 2))
                            last.then_inc(bank_full[b], 1)
                        else:
                            pe.wait_ge(ehid_ready, q + 1 + i * EXP_BLK)
                            for st in range(tiles):
                                for hf in range(2):
                                    b = 4 + 2 * st + hf
                                    if q == 0:
                                        fill(("y", st, hf), b)
                                    for f in range(2):
                                        for p, (xp, w) in enumerate(((ehid_h, w_h), (ehid_h, w_l), (ehid_l, w_h))):
                                            last = mm(bank(b, 0, 512), xp[:, f, st * 128:(st + 1) * 128],
                                                      w[:, f * D + hf * 512:f * D + hf * 512 + 512],
                                                      start=(q == 0 and f == 0 and p == 0),
                                                      stop=(q == EXP_BLK - 1 and f == 1 and p == 2), skip_group_check=True)
                                    if q == EXP_BLK - 1:
                                        last.then_inc(bank_full[b], 1)
                            if q < EXP_BLK - 1:
                                last.then_inc(sums_used, 1)
                            elif tiles == 1:
                                for hf in range(2):
                                    fill(("y", 1, hf), 6 + hf)
                                    pe.nop().then_inc(bank_full[6 + hf], 1)
                        if (kind, q) in (("gate", 1), ("gate", 2), ("gate", 3)):
                            turn_hidden(i, q - 1, tiles)
                        if (kind, q) == ("down", EXP_BLK - 2):
                            turn_hidden(i, EXP_BLK - 1, tiles)
                        if j == 1:
                            for st, b in ((0, 2), (1, 3)):
                                fill(("pickT", st), b)
                                for t in range(4):
                                    last = nc.tensor.transpose(bank(b, t * 128, (t + 1) * 128),
                                                               pick[:, t, st * 128:(st + 1) * 128].bitcast(F32), ident)
                                last.then_inc(bank_full[b], 1)
                            fill(("pickT", 2), 4)
                            for st in range(2):
                                last = nc.tensor.transpose(bank(4, st * 128, (st + 1) * 128),
                                                           pick[:, 4, st * 128:(st + 1) * 128].bitcast(F32), ident)
                            last.then_inc(bank_full[4], 1)
                            fill(("gslot",), 5)
                            for st in range(2):
                                for t in range(NT):
                                    last = mm(bank(5, st, st + 1), pick[:, t, st * 128:(st + 1) * 128].bitcast(F32),
                                              gate_c[:, t:t + 1], start=(t == 0), stop=(t == NT - 1))
                            last.then_inc(bank_full[5], 1)
                        if (kind, q) == ("down", EXP_BLK - 2):
                            pe.wait_ge(pick_ready, 2 + i)
                            gather("next", range(0, KC // 2))
                    gather("next", range(KC // 2, KC))
                    pe.wait_ge(pickT_ready, 3 + i * 3)
                    pe.wait_ge(yl_ready, 4 + i * 4)
                    for r in range(2 * NT):
                        t, hf = divmod(r, 2)
                        fill(("scatter", r), r % 4)
                        for st in range(tiles):
                            for p, yy in enumerate((y_h[:, st, :], y_l[st][:, :])):
                                last = mm(bank(r % 4, 0, 512), pickT[:, st, t * 128:(t + 1) * 128],
                                          yy[:, hf * 512:(hf + 1) * 512],
                                          start=(st == 0 and p == 0), stop=(st == tiles - 1 and p == 1))
                        last.then_inc(bank_full[r % 4], 1)

                pe.wait_ge(trips_ready, 1)
                trips = pe.value_load(trips_i[0:1, 0:1], min_val=E, max_val=ROUNDS * E)
                with pe.Fori(0, trips) as i:
                    fills.enter(i, {0: 9, 1: 7, 2: 9, 3: 7, 4: 2, 5: 2, 6: 1, 7: 1})
                    left = pe.value_load(left_i[0:1, bass.ds(i, 1)], min_val=-T, max_val=T)
                    before = list(fills.total)
                    with pe.If(left > 128):
                        turn(i, 2)
                    with pe.Else():
                        fills.total = list(before)
                        turn(i, 1)
                    fills.leave(1)

            pe.wait_ge(params_landed, 80)
            pe.wait_ge(pool_const, 2)
            fill(("lam",), 0)
            pe.wait_ge(lam_v, 1)
            mm(bank(0, 0, 2 * L), ones[0:64, :], lam2[:, :, :].rearrange("p l a -> p (l a)"),
               start=True, stop=True).then_inc(bank_full[0], 1)
            pe.wait_ge(cond_ready, 1)
            pe.wait_ge(dft_ready, 1)
            for u in range(FIRST):
                ada(u, 6 + u % 2)
                if u:
                    ada_turn(u - 1, 5)
            ada_turn(FIRST - 1, 5)
            for l in range(L):
                turn_norm(l, "pre_a", first_products(unit_no["in", l, 0], [("in", l, 0), ("in", l, 1)]))
                proj_in(l)
                channel_transform(l)
                attention(l)
                fourier(l)
                proj_out(l)
                first = first_products(unit_no["gate", 0, 0], [(("first", 0), "gate", j) for j in range(2)])
                turn_norm(l, "pre_f", first if l == 0 else router_products)
                (dense, experts)[l]()

        def full(eng, key, i=0, back=0):
            b, first, k = fills.named[key]
            first -= back * k
            eng.wait_ge(bank_full[b], first + i * k if k else first)

        def multiplied(eng, n):
            kind, l, u = units[n]
            nb = N_BLK
            if kind == "cos" or (kind == "out" and u % 2 == 0):
                eng.wait_ge(sums_used, 3 * l + {"cos": 1, "out": 2 + u // 2}[kind])
            elif kind == "ada":
                full(eng, ("ada_row", l, u))
            elif kind == "in":
                full(eng, ("in", l, 2 * u + 1) if u < 6 else ("val", l, u - 6, NT - 1))
            elif kind == "sin":
                full(eng, ("mf", l, G - 1))
            elif kind == "out":
                full(eng, ("mix", l, u // 2, NT - 1))
            elif kind == "down":
                full(eng, (("body", l) if u < nb - 1 else ("last", l), "down", 2 * NT - 1), u)
            else:
                full(eng, (("body", l) if u else ("first", l), kind, 1), u - 1)

        def free(ins, key):
            ins.then_inc(bank_free[fills.named[key][0]], 1)

        @block.sync
        def _(sp):
            sp.dma_start(consts[:, :], dram["consts"]).then_inc(params_landed, 16)
            sp.dma_start(vcol[:, :, :], dram["vcol"]).then_inc(params_landed, 16)
            sp.dma_start(lamt[:, :, :], dram["lam"]).then_inc(params_landed, 16)
            sp.dma_start(w_rt[:, :, :], dram["w_router"]).then_inc(params_landed, 16)
            sp.dma_start(w_fn[:, :], dram["w_fnet"][0]).then_inc(params_landed, 16)

            def unit(n, i=0, k=0, slot=None):
                s = n % RING
                if k:
                    sp.wait_ge(wl_ready, n - RING + 1 + i * k)
                elif n >= RING:
                    low_made(sp, n - RING)
                src = dram["stream"][n] if not k else dram["stream"][bass.ds(n + i * k, 1)].rearrange("a p n -> p (a n)")
                sp.dma_start(raw[s][:, :], src).then_inc(raw_landed[s], 16)

            def expert(e, turn):
                for j in range(N_EU):
                    m = N_STATIC + j
                    sp.wait_ge(wl_ready, m - RING + 1 + turn * N_EU)
                    sp.dma_start(raw[m % RING][:, :], dram["stream"][bass.ds(m + e * N_EU, 1)].rearrange("a p n -> p (a n)")).then_inc(raw_landed[m % RING], 16)

            n = 0
            while n < FIRST:
                unit(n)
                n += 1
                if n > 3:
                    sp.dma_start(x[:, n - 4, :], dram["x"][:, n - 4, :]).then_inc(x_here[n - 4], 16)
            for l in range(L):
                first = unit_no["in", l, 0]
                while n < first + RING + 1:
                    unit(n)
                    n += 1
                multiplied(sp, first)
                sp.dma_start(kT[:, :, T_LAT:T], dram["cache_k"][l]).then_inc(cache_landed, 16)
                sp.dma_start(vt[:, NT, :], dram["cache_v"][l]).then_inc(cache_landed, 16)
                if l == 1:
                    sp.wait_ge(x_ready, 2 * NT)
                    sp.dma_start(w_fn[:, :], dram["w_fnet"][1]).then_inc(params_landed, 16)
                ready = unit_no["in", l, 7] + 1
                while n < ready + RING:
                    unit(n)
                    n += 1
                sp.wait_ge(k_out, H * (l + 1))
                sp.wait_ge(v_out, 2 * NT * (l + 1))
                sp.dma_start(out["new_k"][l], kT[:, :, T:T + T_CTX]).then_inc(stored, 16)
                sp.dma_start(out["new_v"][l], vt[:, 4, :]).then_inc(stored, 16)
                if l == 1:
                    break
                body = unit_no["gate", l, 0] + 2 + RING
                while n < body:
                    unit(n)
                    n += 1
                last = unit_no["down", l, N_BLK - 1]
                trips = (last - n) // RING
                with sp.Fori(0, trips) as i:
                    for j in range(RING):
                        unit(n + j, i, RING)
                n += trips * RING
                while n <= last:
                    unit(n)
                    n += 1
            while n < N_STATIC:
                unit(n)
                n += 1
            with sp.Fori(0, E) as e:
                expert(e, e)
            sp.wait_ge(trips_ready, 1)
            rounds = sp.value_load(trips_i[0:1, 1:2], min_val=1, max_val=ROUNDS)
            with sp.If(rounds > 1):
                with sp.Fori(1, rounds) as r:
                    with sp.Fori(0, E) as e:
                        expert(e, r * E + e)
            sp.wait_ge(y_ready, 4 * NT)
            for t in range(NT):
                sp.dma_start(x[:, t, :], x_wait[:, t, :]).then_inc(x_here[t], 16)
            for t in range(NT):
                sp.wait_ge(x_ready, NT * 3 + t + 1)
                sp.dma_start(out["y"][:, t, :], x[:, t, :]).then_inc(stored, 16)
            sp.wait_ge(stored, 16 * (2 * L + NT))

        @block.gpsimd
        def _(pool):
            nc.gpsimd.memset(ones[:, :], 1.0).then_inc(pool_const, 1)
            nc.gpsimd.memset(mhalf[:, :], -0.5).then_inc(pool_const, 1)
            pool.wait_ge(pool_const, 2)
            steps = [0]

            def split(n, i=0, k=0, count=1):
                s = n % RING
                pool.wait_ge(wh_ready, n + 1 + i * k)
                nc.gpsimd.tensor_tensor(wl[s][:, :], raw[s][:, :], wh[s][:, :].bitcast(F32), ALU.subtract).then_inc(wl_ready, count)

            def rsqrt(l, kind, width, no, count=1):
                c = stat_col(l, kind, no)
                pool.wait_ge(ssq_ready, stat_no(l, kind, no))
                nc.gpsimd.tensor_scalar(msq[:, c:c + count], ssq[:, c:c + count], 1.0 / width, EPS, ALU.mult, ALU.add).then_inc(pool_step, 1)
                steps[0] += 1
                pool.wait_ge(pool_step, steps[0])
                nc.gpsimd.tensor_tensor(rstd[:, c:c + count], msq[:, c:c + count], mhalf[:, 0:count], ALU.pow).then_inc(rstd_ready, 1)

            def two_norms(first, second):
                for t in range(NT + 1):
                    if t < NT:
                        rsqrt(*first, D, t)
                    if t:
                        rsqrt(*second, D, t - 1)

            n = 0

            def upto(n1):
                nonlocal n
                while n < n1:
                    split(n)
                    n += 1

            for l in range(L):
                if l == 0:
                    for n in range(1, FIRST):
                        if n not in vector_low:
                            split(n, count=1 + (n - 1 in vector_low))
                    for t in range(NT):
                        rsqrt(0, "pre_a", D, t)
                    n = FIRST
                upto(unit_no["cos", l, 0] + 2)
                rsqrt(l, "sub", V, 0, 20)
                upto(min(unit_no["gate", l, 0] + 1, N_STATIC))
                two_norms((l, "post_a"), (l, "pre_f"))
                if l == 0:
                    upto(unit_no["gate", l, 0] + 2)
                    full(pool, ("turn", 1, KC - 1))
                    nc.gpsimd.memset(acc[:, :, :], 0.0).then_inc(acc_zero, 1)
                if l == 0:
                    last = unit_no["down", l, N_BLK - 1]
                    trips = (last + 1 - n) // RING
                    with pool.Fori(0, trips) as i:
                        for j in range(RING):
                            split(n + j, i, RING)
                    n += trips * RING
                    upto(last + 2)
                else:
                    for j in range(RING):
                        split(n + j)
                    full(pool, ("ht", 1, NT - 1))
                    nc.gpsimd.memset(eacc[:, :, :], 0.0).then_inc(acc_zero, 1)
                    pool.wait_ge(trips_ready, 1)
                    last = pool.value_load(trips_i[0:1, 2:3], min_val=E - 1, max_val=ROUNDS * E - 1)
                    with pool.Fori(0, last) as i:
                        for j in range(RING, N_EU + RING):
                            split(n + j, i, N_EU)
                    for j in range(RING, N_EU):
                        split(n + j, last, N_EU)
                if l + 1 < L:
                    two_norms((l, "post_f"), (l + 1, "pre_a"))
                else:
                    for t in range(NT):
                        rsqrt(l, "post_f", D, t)

        @block.scalar
        def _(act):
            def split(n, i=0, k=0):
                s = n % RING
                act.wait_ge(raw_landed[s], 16 * (n // RING + 1) + i * (16 * (k // RING)))
                if not k and n >= RING:
                    multiplied(act, n - RING)
                nc.scalar.copy(wh[s][:, :], raw[s][:, :]).then_inc(wh_ready, 1)

            def square(l, kind, src, t, to):
                c = stat_col(l, kind, t)
                nc.scalar.activation(to[:, t, :], src[:, t, :], ACT.Square, accum_out=ssq[:, c:c + 1]).then_inc(ssq_ready, 1)

            def normalise(l, kind, t):
                act.wait_ge(rstd_ready, stat_no(l, kind, t))
                c = stat_col(l, kind, t)
                nc.scalar.activation(z[:, t, :], x[:, t, :], ACT.Copy, scale=rstd[:, c:c + 1]).then_inc(z_ready, 1)

            def two_norms(first, second, to):
                r = 2 * first[0] + (first[1] == "post_f")
                for t in range(NT + 2):
                    if t < NT:
                        act.wait_ge(y_ready, NT * r + t + 1)
                        square(*first, acc, t, to)
                    if t >= 2:
                        normalise(*second, t - 2)
                    if 1 <= t <= NT:
                        act.wait_ge(x_ready, NT * r + t)
                        square(*second, x, t - 1, to)

            def norm_high(l, kind):
                m = 2 * l + (kind == "pre_f")
                sh = SH_A if kind == "pre_a" else SH_F
                act.wait_ge(mul_ready, m + 1)
                for c in range(KC):
                    b = fills.named["turn", m, c][0]
                    full(act, ("turn", m, c))
                    if c >= 2:
                        act.wait_ge(hn_ready, KC * m + c - 1)
                    nc.scalar.activation(nrm_v[:, c % 2, 0:T_LAT], bank(b, 0, T_LAT), ACT.Identity,
                                         bias=modc[:, l, sh * KC + c, 0:1], scale=mulc[:, m, c, 0:1]).then_inc(nrm_v_ready, 1)
                    act.wait_ge(nrm_v_ready, KC * m + c + 1)
                    act.wait_ge(nrm_c_ready, KC * m + c + 1)
                    nc.scalar.copy(hn_h[:, c, :], nrm_v[:, c % 2, :]).then_inc(nrm_h_ready, 1)
                    act.nop().then_inc(bank_free[b], 1)

            n = 0

            def ahead(stage):
                nonlocal n
                while n < min(stage + RING, N_STATIC):
                    split(n)
                    n += 1

            act.wait_ge(params_landed, 80)
            cs = cond_s[:, :, :]
            vc = vcol[:, 0, V_C:V_C + 16].rearrange("p (a c) -> p c a", a=2)
            nc.scalar.activation(cs, vc, ACT.Silu).then_inc(cond_act, 1)
            act.wait_ge(cond_act, 1)
            nc.scalar.copy(cond_p[:, :, 0:2], cs).then_inc(cond_act, 1)
            nc.scalar.copy(dft_h[:, :], consts[:, 256:512]).then_inc(act_const, 1)
            nc.scalar.copy(rt_h[:, :, :], w_rt[:, :, :]).then_inc(act_const, 1)
            full(act, ("lam",))
            free(nc.scalar.activation(lame[:, :, :].rearrange("p l a -> p (l a)"), bank(0, 0, 2 * L), ACT.Exp), ("lam",))
            for u in range(FIRST):
                ahead(u)
                if u > 2:
                    act.wait_ge(x_here[u - 3], 16)
                    square(0, "pre_a", x, u - 3, junk)
            for t in range(NT):
                normalise(0, "pre_a", t)
            for l in range(L):
                n_in = unit_no["in", l, 0]
                norm_high(l, "pre_a")
                for u in range(6):
                    ahead(n_in + u)
                    for j in range(2):
                        c = 2 * u + j
                        if c < 4:
                            full(act, ("in", l, c))
                            nc.scalar.copy(qT[:, c, :].rearrange("p (a n) -> p a n", a=2), pair(2 * (c % 4))).then_inc(q_out, 1)
                            act.wait_ge(q_out, H * l + c + 1)
                            act.nop().then_inc(bank_free[2 * (c % 4)], 1)
                        if c >= 8:
                            full(act, ("in", l, c))
                            nc.scalar.copy(fT[:, c - 8, :].rearrange("p (a n) -> p a n", a=2), pair(2 * (c % 4))).then_inc(f_out, 1)
                            act.wait_ge(f_out, G * l + c - 8 + 1)
                            act.nop().then_inc(bank_free[2 * (c % 4)], 1)
                for u in range(6, 8):
                    ahead(n_in + u)
                nu = n_in + 8

                def turned(s):
                    full(act, ("aT", l, s))
                    w = T if s % NT < 4 else 128
                    nc.scalar.copy(aT[:, s % 2, 0:w], bank(4, 0, w)).then_inc(aT_ready, 1)
                    act.wait_ge(aT_ready, 20 * l + s + 1)
                    act.nop().then_inc(bank_free[4], 1)

                for s in range(H * NT):
                    t = s % NT
                    if s:
                        turned(s - 1)
                    act.wait_ge(nmax_ready, 20 * l + s + 1)
                    for m in range(2):
                        src = pair(2 * m) if t < 4 else bank(2 * m, 0, T_CTX)
                        dst = probs[:, s % 2, m, 0:T].rearrange("p (a n) -> p a n", a=2) if t < 4 else probs[:, s % 2, m, 0:T_CTX]
                        if s >= 2 and m == 0:
                            full(act, ("aT", l, s - 2))
                        nc.scalar.activation(dst, src, ACT.Exp, bias=nmx[:, m:m + 1], scale=SCALE,
                                             accum_out=ssum[:, m:m + 1]).then_inc(exp_ready, 1)
                    act.wait_ge(exp_ready, 40 * l + 2 * s + 2)
                    act.nop().then_inc(bank_free[0], 1)
                    for _ in range(ADA_STEPS[l][t]):
                        ahead(nu)
                        nu += 1
                turned(H * NT - 1)
                for t in range(NT):
                    for g2 in range(2):
                        full(act, ("z", l, t, g2))
                        nc.scalar.copy(z_h[:, t, 2 * g2:2 * g2 + 2, :], bank(2 + (2 * t + g2) % 6, 0, 512).rearrange("p (g e) -> p g e", g=2)).then_inc(zh_ready, 1)
                ahead(unit_no["cos", l, 0])
                ahead(unit_no["sin", l, 0])
                act.wait_ge(o_ready, 21 * (l + 1))
                for g in range(G):
                    full(act, ("mf", l, g))
                    nc.scalar.copy(mx_h[:, 4 + g, 0:T_LAT], bank(g, 0, T_LAT)).then_inc(mf_h_ready, 1)
                full(act, ("mfc", l))
                nc.scalar.copy(mx_h[:, 4:8, T_LAT:T], bank(4, 0, 512).rearrange("p (g n) -> p g n", g=4)).then_inc(mf_h_ready, 1)
                for h in range(H):
                    act.wait_ge(sub_v_ready, H * l + h + 1)
                    nc.scalar.copy(mx_h[:, h, :], sub_v[:, h % 2, :]).then_inc(sub_h_ready, 1)
                for u in range(4):
                    ahead(unit_no["out", l, u])
                two_norms((l, "post_a"), (l, "pre_f"), junk2)
                norm_high(l, "pre_f")
                nb = N_BLK
                if l == 1:
                    break

                def silu(key, i):
                    for j in range(2):
                        full(act, (key, "gate", j), i)
                        nc.scalar.activation(sg[:, j, :].rearrange("p (a n) -> p a n", a=2), pair(2 * j), ACT.Silu).then_inc(sg_ready, 1)

                def high(i, k):
                    for j in range(2):
                        act.wait_ge(hv_ready, j + 1 + (i * 2 + 2 if k else 0))
                        nc.scalar.copy(hid_h[:, j, :], sg[:, j, :]).then_inc(hid_h_ready, 1)

                n0 = unit_no["gate", l, 0]
                ahead(n0)
                silu(("first", l), 0)
                act.wait_ge(sg_ready, 2)
                act.nop().then_inc(bank_free[0], 1)
                act.nop().then_inc(bank_free[2], 1)
                high(0, 0)
                nn = n
                assert nn == n0 + 3
                with act.Fori(0, nb - 1) as i:
                    full(act, (("body", l), "up", 1), i, 1)
                    split(nn, i, RING)
                    act.wait_ge(hid_ready, 2 + i * 2)
                    silu(("body", l), i)
                    act.wait_ge(sg_ready, 4 + i * 2)
                    act.nop().then_inc(bank_free[0], 1)
                    act.nop().then_inc(bank_free[2], 1)
                    full(act, (("body", l), "down", 2 * NT - 1), i, 1)
                    split(nn + 1, i, RING)
                    split(nn + 2, i, RING)
                    full(act, (("body", l), "down", 2 * NT - 1), i)
                    high(i, 1)
                n = nn + RING * (nb - 1)
                assert n == unit_no["down", l, nb - 1] + 1
                ahead(n - 1)
                multiplied(act, unit_no["up", l, nb - 1])
                two_norms((l, "post_f"), (l + 1, "pre_a"), junk)

            act.wait_ge(x_ready, 3 * NT)
            act.dma_start(x_wait, x[:, :, :]).then_inc(x_saved, 16)
            def exp_split(j, i):
                m = N_STATIC + j
                act.wait_ge(raw_landed[m % RING], 16 * (m // RING + 1) + i * (16 * N_EU // RING))
                nc.scalar.copy(wh[m % RING][:, :], raw[m % RING][:, :]).then_inc(wh_ready, 1)

            for j in range(RING):
                exp_split(j, 0)
            for t in range(NT):
                for i, ht in enumerate((ht_h, ht_l)):
                    full(act, ("ht", i, t))
                    b = fills.named["ht", i, t][0]
                    nc.scalar.copy(ht[:, t, :], ps[:, b * BANK:b * BANK + D]).then_inc(ht_ready, 1)
                    act.wait_ge(ht_ready, 2 * t + i + 1)
                    act.nop().then_inc(bank_free[b], 1)
                if t == 2:
                    act.wait_ge(gexp_ready, 1)
                    nc.scalar.activation(gexp[:, :], gdif[:, :], ACT.Exp).then_inc(gexp_ready, 1)

            def picked(key, chunks, i):
                for c in chunks:
                    if c % 2 == 0:
                        full(act, (key, "xg", c), i)
                        base = 4 if key == "next" else 0
                        nc.scalar.copy(xg[:, c, :, :].rearrange("p a n -> p (a n)"), bank(c % 4, 0, 2 * SLOTS)).then_inc(xg_act, 1)
                        act.wait_ge(xg_act, base + c // 2 + 1 + i * 4)
                        act.nop().then_inc(bank_free[c % 4], 1)

            picked("ahead", range(KC), 0)
            act.wait_ge(x_saved, 16)
            act.wait_ge(trips_ready, 1)
            last = act.value_load(trips_i[0:1, 2:3], min_val=E - 1, max_val=ROUNDS * E - 1)

            sums = 3 * L
            def turn(i, more):
                for q in range(EXP_BLK):
                    full(act, ("exp", "gate", q), i)
                    if q:
                        full(act, ("hidden", q - 1), i)
                    nc.scalar.activation(esg[:, :, :].rearrange("p a n -> p (a n)"), bank(2 * (q % 2), 0, 2 * SLOTS), ACT.Silu).then_inc(esg_ready, 1)
                    act.wait_ge(esg_ready, q + 1 + i * EXP_BLK)
                    act.nop().then_inc(bank_free[2 * (q % 2)], 1)
                    exp_split((3, 5, 8, 11)[q], i)
                    if q < EXP_BLK - 1 or more:
                        full(act, ("exp", "up", q), i)
                        exp_split((4, 6, 9, N_EU)[q], i)
                    if q:
                        act.wait_ge(sums_used, sums + q + i * (EXP_BLK - 1))
                    if 0 < q < EXP_BLK - 1:
                        exp_split((None, 7, 10)[q], i)
                    full(act, ("hidden", q), i)
                    nc.scalar.copy(ehid_h[:, :, :].rearrange("p a n -> p (a n)"), bank(2 * (q % 2), 0, 2 * SLOTS)).then_inc(ehid_h_ready, 1)
                if more:
                    exp_split(N_EU + 1, i)
                picked("next", range(0, KC // 2), i)
                act.wait_ge(gslot_ready, 1 + i)
                for st in range(2):
                    for hf in range(2):
                        full(act, ("y", st, hf), i)
                        nc.scalar.activation(y_h[:, st, hf * 512:(hf + 1) * 512], bank(4 + 2 * st + hf, 0, 512), ACT.Copy,
                                             scale=gslot[:, st:st + 1]).then_inc(yh_ready, 1)
                if more:
                    exp_split(N_EU + 2, i)
                picked("next", range(KC // 2, KC), i)

            with act.Fori(0, last) as i:
                turn(i, True)
            turn(last, False)
            act.wait_ge(y_ready, 4 * NT)
            for t in range(NT):
                c = stat_col(1, "post_f", t)
                nc.scalar.activation(junk2[:, t, :], eacc[:, t, :], ACT.Square, accum_out=ssq[:, c:c + 1]).then_inc(ssq_ready, 1)

        @block.vector
        def _(dve):
            v = nc.vector
            chain = [0]

            def link(ins):
                chain[0] += 1
                ins.then_inc(dve_step, 1)
                dve.wait_ge(dve_step, chain[0])

            def ada_row(l, u):
                full(dve, ("ada_row", l, u))
                b = fills.named["ada_row", l, u][0]
                v.tensor_copy(arow[:, :], ps[0:4, b * BANK:b * BANK + COLS]).then_inc(arow_ready, 1)
                dve.wait_ge(arow_ready, 24 * l + u + 1)
                dve.nop().then_inc(bank_free[b], 1)

            def ada_col(l, u):
                full(dve, ("ada_col", l, u))
                b = fills.named["ada_col", l, u][0]
                v.tensor_tensor(modc[:, l, 2 * u:2 * u + 2, :], bank(b, BANK - 4, BANK).rearrange("p (j a) -> p j a", j=2),
                                vcol[:, l, V_BADA + 2 * u:V_BADA + 2 * u + 2].unsqueeze(2).broadcast_to([128, 2, 2]),
                                ALU.add).then_inc(mod_ready, 1)
                dve.wait_ge(mod_ready, 24 * l + u + 1)
                dve.nop().then_inc(bank_free[b], 1)

            def modulation(l, kind):
                m = 2 * l + (kind == "pre_f")
                sc, vg = (SC_A, V_GAPRE) if kind == "pre_a" else (SC_F, V_GFPRE)
                link(v.tensor_scalar(mulc[:, m, :, :], modc[:, l, sc * KC:(sc + 1) * KC, :], 1.0, None, ALU.add))
                v.tensor_tensor(mulc[:, m, :, :], mulc[:, m, :, :],
                                vcol[:, l, vg:vg + KC].unsqueeze(2).broadcast_to([128, KC, 2]), ALU.mult).then_inc(mul_ready, 1)

            def norm_low(l, kind):
                m = 2 * l + (kind == "pre_f")
                sh = SH_A if kind == "pre_a" else SH_F
                dve.wait_ge(mul_ready, m + 1)

                def context(c):
                    full(dve, ("turn", m, c))
                    if c >= 2:
                        dve.wait_ge(hn_ready, KC * m + c - 1)
                    b = fills.named["turn", m, c][0]
                    v.tensor_scalar(nrm_v[:, c % 2, T_LAT:T], bank(b + 1, 0, T_CTX), mulc[:, m, c, 1:2],
                                    modc[:, l, sh * KC + c, 1:2], ALU.mult, ALU.add).then_inc(nrm_c_ready, 1)

                context(0)
                for c in range(KC):
                    if c + 1 < KC:
                        context(c + 1)
                    dve.wait_ge(nrm_h_ready, KC * m + c + 1)
                    v.tensor_tensor(hn_l[:, c, :], nrm_v[:, c % 2, :], hn_h[:, c, :].bitcast(F32), ALU.subtract).then_inc(hn_ready, 1)

            def tail(l, kind, produce):
                for t in range(NT + 1):
                    if t < NT:
                        produce(t)
                    if t:
                        residual(l, kind, t - 1)

            def attention(l):
                col = None
                todo = [(0, u) for u in range(8, 24)] + [(1, u) for u in range(8)] if l == 0 else [(1, u) for u in range(8, 24)]

                def drain_o(s):
                    h, t = divmod(s, NT)
                    full(dve, ("o", l, s))
                    v.tensor_copy(o_all[:, t, h * V:(h + 1) * V], bank(6, 0, V)).then_inc(o_ready, 1)
                    dve.wait_ge(o_ready, 21 * l + s + 1)
                    dve.nop().then_inc(bank_free[6], 1)

                for s in range(H * NT):
                    t = s % NT
                    w = T if t < 4 else T_CTX
                    full(dve, ("score", l, s))
                    if t < 4:
                        src = ps[:, 0:4 * BANK].rearrange("p (m a n) -> p m a n", m=2, a=2)[:, :, :, 0:HALF]
                        link(v.tensor_reduce(smx[:, :], src, AX.XY, ALU.max))
                    else:
                        src = ps[:, 0:4 * BANK].rearrange("p (m n) -> p m n", m=2)[:, :, 0:T_CTX]
                        link(v.tensor_reduce(smx[:, :], src, AX.X, ALU.max))
                    v.tensor_scalar(nmx[:, :], smx[:, :], -SCALE, None, ALU.mult).then_inc(nmax_ready, 1)
                    dve.wait_ge(exp_ready, 40 * l + 2 * s + 2)
                    link(v.reciprocal(rsum[:, :], ssum[:, :]))
                    link(v.tensor_scalar(rneg[:, :], rsum[:, 1:2], nlam[:, l:l + 1], None, ALU.mult))
                    p0, p1 = probs[:, s % 2, 0, 0:w], probs[:, s % 2, 1, 0:w]
                    link(v.tensor_scalar(p0, p0, rsum[:, 0:1], None, ALU.mult))
                    v.scalar_tensor_tensor(out=p0, in0=p1, scalar=rneg[:, 0:1], in1=p0, op0=ALU.mult, op1=ALU.add).then_inc(a_ready, 1)
                    for a in range(ADA_STEPS[l][t]):
                        if col:
                            ada_col(*col)
                        col = todo.pop(0)
                        ada_row(*col)
                        if s and a == 0:
                            drain_o(s - 1)
                    if s and ADA_STEPS[l][t] == 0:
                        drain_o(s - 1)
                assert not todo
                if col:
                    ada_col(*col)
                drain_o(H * NT - 1)

            def channel_transform(l):
                for i in range(2):
                    full(dve, ("m12", l, i))
                    b = (0, 7)[i]
                    v.tensor_scalar(m12[:, :, i, :], bank(b, 0, 512).rearrange("p (g e) -> p g e", g=G),
                                    1.0 if i == 0 else -1.0, None, ALU.mult).then_inc(m12_ready, 1)
                    dve.wait_ge(m12_ready, 2 * l + i + 1)
                    dve.nop().then_inc(bank_free[b], 1)

            def fourier(l):
                for t in range(NT):
                    for g2 in range(2):
                        r = 2 * t + g2
                        dve.wait_ge(zh_ready, 10 * l + r + 1)
                        v.tensor_tensor(z_l[:, t, 2 * g2:2 * g2 + 2, :], bank(2 + r % 6, 0, 512).rearrange("p (g e) -> p g e", g=2),
                                        z_h[:, t, 2 * g2:2 * g2 + 2, :].bitcast(F32), ALU.subtract).then_inc(zl_ready, 1)
                        dve.wait_ge(zl_ready, 10 * l + r + 1)
                        dve.nop().then_inc(bank_free[2 + r % 6], 1)
                gate_column(2 * l)
                link(v.tensor_tensor(o_sq[:, :, :], o_all[:, :, :], o_all[:, :, :], ALU.mult))
                c = stat_col(l, "sub")
                v.tensor_reduce(ssq[:, c:c + 20], o_sq[:, :, :].rearrange("p t (h e) -> p (t h) e", h=H), AX.X, ALU.add).then_inc(ssq_ready, 1)
                dve.wait_ge(ssq_ready, stat_no(l, "sub"))
                dve.wait_ge(rstd_ready, stat_no(l, "sub"))
                v.tensor_tensor(o_norm[:, :, :].rearrange("p t (h e) -> p (t h) e", h=H), o_all[:, :, :].rearrange("p t (h e) -> p (t h) e", h=H),
                                rstd[:, c:c + 20].unsqueeze(2).broadcast_to([128, 20, V]), ALU.mult).then_inc(o_ready, 1)
                gate_rows(2 * l)
                for g in range(G):
                    dve.wait_ge(mf_h_ready, 5 * l + g + 1)
                    v.tensor_tensor(mx_l[:, 4 + g, 0:T_LAT], bank(g, 0, T_LAT), mx_h[:, 4 + g, 0:T_LAT].bitcast(F32), ALU.subtract).then_inc(mf_ready, 1)
                    dve.wait_ge(mf_ready, 2 * G * l + g + 1)
                    dve.nop().then_inc(bank_free[g], 1)
                dve.wait_ge(mf_h_ready, 5 * l + 5)
                v.tensor_tensor(mx_l[:, 4:8, T_LAT:T], bank(4, 0, 512).rearrange("p (g n) -> p g n", g=4),
                                mx_h[:, 4:8, T_LAT:T].bitcast(F32), ALU.subtract).then_inc(mf_ready, 4)
                dve.wait_ge(mf_ready, 2 * G * (l + 1))
                dve.nop().then_inc(bank_free[4], 1)

                def low(h):
                    dve.wait_ge(sub_h_ready, H * l + h + 1)
                    v.tensor_tensor(mx_l[:, h, :], sub_v[:, h % 2, :], mx_h[:, h, :].bitcast(F32), ALU.subtract).then_inc(mxa_ready, 1)

                for h in range(H):
                    full(dve, ("sub", l, h))
                    b = fills.named["sub", l, h][0]
                    if h >= 2:
                        dve.wait_ge(mxa_ready, H * l + h - 1)
                    v.tensor_scalar(sub_v[:, h % 2, :], ps[:, b * BANK:b * BANK + T], gsub[:, l:l + 1], None, ALU.mult).then_inc(sub_v_ready, 1)
                    dve.wait_ge(sub_v_ready, H * l + h + 1)
                    dve.nop().then_inc(bank_free[b], 1)
                    if h:
                        low(h - 1)
                low(H - 1)

            def gate_column(g):
                l, f = divmod(g, 2)
                vec, gain = ((GT_A, V_GAPOST), (GT_F, V_GFPOST))[f]
                v.tensor_tensor(gcol[:, :, :], modc[:, l, vec * KC:(vec + 1) * KC, :],
                                vcol[:, l, gain:gain + KC].unsqueeze(2).broadcast_to([128, KC, 2]), ALU.mult).then_inc(gcol_ready, 1)

            def gate_rows(g):
                for cond in range(2):
                    for hf in range(2):
                        full(dve, ("gate_bc", g, cond, hf))
                        v.tensor_copy(gate_bc[:, cond, hf * 512:(hf + 1) * 512], bank(4 + 2 * cond + hf, 0, 512)).then_inc(gate_ready, 1)
                dve.wait_ge(gate_ready, 4 * (g + 1))
                for b in range(4, 8):
                    dve.nop().then_inc(bank_free[b], 1)

            def residual(l, kind, t):
                r = 2 * l + (kind == "post_f")
                y = eacc if (l, kind) == (1, "post_f") else acc
                dve.wait_ge(rstd_ready, stat_no(l, kind, t))
                c = stat_col(l, kind, t)
                link(v.scalar_tensor_tensor(out=y[:, t, :], in0=y[:, t, :], scalar=rstd[:, c:c + 1],
                                            in1=gate_bc[:, 0 if t < 4 else 1, :], op0=ALU.mult, op1=ALU.mult))
                if r == 3:
                    dve.wait_ge(x_here[t], 32)
                v.tensor_tensor(x[:, t, :], x[:, t, :], y[:, t, :], ALU.add).then_inc(x_ready, 1)

            def products(l, key, i, k):
                for j in range(2):
                    full(dve, (key, "up", j), i)
                    view = sg[:, j, :].rearrange("p (a n) -> p a n", a=2)
                    v.tensor_tensor(view, view, pair(2 * j), ALU.mult).then_inc(hv_ready, 1)
                dve.wait_ge(hv_ready, 2 + (i * 2 + 2 if k else 0))
                dve.nop().then_inc(bank_free[0], 1)
                dve.nop().then_inc(bank_free[2], 1)

            def low_hidden(l, i, k):
                for j in range(2):
                    dve.wait_ge(hid_h_ready, j + 1 + (i * 2 + 2 if k else 0))
                    v.tensor_tensor(hid_l[:, j, :], sg[:, j, :], hid_h[:, j, :].bitcast(F32), ALU.subtract).then_inc(hid_ready, 1)

            def add_down(l, key, i, k, rs):
                for r in rs:
                    t, hf = divmod(r, 2)
                    full(dve, (key, "down", r), i)
                    a = acc[:, t, hf * 512:(hf + 1) * 512]
                    v.tensor_tensor(a, a, bank(4 + r % 4, 0, 512), ALU.add).then_inc(bank_free[4 + r % 4], 1)

            def route():
                full(dve, ("router",))
                v.tensor_copy(lgT[:, :].rearrange("p (a n) -> p a n", a=2), pair(0)[0:E]).then_inc(lgT_ready, 1)
                dve.wait_ge(lgT_ready, 1)
                dve.nop().then_inc(bank_free[0], 1)
                full(dve, ("logits",))
                link(v.tensor_copy(logit[:, :, :].rearrange("p t e -> p (t e)"), bank(0, 0, NT * E)))
                dve.nop().then_inc(bank_free[0], 1)
                for t in range(NT):
                    link(v.max(top8[:, t, :], logit[:, t, :]))
                    link(v.max_index(idx8[:, t, :], top8[:, t, :], logit[:, t, :]))
                link(v.tensor_copy(idxf[:, :, :], idx8[:, :, 0:2]))
                v.tensor_tensor(gdif[:, :], top8[:, :, 1], top8[:, :, 0], ALU.subtract).then_inc(gexp_ready, 1)
                io = iota8.unsqueeze(1).broadcast_to([128, NT, E])
                link(v.tensor_tensor(sel[:, :, :], io, idxf[:, :, 0:1].broadcast_to([128, NT, E]), ALU.is_equal))
                link(v.tensor_tensor(gsel[:, :, :], io, idxf[:, :, 1:2].broadcast_to([128, NT, E]), ALU.is_equal))
                dve.wait_ge(gexp_ready, 2)
                link(v.tensor_scalar(gden[:, :], gexp[:, :], 1.0, None, ALU.add))
                link(v.reciprocal(g12[:, :, 0], gden[:, :]))
                link(v.tensor_tensor(g12[:, :, 1], g12[:, :, 0], gexp[:, :], ALU.mult))
                link(v.tensor_tensor(gates[:, :, :], sel[:, :, :], g12[:, :, 0:1].broadcast_to([128, NT, E]), ALU.mult))
                link(v.tensor_tensor(pos[:, :, :], gsel[:, :, :], g12[:, :, 1:2].broadcast_to([128, NT, E]), ALU.mult))
                link(v.tensor_tensor(gates[:, :, :], gates[:, :, :], pos[:, :, :], ALU.add))
                link(v.tensor_tensor(sel[:, :, :], sel[:, :, :], gsel[:, :, :], ALU.add))
                link(v.memset(csel[:, 0, :], 0.0))
                for t in range(1, NT):
                    link(v.tensor_tensor(csel[:, t, :], csel[:, t - 1, :], sel[:, t - 1, :], ALU.add))
                v.tensor_tensor(tsel[:, :], csel[:, NT - 1, :], sel[:, NT - 1, :], ALU.add).then_inc(sel_ready, 1)
                full(dve, ("pos",))
                link(v.tensor_scalar(pos[:, :, :].rearrange("p t e -> p (t e)"), bank(0, 0, NT * E), FAR, None, ALU.add))
                link(v.tensor_copy(total[:, :], bank(0, NT * E, (NT + 1) * E)))
                link(v.tensor_reduce(most[:, 0:1], total[:, :], AX.X, ALU.max))
                dve.nop().then_inc(bank_free[0], 1)
                link(v.tensor_tensor(pos[:, :, :], pos[:, :, :], sel[:, :, :], ALU.mult))
                for r in range(ROUNDS):
                    link(v.tensor_scalar(slot_x[:, :, r * E:(r + 1) * E], pos[:, :, :], -FAR - r * SLOTS, None, ALU.add))
                    link(v.tensor_copy(gate_x[:, :, r * E:(r + 1) * E], gates[:, :, :]))
                link(v.memset(slot_x[:, :, ROUNDS * E:], -FAR))
                link(v.memset(gate_x[:, :, ROUNDS * E:], 0.0))
                pick_first()
                for r in range(1, ROUNDS):
                    link(v.tensor_scalar(most[:, r:r + 1], most[:, 0:1], float(r * SLOTS), None, ALU.is_gt))
                link(v.tensor_reduce(trips_f[:, 1:2], most[:, 1:ROUNDS], AX.X, ALU.add))
                link(v.tensor_scalar(trips_f[:, 1:2], trips_f[:, 1:2], 1.0, None, ALU.add))
                link(v.tensor_scalar(trips_f[:, 0:1], trips_f[:, 1:2], float(E), None, ALU.mult))
                link(v.tensor_scalar(trips_f[:, 2:3], trips_f[:, 0:1], -1.0, None, ALU.add))
                for r in range(ROUNDS):
                    link(v.tensor_scalar(left_f[:, r * E:(r + 1) * E], total[:, :], -float(r * SLOTS), None, ALU.add))
                link(v.tensor_copy(left_i[:, :], left_f[:, :]))
                v.tensor_copy(trips_i[:, :], trips_f[:, :]).then_inc(trips_ready, 1)

            def pick_first():
                link(v.tensor_copy(slot_c[:, :], slot_x[:, :, 0]))
                link(v.tensor_copy(gate_c[:, :], gate_x[:, :, 0]))
                for t in range(NT):
                    ins = v.tensor_scalar(pick[:, t, :], iota_s, slot_c[:, t:t + 1], None, ALU.is_equal)
                ins.then_inc(pick_ready, 1)

            def picked(key, chunks, i):
                for c in chunks:
                    if c % 2:
                        full(dve, (key, "xg", c), i)
                        base = 4 if key == "next" else 0
                        v.tensor_copy(xg[:, c, :, :].rearrange("p a n -> p (a n)"), bank(c % 4, 0, 2 * SLOTS)).then_inc(xg_dve, 1)
                        dve.wait_ge(xg_dve, base + c // 2 + 1 + i * 4)
                        dve.nop().then_inc(bank_free[c % 4], 1)

            def experts():
                picked("ahead", range(KC), 0)
                gate_rows(3)
                dve.wait_ge(acc_zero, 2)
                dve.wait_ge(trips_ready, 1)
                trips = dve.value_load(trips_i[0:1, 0:1], min_val=E, max_val=ROUNDS * E)
                with dve.Fori(0, trips) as i:
                    for q in range(EXP_BLK):
                        full(dve, ("exp", "up", q), i)
                        dve.wait_ge(esg_ready, q + 1 + i * EXP_BLK)
                        sg2 = esg[:, :, :].rearrange("p a n -> p (a n)")
                        v.tensor_tensor(sg2, sg2, bank(2 * (q % 2) + 1, 0, 2 * SLOTS), ALU.mult).then_inc(ehv_ready, 1)
                        dve.wait_ge(ehv_ready, q + 1 + i * EXP_BLK)
                        dve.nop().then_inc(bank_free[2 * (q % 2) + 1], 1)
                        if q == 0:
                            for st in range(2):
                                full(dve, ("pickT", st), i)
                                v.tensor_copy(pickT[:, st, 0:T_LAT], bank(2 + st, 0, T_LAT)).then_inc(pickT_ready, 1)
                                dve.wait_ge(pickT_ready, st + 1 + i * 3)
                                dve.nop().then_inc(bank_free[2 + st], 1)
                            full(dve, ("pickT", 2), i)
                            v.tensor_copy(pickT[:, :, T_LAT:T], bank(4, 0, 256).rearrange("p (a n) -> p a n", a=2)).then_inc(pickT_ready, 1)
                            dve.wait_ge(pickT_ready, 3 + i * 3)
                            dve.nop().then_inc(bank_free[4], 1)
                            full(dve, ("gslot",), i)
                            v.tensor_copy(gslot[:, :], bank(5, 0, 2)).then_inc(gslot_ready, 1)
                            dve.wait_ge(gslot_ready, 1 + i)
                            dve.nop().then_inc(bank_free[5], 1)
                        dve.wait_ge(ehid_h_ready, q + 1 + i * EXP_BLK)
                        v.tensor_tensor(ehid_l[:, :, :].rearrange("p a n -> p (a n)"), bank(2 * (q % 2), 0, 2 * SLOTS),
                                        ehid_h[:, :, :].rearrange("p a n -> p (a n)").bitcast(F32), ALU.subtract).then_inc(ehid_ready, 1)
                        dve.wait_ge(ehid_ready, q + 1 + i * EXP_BLK)
                        dve.nop().then_inc(bank_free[2 * (q % 2)], 1)
                        if q == 0:
                            v.tensor_copy(slot_c[:, :], slot_x[:, :, bass.ds(i + 1, 1)].rearrange("p t a -> p (t a)")).then_inc(slot_ready, 1)
                            v.tensor_copy(gate_c[:, :], gate_x[:, :, bass.ds(i + 1, 1)].rearrange("p t a -> p (t a)")).then_inc(slot_ready, 1)
                            dve.wait_ge(slot_ready, 2 + i * 2)
                            for t in range(NT):
                                ins = v.tensor_scalar(pick[:, t, :], iota_s, slot_c[:, t:t + 1], None, ALU.is_equal)
                            ins.then_inc(pick_ready, 1)
                    picked("next", range(0, KC // 2), i)
                    for st in range(2):
                        for hf in range(2):
                            b = 4 + 2 * st + hf
                            r = 2 * st + hf
                            dve.wait_ge(yh_ready, r + 1 + i * 4)
                            v.scalar_tensor_tensor(out=y_l[st][:, hf * 512:(hf + 1) * 512], in0=bank(b, 0, 512), scalar=gslot[:, st:st + 1],
                                                   in1=y_h[:, st, hf * 512:(hf + 1) * 512].bitcast(F32), op0=ALU.mult, op1=ALU.subtract).then_inc(yl_ready, 1)
                            dve.wait_ge(yl_ready, r + 1 + i * 4)
                            dve.nop().then_inc(bank_free[b], 1)
                    picked("next", range(KC // 2, KC), i)
                    for r in range(2 * NT):
                        t, hf = divmod(r, 2)
                        full(dve, ("scatter", r), i)
                        a = eacc[:, t, hf * 512:(hf + 1) * 512]
                        v.tensor_tensor(a, a, bank(r % 4, 0, 512), ALU.add).then_inc(bank_free[r % 4], 1)
                dve.drain().then_inc(y_ready, NT)

            dve.wait_ge(params_landed, 80)
            lt = lamt[:, :, :].rearrange("p l (a b) -> p l a b", a=2)
            v.tensor_tensor(lam2[:, :, :], lt[:, :, :, 0], lt[:, :, :, 1], ALU.mult).then_inc(lam_v, 1)
            dve.wait_ge(cond_act, 2)
            v.tensor_tensor(cond_p[:, :, 2:4], cond_s[:, :, :], cond_p[:, :, 0:2].bitcast(F32), ALU.subtract).then_inc(cond_ready, 1)
            dve.wait_ge(act_const, 2)
            v.tensor_tensor(dft_l[:, :], consts[:, 256:512], dft_h[:, :].bitcast(F32), ALU.subtract).then_inc(dft_ready, 1)
            v.tensor_tensor(rt_l[:, :, :], w_rt[:, :, :], rt_h[:, :, :].bitcast(F32), ALU.subtract).then_inc(dft_ready, 1)
            dve.wait_ge(bank_free[0], 1)
            link(v.tensor_tensor(nlam[:, :], lame[:, :, 1], lame[:, :, 0], ALU.subtract))
            for l in range(L):
                lam_init = 0.8 - 0.6 * math.exp(-0.3 * l)
                link(v.tensor_scalar(nlam[:, l:l + 1], nlam[:, l:l + 1], -lam_init, None, ALU.add))
                link(v.tensor_scalar(gsub[:, l:l + 1], vcol[:, l, V_SUB:V_SUB + 1], 1.0 - lam_init, None, ALU.mult))

            def low_first(n):
                dve.wait_ge(wh_ready, n + 1)
                v.tensor_tensor(wl[n % RING][:, :], raw[n % RING][:, :], wh[n % RING][:, :].bitcast(F32), ALU.subtract).then_inc(wl_first, 1)

            low_first(0)
            low_first(2)
            for u in range(FIRST):
                ada_row(0, u)
                if u == 1:
                    low_first(4)
                ada_col(0, u)
            modulation(0, "pre_a")
            for l in range(L):
                norm_low(l, "pre_a")
                for c in range(4, 8):
                    b = 2 * (c % 4)
                    full(dve, ("in", l, c))
                    v.tensor_copy(kT[:, c - 4, 0:HALF], bank(b, 0, HALF)).then_inc(dve_step, 1)
                    v.tensor_copy(kT[:, c - 4, HALF:T_LAT], bank(b + 1, 0, T_LAT - HALF)).then_inc(dve_step, 1)
                    chain[0] += 2
                    dve.wait_ge(dve_step, chain[0])
                    v.tensor_copy(kT[:, c - 4, T:T + T_CTX], bank(b + 1, T_LAT - HALF, HALF)).then_inc(k_out, 1)
                    dve.wait_ge(k_out, H * l + c - 3)
                    dve.nop().then_inc(bank_free[b], 1)
                for c in range(2 * H):
                    full(dve, ("rot", l, c))
                    a = (qT if c % 2 == 0 else kT)[:, c // 2, 0:T_LAT]
                    link(v.tensor_tensor(rope_t[:, :], bank(c, 0, T_LAT), sin_r, ALU.mult))
                    dve.nop().then_inc(bank_free[c], 1)
                    link(v.tensor_tensor(a, a, cos_r, ALU.mult))
                    v.tensor_tensor(a, a, rope_t[:, :], ALU.add).then_inc(rope_ready, 1)
                    dve.wait_ge(rope_ready, 2 * H * l + c + 1)
                for u in range(2):
                    for t in range(NT):
                        full(dve, ("val", l, u, t))
                        v.tensor_copy(vt[:, t, u * 256:(u + 1) * 256], bank((5 * u + t) % 8, 0, 256)).then_inc(v_out, 1)
                        dve.wait_ge(v_out, 2 * NT * l + 5 * u + t + 1)
                        dve.nop().then_inc(bank_free[(5 * u + t) % 8], 1)
                channel_transform(l)
                attention(l)
                fourier(l)
                modulation(l, "pre_f")

                def mixed(hf, t):
                    full(dve, ("mix", l, hf, t))
                    b = (5 * hf + t) % 8
                    v.tensor_copy(acc[:, t, hf * 512:(hf + 1) * 512], bank(b, 0, 512)).then_inc(y_ready if hf else dve_step, 1)
                    if hf == 0:
                        chain[0] += 1
                        dve.wait_ge(dve_step, chain[0])
                    else:
                        dve.wait_ge(y_ready, NT * 2 * l + t + 1)
                    dve.nop().then_inc(bank_free[b], 1)

                for t in range(NT):
                    mixed(0, t)
                tail(l, "post_a", lambda t: mixed(1, t))
                gate_column(2 * l + 1)
                norm_low(l, "pre_f")
                if l == 1:
                    route()
                    experts()
                    for t in range(NT):
                        residual(1, "post_f", t)
                    break
                gate_rows(1)
                nb = N_BLK
                dve.wait_ge(sg_ready, 2)
                products(l, ("first", l), 0, 0)
                low_hidden(l, 0, 0)
                dve.wait_ge(acc_zero, 1)
                with dve.Fori(0, nb - 1) as i:
                    dve.wait_ge(sg_ready, 4 + i * 2)
                    products(l, ("body", l), i, 1)
                    add_down(l, ("body", l), i, 1, range(2 * NT))
                    low_hidden(l, i, 1)
                modulation(l + 1, "pre_a")

                def summed(t):
                    rs = (2 * t, 2 * t + 1)
                    add_down(l, ("last", l), 0, 0, rs)
                    for r in rs:
                        dve.wait_ge(bank_free[4 + r % 4], fills.named[(("last", l), "down", r)][1])
                    dve.nop().then_inc(y_ready, 1)

                tail(l, "post_f", summed)


def dft(n):
    j = np.outer(np.arange(n), np.arange(n)) % n
    return (np.cos(2 * np.pi * j / n) / math.sqrt(n)).astype(np.float32), (np.sin(2 * np.pi * j / n) / math.sqrt(n)).astype(np.float32)


def shape_constants():
    c, s = dft(128)
    rot = np.zeros((128, 128), np.float32)
    for d in range(128):
        b, r = divmod(d, 16)
        if b % 2 == 0:
            rot[d + 16, d] = -1.0
        else:
            rot[d - 16, d] = 1.0
    grid_w, half = 64, QK // 2
    inv = (1.0 / (np.float32(10000.0) ** (np.arange(0, half, 2, dtype=np.float32) / np.float32(half)))).astype(np.float32)
    pos = np.arange(T_LAT)
    tabs = []
    for p in (pos // grid_w, pos % grid_w):
        a = p.astype(np.float32)[:, None] * inv[None, :]
        tabs += [a, a]
    ang = np.concatenate(tabs, axis=1)
    ang = np.concatenate([ang, ang], axis=1).T
    iota = np.tile(np.concatenate([np.arange(8), np.arange(SLOTS)]).astype(np.float32), (128, 1))
    tri = np.triu(np.ones((128, 128), np.float32), 1)
    sel = np.zeros((128, 2), np.float32)
    for r in range(4):
        sel[r, r % 2] = 1.0
    consts = np.concatenate([np.eye(128, dtype=np.float32), rot, c, s, np.cos(ang), np.sin(ang), iota, tri, sel], axis=1)
    c5, s5 = dft(T_LAT)
    lay = lambda a: a.reshape(4, 128, T_LAT).transpose(1, 0, 2).reshape(128, UNIT)
    return np.ascontiguousarray(consts.astype(np.float32)), lay(c5), lay(s5)


def kernel(x_prompt, x_sample, cache_k, cache_v, c, c_ctx, g_attn_pre, g_attn_post, g_ffn_pre, g_ffn_post,
           w_ada, b_ada, w_in, lam_params, g_subln, w_fnet, w_out, w_gate, w_up, w_down, w_router,
           e_gate, e_up, e_down):
    import concourse.bacc as bacc
    from concourse.bass_utils import run_bass_kernel_spmd

    A = np.asarray
    consts, cos5, sin5 = shape_constants()

    def wide(w, u):
        return A(w)[:, u * COLS:(u + 1) * COLS].reshape(KC, 128, COLS).transpose(1, 0, 2).reshape(128, UNIT)

    def rows(w, r, n):
        w = A(w)[r:r + n]
        return w.reshape(n // 128, 128, w.shape[1]).transpose(1, 0, 2).reshape(128, UNIT)

    in_cols = [0, 1, 2, 3, 6, 7, 4, 5]
    units = plan_units()
    stream = np.empty((len(units), 128, UNIT), np.float32)
    for n, (kind, l, u) in enumerate(units):
        e, q = divmod(u, EXP_BLK)
        if kind == "ada":
            stream[n] = wide(w_ada[l], u)
        elif kind == "in":
            stream[n] = wide(w_in[l], in_cols[u])
        elif kind == "cos":
            stream[n] = cos5
        elif kind == "sin":
            stream[n] = sin5
        elif kind == "out":
            stream[n] = rows(A(w_out[l])[:, (u // 2) * 512:(u // 2 + 1) * 512], (1 - u % 2) * 512, 512)
        elif kind == "gate":
            stream[n] = wide(w_gate[0], u) if l == 0 else wide(e_gate[0][e], q)
        elif kind == "up":
            stream[n] = wide(w_up[0], u) if l == 0 else wide(e_up[0][e], q)
        else:
            stream[n] = rows(w_down[0], u * COLS, COLS) if l == 0 else rows(e_down[0][e], q * COLS, COLS)
    vrows = np.zeros((L, 128, 128), np.float32)
    for l in range(L):
        parts = [b_ada[l], g_attn_pre[l], g_attn_post[l], g_ffn_pre[l], g_ffn_post[l], c[0], c_ctx, g_subln[l]]
        flat = np.concatenate([A(p).reshape(-1, 128) for p in parts], axis=0)
        vrows[l, :flat.shape[0]] = flat
    x_all = np.concatenate([A(x_sample)[0], A(x_prompt)[0]], axis=0)
    arrays = {
        "stream": stream,
        "consts": consts,
        "vcol": vrows.transpose(2, 0, 1),
        "x": x_all.reshape(NT, 128, D).transpose(1, 0, 2),
        "lam": A(lam_params).transpose(2, 0, 1),
        "w_router": A(w_router)[0].reshape(KC, 128, E).transpose(1, 0, 2),
        "w_fnet": A(w_fnet).transpose(0, 2, 1, 3).reshape(L, 128, G * 128),
        "cache_k": A(cache_k)[0].reshape(L, PAST, H, 2 * QK).transpose(0, 3, 2, 1),
        "cache_v": A(cache_v)[0].reshape(L, PAST, H * V),
    }
    arrays = {k: np.ascontiguousarray(a) for k, a in arrays.items()}
    nc = bacc.Bacc("TRN2", target_bir_lowering=False, num_devices=1)
    dram = {k: nc.dram_tensor(k, a.shape, F32, kind="ExternalInput").ap() for k, a in arrays.items()}
    shapes = {"y": (128, NT, D), "new_k": (L, 128, H, T_CTX), "new_v": (L, 128, H * V)}
    out = {k: nc.dram_tensor(k, s, F32, kind="ExternalOutput").ap() for k, s in shapes.items()}
    build(nc, dram, out)
    r = run_bass_kernel_spmd(nc, [arrays], core_ids=[0]).results[0]
    y = A(r["y"]).transpose(1, 0, 2).reshape(T, D)
    new_k = A(r["new_k"]).transpose(0, 3, 2, 1).reshape(1, L, T_CTX, H, 2, QK)
    new_v = A(r["new_v"]).reshape(1, L, T_CTX, H, V)
    return (np.ascontiguousarray(y[T_LAT:])[None], np.ascontiguousarray(y[:T_LAT])[None],
            np.ascontiguousarray(new_k), np.ascontiguousarray(new_v))
```
